# Optimizing a Trainium2 kernel written in Bass

```python
import jax, jax.numpy as jnp
from jax import lax
import numpy as np

D_MODEL = 1024
BATCH = 1
SEQ = 512
DEPTH = 1

CHUNK = 64
LEFT_CHUNKS = 8
HEAD_DIM = 64
N_HEADS_A = 8
N_HEADS_B = 8
WIDTH_A = N_HEADS_A * HEAD_DIM
WIDTH_B = N_HEADS_B * HEAD_DIM
MAX_REL = 128
N_REL = 2 * MAX_REL + 1
QUERY_BLOCK = 128
D_FF = 2816
CONV_WIDTH = 3
IN_WIDTH = 3 * WIDTH_A + 3 * WIDTH_B + 2 * D_MODEL
EPS = 1e-6


def rms_norm(x, gain):
    xf = x.astype(jnp.float32)
    y = xf * lax.rsqrt(jnp.mean(xf * xf, axis=-1, keepdims=True) + EPS)
    return (y * gain.astype(jnp.float32)).astype(x.dtype)

def chunked_attention(q, k, v, q_gain, k_gain, rel_bias):
    b, s, h, dh = q.shape
    nc = s // CHUNK
    band = (LEFT_CHUNKS + 1) * CHUNK
    q = rms_norm(q, q_gain)
    k = rms_norm(k, k_gain)
    qc = q.reshape(b, nc, CHUNK, h, dh)
    pad = ((0, 0), (LEFT_CHUNKS * CHUNK, 0), (0, 0), (0, 0))
    kp = jnp.pad(k, pad).reshape(b, nc + LEFT_CHUNKS, CHUNK, h, dh)
    vp = jnp.pad(v, pad).reshape(b, nc + LEFT_CHUNKS, CHUNK, h, dh)
    kb = jnp.concatenate([kp[:, i:i + nc] for i in range(LEFT_CHUNKS + 1)], axis=2)
    vb = jnp.concatenate([vp[:, i:i + nc] for i in range(LEFT_CHUNKS + 1)], axis=2)
    scores = jnp.einsum('bnqhd,bnkhd->bnhqk', qc, kb).astype(jnp.float32) * (dh ** -0.5)
    r = jnp.arange(CHUNK)[:, None]
    key_off = jnp.arange(band)[None, :] - LEFT_CHUNKS * CHUNK
    rel = r - key_off
    idx = jnp.clip(rel, -MAX_REL, MAX_REL) + MAX_REL
    bias = rel_bias[:, idx].astype(jnp.float32)
    valid = (jnp.arange(nc)[:, None] * CHUNK + key_off) >= 0
    scores = jnp.where(valid[None, :, None, None, :], scores + bias[None, None], -jnp.inf)
    probs = jax.nn.softmax(scores, axis=-1).astype(v.dtype)
    out = jnp.einsum('bnhqk,bnkhd->bnqhd', probs, vb)
    return out.reshape(b, s, h * dh)

def stick_breaking_attention(q, k, v):
    b, s, h, dh = q.shape
    nb = s // QUERY_BLOCK
    kh = k.transpose(0, 2, 1, 3)
    vh = v.transpose(0, 2, 1, 3)
    qblocks = q.transpose(0, 2, 1, 3).reshape(b, h, nb, QUERY_BLOCK, dh).transpose(2, 0, 1, 3, 4)
    key_pos = jnp.arange(s)

    def block(args):
        qb, blk = args
        z = jnp.einsum('bhqd,bhkd->bhqk', qb, kh).astype(jnp.float32) * (dh ** -0.5)
        q_pos = blk * QUERY_BLOCK + jnp.arange(QUERY_BLOCK)
        causal = key_pos[None, :] < q_pos[:, None]
        log_keep = jnp.where(causal, -jax.nn.softplus(z), 0.0)
        log_after = lax.cumsum(log_keep, axis=3, reverse=True) - log_keep
        w = jnp.where(causal, jnp.exp(jax.nn.log_sigmoid(z) + log_after), 0.0)
        return jnp.einsum('bhqk,bhkd->bhqd', w.astype(vh.dtype), vh)

    out = lax.map(block, (qblocks, jnp.arange(nb)))
    return out.transpose(1, 0, 3, 2, 4).reshape(b, s, h * dh)

def conv_glu(x, w_up, conv_w, conv_b, w_down):
    hid = x @ w_up
    hid = lax.conv_general_dilated(
        hid, conv_w[:, None, :], window_strides=(1,),
        padding=((CONV_WIDTH - 1, 0),),
        dimension_numbers=('NWC', 'WIO', 'NWC'),
        feature_group_count=2 * D_FF) + conv_b
    gate, up = hid[..., :D_FF], hid[..., D_FF:]
    return (jax.nn.silu(gate) * up) @ w_down

def first_inputs(seed: int = 0) -> dict:
    key = jax.random.key(seed)
    ks = jax.random.split(key, 16)
    f32 = jnp.float32
    nrm = lambda k, shape, scale: jax.random.normal(k, shape, f32) * scale
    return {
        "x": nrm(ks[0], (BATCH, SEQ, D_MODEL), 1.0),
        "norm1_g": 1.0 + nrm(ks[1], (DEPTH, D_MODEL), 0.02),
        "w_in": nrm(ks[2], (DEPTH, D_MODEL, IN_WIDTH), D_MODEL ** -0.5),
        "q_norm_g": 1.0 + nrm(ks[3], (DEPTH, HEAD_DIM), 0.02),
        "k_norm_g": 1.0 + nrm(ks[4], (DEPTH, HEAD_DIM), 0.02),
        "rel_bias": nrm(ks[5], (DEPTH, N_HEADS_A, N_REL), 0.2),
        "w_branch_a": nrm(ks[6], (DEPTH, WIDTH_A, D_MODEL), WIDTH_A ** -0.5),
        "w_branch_b": nrm(ks[7], (DEPTH, WIDTH_B, D_MODEL), WIDTH_B ** -0.5),
        "w_out": nrm(ks[8], (DEPTH, D_MODEL, D_MODEL), D_MODEL ** -0.5),
        "norm2_g": 1.0 + nrm(ks[9], (DEPTH, D_MODEL), 0.02),
        "w_ffn_up": nrm(ks[10], (DEPTH, D_MODEL, 2 * D_FF), D_MODEL ** -0.5),
        "ffn_conv_w": nrm(ks[11], (DEPTH, CONV_WIDTH, 2 * D_FF), CONV_WIDTH ** -0.5),
        "ffn_conv_b": nrm(ks[12], (DEPTH, 2 * D_FF), 0.01),
        "w_ffn_down": nrm(ks[13], (DEPTH, D_FF, D_MODEL), D_FF ** -0.5),
    }

def first_block(x, norm1_g, w_in, q_norm_g, k_norm_g, rel_bias, w_branch_a, w_branch_b,
              w_out, norm2_g, w_ffn_up, ffn_conv_w, ffn_conv_b, w_ffn_down):
    b, s, _ = x.shape
    o1 = 3 * WIDTH_A
    o2 = o1 + 3 * WIDTH_B
    for l in range(DEPTH):
        hn = rms_norm(x, norm1_g[l])
        proj = hn @ w_in[l]
        qa, ka, va = [proj[..., i * WIDTH_A:(i + 1) * WIDTH_A].reshape(b, s, N_HEADS_A, HEAD_DIM)
                      for i in range(3)]
        qb, kb, vb = [proj[..., o1 + i * WIDTH_B:o1 + (i + 1) * WIDTH_B].reshape(b, s, N_HEADS_B, HEAD_DIM)
                      for i in range(3)]
        gate_a = proj[..., o2:o2 + D_MODEL]
        gate_b = proj[..., o2 + D_MODEL:o2 + 2 * D_MODEL]
        out_a = chunked_attention(qa, ka, va, q_norm_g[l], k_norm_g[l], rel_bias[l])
        out_b = stick_breaking_attention(qb, kb, vb)
        mixed = (jax.nn.sigmoid(gate_a) * (out_a @ w_branch_a[l])
                 + jax.nn.sigmoid(gate_b) * (out_b @ w_branch_b[l]))
        x = x + mixed @ w_out[l]
        x = x + conv_glu(rms_norm(x, norm2_g[l]), w_ffn_up[l], ffn_conv_w[l],
                         ffn_conv_b[l], w_ffn_down[l])
    return x


PLE_DIM = 256
HG_HEADS = 4
HG_DK = 128
HG_DV = 128
HG_KW = HG_HEADS * HG_DK
HG_VW = HG_HEADS * HG_DV
HG_CHUNK = 64
FOX_HEADS = 8
FOX_DH = 64
FOX_W = FOX_HEADS * FOX_DH
FOX_BLOCK = 128
D_FF_2 = ((-(-8 * D_MODEL // 3) + 255) // 256) * 256

OFF_HG_Q = 0
OFF_HG_F = OFF_HG_Q + HG_KW
OFF_HG_I = OFF_HG_F + HG_KW
OFF_HG_G = OFF_HG_I + HG_VW
OFF_FOX_Q = OFF_HG_G + HG_VW
OFF_FOX_K = OFF_FOX_Q + FOX_W
OFF_FOX_V = OFF_FOX_K + FOX_W
OFF_FOX_F = OFF_FOX_V + FOX_W
OFF_GATE = OFF_FOX_F + FOX_HEADS
IN_COLS = OFF_GATE + 2 * D_MODEL


def rms_norm_2(x, g):
    xf = x.astype(jnp.float32)
    y = xf * lax.rsqrt(jnp.mean(xf * xf, axis=-1, keepdims=True) + EPS)
    return (y * g.astype(jnp.float32)).astype(x.dtype)

def hgrn2_mixer(q, f_logit, i, g, lb, o_gain):
    B, S, _ = q.shape
    f32 = jnp.float32
    qf = jax.nn.silu(q.astype(f32))
    fg = lb + (1.0 - lb) * jax.nn.sigmoid(f_logit.astype(f32))
    kf = 1.0 - fg
    logf = jnp.log(fg)
    vf = i.astype(f32)
    n = S // HG_CHUNK

    def to_chunks(t, d):
        return t.reshape(B, n, HG_CHUNK, HG_HEADS, d).transpose(1, 0, 3, 2, 4)

    qc = to_chunks(qf, HG_DK)
    kc = to_chunks(kf, HG_DK)
    vc = to_chunks(vf, HG_DV)
    bc = jnp.cumsum(to_chunks(logf, HG_DK), axis=3)
    causal = jnp.tril(jnp.ones((HG_CHUNK, HG_CHUNK), dtype=bool))[:, :, None]

    def step(state, xs):
        qt, kt, vt, bt = xs
        inter = jnp.einsum('bhtc,bhcv->bhtv', qt * jnp.exp(bt), state)
        diff = bt[:, :, :, None, :] - bt[:, :, None, :, :]
        decay = jnp.exp(jnp.where(causal, diff, -jnp.inf))
        scores = jnp.einsum('bhtc,bhsc,bhtsc->bhts', qt, kt, decay)
        intra = jnp.einsum('bhts,bhsv->bhtv', scores, vt)
        b_last = bt[:, :, -1:, :]
        new_state = (jnp.exp(b_last[:, :, 0, :])[..., None] * state
                     + jnp.einsum('bhsc,bhsv->bhcv', kt * jnp.exp(b_last - bt), vt))
        return new_state, inter + intra

    s0 = jnp.zeros((B, HG_HEADS, HG_DK, HG_DV), f32)
    _, o = lax.scan(step, s0, (qc, kc, vc, bc))
    o = o.transpose(1, 0, 3, 2, 4).reshape(B, S, HG_HEADS, HG_DV)
    o = rms_norm_2(o, o_gain).reshape(B, S, HG_VW)
    o = o * jax.nn.silu(g.astype(f32))
    return o.astype(q.dtype)

def forgetting_attention(q, k, v, f_logit, f_bias, q_gain, k_gain):
    B, S, _ = q.shape
    f32 = jnp.float32

    def heads(t):
        return t.reshape(B, S, FOX_HEADS, FOX_DH).transpose(0, 2, 1, 3)

    qh = rms_norm_2(heads(q), q_gain).astype(f32)
    kh = rms_norm_2(heads(k), k_gain).astype(f32)
    vh = heads(v)
    logf = jax.nn.log_sigmoid(f_logit.astype(f32) + f_bias.astype(f32))
    c = jnp.cumsum(logf, axis=1).transpose(0, 2, 1)
    scale = FOX_DH ** -0.5
    outs = []
    for blk in range(S // FOX_BLOCK):
        t0 = blk * FOX_BLOCK
        t1 = t0 + FOX_BLOCK
        s = jnp.einsum('bhtd,bhsd->bhts', qh[:, :, t0:t1], kh[:, :, :t1]) * scale
        s = s + c[:, :, t0:t1, None] - c[:, :, None, :t1]
        mask = (t0 + jnp.arange(FOX_BLOCK))[:, None] >= jnp.arange(t1)[None, :]
        s = jnp.where(mask, s, -jnp.inf)
        pr = jax.nn.softmax(s, axis=-1).astype(vh.dtype)
        outs.append(jnp.einsum('bhts,bhsd->bhtd', pr, vh[:, :, :t1]))
    o = jnp.concatenate(outs, axis=2)
    return o.transpose(0, 2, 1, 3).reshape(B, S, FOX_W)

def second_inputs(seed: int = 0) -> dict:
    key = jax.random.key(seed)
    ks = jax.random.split(key, 24)
    f32 = jnp.float32

    def w(k, shape, fan_in):
        return jax.random.normal(k, shape, f32) * (fan_in ** -0.5)

    def gain(k, shape):
        return 1.0 + 0.02 * jax.random.normal(k, shape, f32)

    return {
        "x": jax.random.normal(ks[0], (BATCH, SEQ, D_MODEL), f32),
        "p": jax.random.normal(ks[1], (DEPTH, BATCH, SEQ, PLE_DIM), f32),
        "norm_mix_g": gain(ks[2], (DEPTH, D_MODEL)),
        "w_in": w(ks[3], (DEPTH, D_MODEL, IN_COLS), D_MODEL),
        "hg_lb_logits": 0.1 * jax.random.normal(ks[4], (DEPTH + 1, HG_KW), f32),
        "hg_onorm_g": gain(ks[5], (DEPTH, HG_DV)),
        "fox_f_bias": jax.random.uniform(ks[6], (DEPTH, FOX_HEADS), f32, minval=1.0, maxval=4.0),
        "fox_q_norm_g": gain(ks[7], (DEPTH, FOX_DH)),
        "fox_k_norm_g": gain(ks[8], (DEPTH, FOX_DH)),
        "w_branch_a": w(ks[9], (DEPTH, HG_VW, D_MODEL), HG_VW),
        "w_branch_b": w(ks[10], (DEPTH, FOX_W, D_MODEL), FOX_W),
        "w_out": w(ks[11], (DEPTH, D_MODEL, D_MODEL), D_MODEL),
        "norm_ffn_g": gain(ks[12], (DEPTH, D_MODEL)),
        "w_ffn_gate": w(ks[13], (DEPTH, D_MODEL, D_FF_2), D_MODEL),
        "w_ffn_up": w(ks[14], (DEPTH, D_MODEL, D_FF_2), D_MODEL),
        "w_ffn_down": w(ks[15], (DEPTH, D_FF_2, D_MODEL), D_FF_2),
        "norm_ple_g": gain(ks[16], (DEPTH, D_MODEL)),
        "w_ple_gate": w(ks[17], (DEPTH, D_MODEL, D_MODEL), D_MODEL),
        "w_ple_proj": w(ks[18], (DEPTH, PLE_DIM, D_MODEL), PLE_DIM),
    }

def second_block(x, p, norm_mix_g, w_in, hg_lb_logits, hg_onorm_g, fox_f_bias, fox_q_norm_g,
              fox_k_norm_g, w_branch_a, w_branch_b, w_out, norm_ffn_g, w_ffn_gate, w_ffn_up,
              w_ffn_down, norm_ple_g, w_ple_gate, w_ple_proj):
    lower_bounds = jnp.cumsum(jax.nn.softmax(hg_lb_logits.astype(jnp.float32), axis=0), axis=0)
    for layer in range(DEPTH):
        h = rms_norm_2(x, norm_mix_g[layer])
        z = h @ w_in[layer]
        y_a = hgrn2_mixer(z[..., OFF_HG_Q:OFF_HG_F], z[..., OFF_HG_F:OFF_HG_I],
                          z[..., OFF_HG_I:OFF_HG_G], z[..., OFF_HG_G:OFF_FOX_Q],
                          lower_bounds[layer], hg_onorm_g[layer])
        y_b = forgetting_attention(z[..., OFF_FOX_Q:OFF_FOX_K], z[..., OFF_FOX_K:OFF_FOX_V],
                                   z[..., OFF_FOX_V:OFF_FOX_F], z[..., OFF_FOX_F:OFF_GATE],
                                   fox_f_bias[layer], fox_q_norm_g[layer], fox_k_norm_g[layer])
        gate_a = jax.nn.sigmoid(z[..., OFF_GATE:OFF_GATE + D_MODEL])
        gate_b = jax.nn.sigmoid(z[..., OFF_GATE + D_MODEL:IN_COLS])
        merged = gate_a * (y_a @ w_branch_a[layer]) + gate_b * (y_b @ w_branch_b[layer])
        x = x + merged @ w_out[layer]
        hf = rms_norm_2(x, norm_ffn_g[layer])
        x = x + (jax.nn.silu(hf @ w_ffn_gate[layer]) * (hf @ w_ffn_up[layer])) @ w_ffn_down[layer]
        hp = rms_norm_2(x, norm_ple_g[layer])
        x = x + jax.nn.sigmoid(hp @ w_ple_gate[layer]) * (p[layer] @ w_ple_proj[layer])
    return x


def setup_inputs(seed=0):
    out = dict(first_inputs(seed))
    for name, value in second_inputs(seed + 1).items():
        if name != "x":
            out[name + "_2"] = value
    return out


def reference(
    x, norm1_g, w_in, q_norm_g, k_norm_g, rel_bias, w_branch_a, w_branch_b, w_out, norm2_g,
    w_ffn_up, ffn_conv_w, ffn_conv_b, w_ffn_down, p_2, norm_mix_g_2, w_in_2, hg_lb_logits_2,
    hg_onorm_g_2, fox_f_bias_2, fox_q_norm_g_2, fox_k_norm_g_2, w_branch_a_2, w_branch_b_2,
    w_out_2, norm_ffn_g_2, w_ffn_gate_2, w_ffn_up_2, w_ffn_down_2, norm_ple_g_2, w_ple_gate_2,
    w_ple_proj_2,
):
    x = first_block(
        x, norm1_g, w_in, q_norm_g, k_norm_g, rel_bias, w_branch_a, w_branch_b, w_out, norm2_g,
        w_ffn_up, ffn_conv_w, ffn_conv_b, w_ffn_down,
    )
    return second_block(
        x, p_2, norm_mix_g_2, w_in_2, hg_lb_logits_2, hg_onorm_g_2, fox_f_bias_2,
        fox_q_norm_g_2, fox_k_norm_g_2, w_branch_a_2, w_branch_b_2, w_out_2, norm_ffn_g_2,
        w_ffn_gate_2, w_ffn_up_2, w_ffn_down_2, norm_ple_g_2, w_ple_gate_2, w_ple_proj_2,
    )


_drawn_inputs = setup_inputs


def setup_inputs(seed=0):
    import zlib

    import numpy as np

    out = dict(_drawn_inputs(seed))
    spreads = {}
    factors = {'norm1_g': 5.031,
     'q_norm_g': 8.0,
     'k_norm_g': 8.0,
     'rel_bias': 4.553,
     'norm2_g': 3.615,
     'ffn_conv_b': 7.32,
     'norm_mix_g_2': 6.45,
     'hg_lb_logits_2': 8.0,
     'hg_onorm_g_2': 8.0,
     'fox_q_norm_g_2': 21.637,
     'fox_k_norm_g_2': 8.0,
     'norm_ffn_g_2': 18.077,
     'norm_ple_g_2': 64.0,
     'p_2': 2.67,
     'w_ple_gate_2': 3.974,
     'w_ple_proj_2': 2.673}
    for name, (base, spread) in spreads.items():
        noise = np.random.default_rng([zlib.crc32(name.encode()), seed]).standard_normal(out[name].shape)
        drawn = base * np.exp(spread * noise) if base else spread * noise
        out[name] = __import__('jax').numpy.asarray(drawn.astype(out[name].dtype))
    for name, factor in factors.items():
        out[name] = (out[name] * factor).astype(out[name].dtype)
    return out
```

```python
import concourse.bass as bass
from concourse import mybir
from contextlib import ExitStack

F32 = mybir.dt.float32
F32R = mybir.dt.float32r
U32 = mybir.dt.uint32
ALU = mybir.AluOpType
ACT = mybir.ActivationFunctionType
AX = mybir.AxisListType

P = 128
S = 512
TB = S // P
D = 1024
DC = D // P
FF = 2816
FC = FF // P
NH = 8
HD = 64
HH = 4
CH = 64
NREL = 257
EPS = 1e-6
NEG = -1e30
SPLIT_SLOTS = 8
RAW_SLOTS = 4
LEVELS = (32, 16, 8, 4, 2, 1)
STEPS = TB * NH


class Phase:

    def __init__(self, name, kc, groups):
        self.name, self.kc, self.groups = name, kc, groups


PHASES = [Phase(*a) for a in (
    ("qB", 8, 1), ("kB", 8, 1), ("vB", 8, 1), ("qA", 8, 1), ("kA", 8, 1), ("vA", 8, 1),
    ("gateB", 8, 2), ("branchB", 4, 2), ("gateA", 8, 2), ("branchA", 4, 2), ("out1", 8, 2),
    ("up1", 8, 11), ("down1", 22, 2),
    ("hq", 8, 1), ("hf", 8, 1), ("hi", 8, 1), ("hg", 8, 1), ("fq", 8, 1), ("fk", 8, 1), ("fv", 8, 1),
    ("gateH", 8, 2), ("branchH", 4, 2), ("gateF", 8, 2), ("branchF", 4, 2), ("out2", 8, 2),
    ("up2", 8, 11), ("down2", 22, 2), ("pgate", 8, 2), ("pproj", 2, 2))]
PH = {}
_slot = _group = 0
for _p in PHASES:
    _p.slot0, _p.group0 = _slot, _group
    _slot += _p.kc * _p.groups
    _group += _p.groups
    PH[_p.name] = _p
SLOTS = _slot
OWNER = {name: "adad" for name in ("qB", "kB", "vB", "qA", "kA", "vA", "hi", "fq", "fk", "fv")}
OWNER |= {name: "aaaa" for name in ("gateB", "gateA", "gateH", "gateF", "pgate", "hq", "hf", "hg")}
OWNER |= {name: "dddd" for name in ("branchB", "branchA", "branchH", "branchF", "out1", "out2",
                                    "down1", "down2", "pproj", "up1")}
OWNER["up2"] = "aadd"


def taken_before(name, g, who):
    total = 0
    for p in PHASES:
        per = OWNER[p.name].count(who)
        if p.name == name:
            return g * per + total if per else total
        total += per * p.groups
    raise KeyError(name)


def previous_group(name, g):
    if g:
        return name, g - 1
    i = PHASES.index(PH[name])
    return (PHASES[i - 1].name, PHASES[i - 1].groups - 1) if i else None



def make_schedule():
    s = []

    def groups(name, extras=(), g0=0, g1=None):
        p = PH[name]
        extras = list(extras)
        todo = [(g, k) for g in range(g0, p.groups if g1 is None else g1) for k in range(p.kc)]
        n, done = len(todo), 0
        for i, (g, k) in enumerate(todo):
            s.append(("slot", name, g, k))
            if k == p.kc - 1:
                s.append(("take", name, g))
            upto = (i + 1) * len(extras) // n
            s.extend(extras[done:upto])
            done = upto

    def spread(names, extras):
        n = sum(PH[x].kc * PH[x].groups for x in names)
        at = done = 0
        for x in names:
            at += PH[x].kc * PH[x].groups
            upto = at * len(extras) // n
            groups(x, extras[done:upto])
            done = upto

    def attention(kind):
        return [("att", kind, i) for i in range(STEPS + 5)]

    s.append(("start",))
    s.extend(("sumsq", 0, j) for j in range(DC))
    s.append(("norm", 0))
    groups("qB")
    groups("kB", [("bias", h) for h in range(NH)])
    groups("vB")
    b_steps, a_steps = attention("B"), attention("A")
    spread(["qA"], b_steps[:11])
    groups("kA", b_steps[11:20] + [("qknorm", "qA", n) for n in range(4)])
    groups("vA", b_steps[20:] + [("qknorm", "kA", n) for n in range(4)])
    spread(["gateB", "branchB"], a_steps)
    groups("gateA")
    groups("branchA")
    sums = lambda n, a, b: [("sumsq", n, j) for j in range(a, b)]
    groups("out1", g1=1)
    groups("out1", [None] * 4 + sums(1, 0, 4), g0=1)
    s.extend(sums(1, 4, 8))
    s.append(("norm", 1))
    s.append(("up", "up1"))
    groups("down1", g1=1)
    groups("down1", [None] * 4 + sums(2, 0, 4), g0=1)
    s.extend(sums(2, 4, 8))
    s.append(("norm", 2))
    groups("hq")
    groups("hf")
    s.append(("hg_decay",))
    groups("hi", [("foxf",)])
    groups("hg", [("hg_level", x) for x in range(2)])
    hg = [("hg_level", x) for x in range(2, 7)]
    spread(["fq"], hg)
    groups("fk", [("hg_scale",), ("hg_kt",)] + [("qknorm", "fq", n) for n in range(4)])
    groups("fv", [("hg_state", c) for c in range(7)] + [("qknorm", "fk", n) for n in range(4)]
           + [("foxc", h) for h in range(0)])
    s.extend(("hg_out", p) for p in range(TB + 1))
    s.extend(("foxc", h) for h in range(NH))
    f_steps = attention("F")
    spread(["gateH", "branchH"], f_steps)
    groups("gateF")
    groups("branchF")
    groups("out2", g1=1)
    groups("out2", [None] * 4 + sums(3, 0, 4), g0=1)
    s.extend(sums(3, 4, 8))
    s.append(("norm", 3))
    s.append(("up", "up2"))
    groups("down2", g1=1)
    groups("down2", [None] * 4 + sums(4, 0, 4), g0=1)
    s.extend(sums(4, 4, 8))
    s.append(("norm", 4))
    groups("pgate", [("pT",)])
    groups("pproj")
    s.append(("finish",))
    return [x for x in s if x is not None]


SCHEDULE = make_schedule()
PAIRS = ("SC0", "SC1", "PT", "OUT")


def bank_uses():
    use, count = {}, [0] * 8

    def take(key, bank):
        use[key] = (bank, count[bank])
        count[bank] += 1

    for x in SCHEDULE:
        if x[0] == "start":
            for j in range(4, 8):
                take(("x", j), j)
        elif x[0] == "sumsq" and x[2] == 0:
            take(("norm", x[1]), 4)
        elif x[0] == "qknorm":
            take(x, 4 + x[2] % 2)
        elif x[0] == "bias":
            take(x, 4 + x[1] % 2)
        elif x[0] == "foxf":
            take(("foxf", 0), 5)
            take(("foxf", 1), 5)
            take(("foxf", 2), 5)
        elif x[0] == "foxc":
            take(x, 4 + x[1] % 2)
        elif x[0] == "att":
            kind, i = x[1:]
            if i < STEPS:
                take(("sc", kind, i), 4 + i % 2)
            if 0 <= i - 2 < STEPS:
                take(("pt", kind, i - 2), 6)
            j = i - 3
            if 0 <= j < STEPS and j % NH == 0:
                take(("out", kind, j // NH), 7)
            j = i - 5 + 1
            if j > 0 and j % NH == 0:
                take(("ot", kind, j // NH - 1), 6)
        elif x[0] == "hg_level":
            for h in range(HH):
                take(("lev", x[1], h), 4 + h)
        elif x[0] == "hg_kt":
            for h in range(HH):
                take(("kt", h), 4 + h)
        elif x[0] == "hg_state":
            take(("st", x[1]), 4 + x[1] % 2)
        elif x[0] == "hg_out":
            if x[1] < TB:
                take(("ho", x[1]), 4 + x[1] % 2)
            if x[1] > 0:
                take(("hot", x[1] - 1), 6)
        elif x[0] == "up":
            for j in range(4, 8):
                use[(x[1], j)] = (j, count[j])
        elif x[0] == "pT":
            take(("pT", 0), 4)
            take(("pT", 1), 5)
        elif x[0] == "finish":
            for j in range(8):
                take(("fin", j), 4 + j % 4)
    return use


USE = bank_uses()


def two_block_kernel(nc, a, out):
    ctx = ExitStack()
    with ctx:
        KB = 1024
        base = nc.sbuf_base + 64
        base += -base % 64
        at = [base]

        def place(name, shape, dt=F32, offset=None):
            n = 4
            for d in shape[1:]:
                n *= d
            if offset is None:
                offset = at[0]
                at[0] += n + (-n % 64)
            return nc.alloc_sbuf_tensor_at(name, shape, dt, offset=offset)

        xT = place("xT", [P, DC, S])
        h_hi = place("h_hi", [P, DC, S], F32R)
        h_lo = place("h_lo", [P, DC, S], F32R)
        w_raw = place("w_raw", [P, RAW_SLOTS, S])
        w_hi = place("w_hi", [P, SPLIT_SLOTS, S], F32R)
        w_lo = place("w_lo", [P, SPLIT_SLOTS, S], F32R)
        ident = place("ident", [P, P])
        mean_d = place("mean_d", [P, P])
        mean_h = place("mean_h", [P, P])
        ones = place("ones", [P, P])
        reverse = place("reverse", [P, P])
        tri = place("tri", [P, P])
        strict = place("strict", [P, P])
        causal = place("causal", [P, P])
        level_mask = place("level_mask", [P, 7, P])
        chunk_start = place("chunk_start", [P, S])
        vec = place("vec", [P, 53 + 176])
        qk_gain = place("qk_gain", [P, 2])
        lb = place("lb", [P, 6, HH])
        mneg = place("mneg", [P, 2, STEPS])
        rsum = place("rsum", [P, 2, STEPS])
        rinv = place("rinv", [P, 2, STEPS])
        fbias = place("fbias", [P, NH])
        fx = place("fx", [P, 3, TB, NH])
        ctok = place("ctok", [P, TB, NH])
        decay = place("decay", [P, HH, NH])
        hstat = place("hstat", [P, TB, 3, HH])
        wf_raw = place("wf_raw", [P, DC, NH])
        wf_hi = place("wf_hi", [P, DC, NH], F32R)
        wf_lo = place("wf_lo", [P, DC, NH], F32R)
        U = at[0]
        assert U + 112 * KB <= nc.sbuf_usable_end, (U, nc.sbuf_usable_end)

        def u(name, kb, shape, dt=F32):
            return place(name, shape, dt, offset=U + kb * KB)

        work = [u(f"work{i}", 96 + 2 * i, [P, S]) for i in range(8)]
        sq_ring = [work[6], work[7]]
        xtok = u("xtok", 0, [P, TB, D])
        vrows = u("vrows", 16, [P, 3, P])
        rb = u("rb", 88, [NH, NREL])
        rb_ext = u("rb_ext", 90, [NH, 640])
        qk1 = {"qB": u("qB", 0, [P, 4, S]), "kB": u("kB", 8, [P, 4, S]), "qA": u("qA", 24, [P, 4, S]),
               "kA": u("kA", 32, [P, 4, S]), "fq": u("fq", 72, [P, 4, S]), "fk": u("fk", 80, [P, 4, S])}
        vtok = {"vB": u("vB", 16, [P, 4, S]), "vA": u("vA", 40, [P, 4, S]),
                "fv": u("fv", 88, [P, 4, S]), "hi": u("hv", 24, [P, 4, S])}
        bias_mask = u("bias_mask", 48, [P, NH, S])
        bias_up = u("bias_up", 64, [P, NH, S])
        yB = (u("yB_hi", 64, [P, 4, S], F32R), u("yB_lo", 72, [P, 4, S], F32R))
        yA = (u("yA_hi", 80, [P, 4, S], F32R), u("yA_lo", 88, [P, 4, S], F32R))
        keep = [u(f"keep{i}", 80 + 2 * i, [P, S]) for i in range(2)]
        after = [u(f"after{i}", 84 + 2 * i, [P, S]) for i in range(2)]
        sig = {"gateB": u("sigB", 0, [P, DC, S]), "gateA": u("sigA", 24, [P, DC, S]),
               "gateH": u("sigH", 56, [P, DC, S]), "gateF": u("sigF", 72, [P, DC, S]),
               "pgate": u("sigP", 16, [P, DC, S])}
        g_hi = u("g_hi", 0, [P, FC, S], F32R)
        g_lo = u("g_lo", 44, [P, FC, S], F32R)
        acc = u("acc", 88, [P, 4, S])
        hq = u("hq", 0, [P, HH, S])
        hk = u("hk", 8, [P, HH, S])
        hb = u("hb", 16, [P, HH, S])
        hv = vtok["hi"]
        hgate = u("hgate", 32, [P, HH, S])
        hS = u("hS", 40, [P, HH, S])
        hE = u("hE", 48, [P, HH, S])
        hQ = u("hQ", 56, [P, HH, S])
        hK = u("hK", 64, [P, HH, S])
        state = u("state", 0, [P, NH, S])
        hKt = u("hKt", 16, [P, HH, S])
        yH = (u("yH_hi", 48, [P, 4, S], F32R), u("yH_lo", 16, [P, 4, S], F32R))
        yF = (u("yF_hi", 0, [P, 4, S], F32R), u("yF_lo", 8, [P, 4, S], F32R))
        cT = work[5]
        c_rows = u("c_rows", 24, [P, NH, S])
        ptok = u("ptok", 0, [P, TB, 256])
        pT_hi = u("pT_hi", 4, [P, 2, S], F32R)
        pT_lo = u("pT_lo", 8, [P, 2, S], F32R)
        otok = u("otok", 32, [P, TB, D])

        ps = [ctx.enter_context(nc.psum_tensor(f"bank{i}", [P, S], F32)) for i in range(8)]
        bias_dram = nc.dram_tensor("bias_ext", (NH, 640), F32, kind="Internal").ap()

        def sem(name):
            return ctx.enter_context(nc.semaphore(name))

        raw_full = [sem(f"raw_full{i}") for i in range(RAW_SLOTS)]
        hi_full, lo_full = sem("hi_full"), sem("lo_full")
        slot_used = sem("slot_used")
        tile_done = sem("tile_done")
        taken = {"a": sem("taken_act"), "d": sem("taken_dve")}
        act_seq, dve_seq, pool_seq = sem("act_seq"), sem("dve_seq"), sem("pool_seq")
        bank_free = {b: sem(f"bank_free{b}") for b in range(4, 8)}
        const_ready = sem("const_ready")
        const_dve = sem("const_dve")
        x_full, vec_full, rb_full, bias_full, small_full = (sem(n) for n in (
            "x_full", "vec_full", "rb_full", "bias_full", "small_full"))
        vec_done, vec_ready, rb_ready, scratch_full = (sem(n) for n in (
            "vec_done", "vec_ready", "rb_ready", "scratch_full"))
        xt_done = sem("xt_done")
        x_ready = sem("x_ready")
        sq_ready, sq_used = sem("sq_ready"), sem("sq_used")
        rstd_ready = sem("rstd_ready")
        hf_ready, hhi_ready, hlo_ready = sem("hf_ready"), sem("hhi_ready"), sem("hlo_ready")
        qkrs_ready = sem("qkrs_ready")
        qk_ready = {n: sem(f"{n}_ready") for n in ("qA", "kA", "fq", "fk")}
        A = {}
        for kind in "BAF":
            A[kind] = {n: sem(f"{n}{kind}") for n in (
                "sc_done", "s_ready", "p_ready", "tr_done", "pv_done", "ot_ready", "ot_done",
                "yhi", "ylo", "keep_ready", "beta_ready", "after_ready")}
        mix_ready, mixhi_ready, mixlo_ready = sem("mix_ready"), sem("mixhi_ready"), sem("mixlo_ready")
        up_sem = {n: {k: sem(f"{n}_{k}") for k in (
            "first", "conv1", "conv2", "silu", "prod", "hi", "lo")} for n in ("up1", "up2")}
        hgs = {n: sem(f"hg_{n}") for n in (
            "lb", "lb_exp", "fg", "k", "log", "b", "diff", "exp", "Q", "K", "lev_done", "merged", "zero",
            "eb", "el", "kt_done", "kt", "u_done", "state", "o_done", "o_sq", "o_ms", "o_rs",
            "o_tok", "ot_done", "y", "yhi", "ylo", "scale", "kd")}
        ff = {n: sem(f"fox_{n}") for n in (
            "w_hi", "w_lo", "mm", "x", "e", "l", "logf", "cmm", "c", "ct", "ctsb", "row_mm", "rows")}
        p_full, p_done, p_hi, p_lo = (sem(n) for n in ("p_full", "p_done", "p_hi", "p_lo"))
        fin_done, fin_copied, out_full = sem("fin_done"), sem("fin_copied"), sem("out_full")
        bias_mm, bias_ready = sem("bias_mm"), sem("bias_ready")

        def kinds(kind):
            return {"B": ("qB", "kB", "vB", yB), "A": ("qA", "kA", "vA", yA), "F": ("fq", "fk", "fv", yF)}[kind]


        def slots_used(e, name, g, k):
            p = PH[name]
            if k == p.kc - 1:
                e.wait_ge(tile_done, (g + (p.group0 + 1)) * 4)
            else:
                before = p.slot0 - p.group0
                e.wait_ge(slot_used, g * (p.kc - 1) + (before + k + 1))

        def tile_ready(e, name, g, n):
            e.wait_ge(tile_done, g * 4 + (PH[name].group0 * 4 + n + 1))

        def tile_taken(e, name, g, n):
            who = OWNER[name][n]
            e.wait_ge(taken[who], taken_before(name, g, who) + (OWNER[name][:n + 1].count(who)))

        def bank_wait(e, key):
            b, n = USE[key]
            if n:
                e.wait_ge(bank_free[b], n)
            return ps[b]

        def source(name, k, cols):
            r = slice(k * P, (k + 1) * P)
            win = {"qA": 0, "kA": 512, "vA": 1024, "qB": 1536, "kB": 2048, "vB": 2560,
                   "gateA": 3072, "gateB": 4096}
            win2 = {"hq": 0, "hf": 512, "hi": 1024, "hg": 1536, "fq": 2048, "fk": 2560, "fv": 3072,
                    "gateH": 3592, "gateF": 4616}
            rest = {"branchA": "w_branch_a", "branchB": "w_branch_b", "out1": "w_out",
                    "down1": "w_ffn_down", "branchH": "w_branch_a_2", "branchF": "w_branch_b_2",
                    "out2": "w_out_2", "down2": "w_ffn_down_2", "pgate": "w_ple_gate_2",
                    "pproj": "w_ple_proj_2"}
            if name == "up1":
                w = a["w_ffn_up"][0].rearrange("k (t c) -> k t c", t=2)
                return [(slice(0, 512), w[r, :, bass.ds(cols * 256, 256)])]
            if name == "up2":
                return [(slice(0, 256), a["w_ffn_gate_2"][0][r, bass.ds(cols * 256, 256)]),
                        (slice(256, 512), a["w_ffn_up_2"][0][r, bass.ds(cols * 256, 256)])]
            if name in win:
                w, c0 = a["w_in"][0], win[name]
            elif name in win2:
                w, c0 = a["w_in_2"][0], win2[name]
            else:
                w, c0 = a[rest[name]][0], 0
            return [(slice(0, 512), w[r, c0 + cols * 512:c0 + (cols + 1) * 512])]

        block = ctx.enter_context(nc.Block())

        @block.sync
        def _(e):
            for tb in range(TB):
                e.dma_start(xtok[:, tb, :], a["x"][0, tb * P:(tb + 1) * P, :]).then_inc(x_full, 16)
            gains = ("norm1_g", "norm2_g", "norm_mix_g_2", "norm_ffn_g_2", "norm_ple_g_2")
            for i, n in enumerate(gains):
                e.dma_start(vrows[8 * i:8 * i + 8, 0, :], a[n].rearrange("a (r c) -> (a r) c", c=P)).then_inc(vec_full, 16)
            for i, n in enumerate(("q_norm_g", "k_norm_g", "fox_q_norm_g_2", "fox_k_norm_g_2")):
                for half in range(2):
                    e.dma_start(vrows[40 + i:41 + i, 0, 64 * half:64 * half + 64], a[n]).then_inc(vec_full, 16)
            e.dma_start(vrows[44:45, 0, :], a["hg_onorm_g_2"]).then_inc(vec_full, 16)
            e.dma_start(vrows[45:53, 0, :], a["hg_lb_logits_2"].rearrange("a (r c) -> (a r) c", c=P)).then_inc(vec_full, 16)
            cw = a["ffn_conv_w"][0].rearrange("t (r c) -> t r c", c=P)
            for t in range(3):
                row = 44 * (t % 2)
                e.dma_start(vrows[row:row + 44, 1 + t // 2, :], cw[t]).then_inc(vec_full, 16)
            e.dma_start(vrows[44:88, 2, :], a["ffn_conv_b"][0].rearrange("(r c) -> r c", c=P)).then_inc(vec_full, 16)
            e.dma_start(rb[:, :], a["rel_bias"][0]).then_inc(rb_full, 16)
            e.dma_start(fbias[:, :], a["fox_f_bias_2"].to_broadcast([P, NH])).then_inc(small_full, 16)
            with nc.allow_non_contiguous_dma(reason="eight columns of the fused input projection"):
                e.dma_start(wf_raw[:, :, :], a["w_in_2"][0][:, 3584:3592].rearrange("(k p) c -> p k c", p=P)).then_inc(small_full, 16)

            def load(name, g, k, s):
                pos = (PH[name].slot0 + (g * PH[name].kc if isinstance(g, int) else 0) + k)
                if not (isinstance(g, int) and pos < RAW_SLOTS):
                    e.wait_ge(hi_full, s - (RAW_SLOTS - 1))
                    e.wait_ge(lo_full, s - (RAW_SLOTS - 1))
                pos %= RAW_SLOTS
                parts = source(name, k, g)
                for cols, src in parts:
                    dst = w_raw[:, pos, cols]
                    if name == "up1":
                        dst = dst.rearrange("p (t c) -> p t c", t=2)
                    e.dma_start(dst, src).then_inc(raw_full[pos], 32 // len(parts))

            for i, p in enumerate(PHASES):
                if p.name in ("up1", "up2"):
                    with e.Fori(0, p.groups) as g:
                        for k in range(p.kc):
                            load(p.name, g, k, g * p.kc + (p.slot0 + k))
                else:
                    for g in range(p.groups):
                        for k in range(p.kc):
                            load(p.name, g, k, p.slot0 + g * p.kc + k)
                if p.name == "qB":
                    e.wait_ge(rb_ready, 1)
                    e.dma_start(bias_dram, rb_ext[:, :]).then_inc(scratch_full, 16)
                    e.wait_ge(scratch_full, 16)
                    e.dma_start(bias_up[:, :, :], bass.AP(bias_dram.tensor, 0, [[1, P], [640, NH], [1, S]])).then_inc(bias_full, 16)
                if p.name == "pgate":
                    e.wait_ge(x_ready, 5 * DC)
                    e.dma_start(ptok[:, :, :], a["p_2"][0, 0].rearrange("(t p) c -> p t c", p=P)).then_inc(p_full, 16)
            for half in range(2):
                for tb in range(TB):
                    e.wait_ge(fin_copied, half * TB + tb + 1)
                    e.dma_start(out[0, tb * P:(tb + 1) * P, half * 512:(half + 1) * 512],
                                otok[:, tb, half * 512:(half + 1) * 512]).then_inc(out_full, 16)
            e.wait_ge(out_full, 2 * TB * 16)

        @block.gpsimd
        def _(e):
            seq = [0]

            def link(ins):
                seq[0] += 1
                ins.then_inc(pool_seq, 1)
                e.wait_ge(pool_seq, seq[0])

            def lo(pos, s):
                e.wait_ge(hi_full, s + 1)
                e.tensor_tensor(w_lo[:, pos % SPLIT_SLOTS, :], w_raw[:, pos % RAW_SLOTS, :],
                                w_hi[:, pos % SPLIT_SLOTS, :].bitcast(F32), ALU.subtract).then_inc(lo_full, 1)

            link(e.memset(ident[:, :], 0.0))
            link(e.affine_select(out=ident[:, :], in_=ident[:, :], compare_op=ALU.not_equal, fill=1.0,
                                 base=0, pattern=[[-1, P]], channel_multiplier=1))
            link(e.memset(reverse[:, :], 0.0))
            link(e.affine_select(out=reverse[:, :], in_=reverse[:, :], compare_op=ALU.not_equal, fill=1.0,
                                 base=1 - P, pattern=[[1, P]], channel_multiplier=1))
            e.nop().then_inc(const_ready, 1)
            link(e.memset(strict[:, :], 0.0))
            link(e.affine_select(out=strict[:, :], in_=strict[:, :], compare_op=ALU.is_gt, fill=NEG,
                                 base=0, pattern=[[-1, P]], channel_multiplier=1))
            link(e.memset(causal[:, :], 0.0))
            link(e.affine_select(out=causal[:, :], in_=causal[:, :], compare_op=ALU.is_ge, fill=NEG,
                                 base=0, pattern=[[-1, P]], channel_multiplier=1))
            link(e.memset(tri[:, :], 1.0))
            link(e.affine_select(out=tri[:, :], in_=tri[:, :], compare_op=ALU.is_ge, fill=0.0,
                                 base=0, pattern=[[1, P]], channel_multiplier=-1))
            for x in SCHEDULE:
                if x[0] == "start":
                    for s in range(SPLIT_SLOTS):
                        lo(s, s)
                    link(e.memset(level_mask[:, :, :], 0.0))
                    for x, m in enumerate(LEVELS):
                        v = level_mask[:, x, :].rearrange("p (n w) -> p n w", w=2 * m)[:, :, m:]
                        n = P // (2 * m)
                        link(e.memset(v, 1.0))
                        link(e.affine_select(out=v, in_=v, compare_op=ALU.is_ge, fill=0.0, base=0,
                                             pattern=[[-2 * m, n], [0, m]], channel_multiplier=1))
                        link(e.affine_select(out=v, in_=v, compare_op=ALU.is_ge, fill=0.0, base=m - 1,
                                             pattern=[[2 * m, n], [0, m]], channel_multiplier=-1))
                    link(e.affine_select(out=level_mask[:, 6, :], in_=level_mask[:, 6, :], compare_op=ALU.not_equal,
                                         fill=1.0, base=0, pattern=[[-1, P]], channel_multiplier=1))
                    e.nop().then_inc(const_ready, 1)
                elif x[0] == "slot":
                    s = PH[x[1]].slot0 + x[2] * PH[x[1]].kc + x[3] + SPLIT_SLOTS
                    if s < SLOTS:
                        lo(s, s)
                elif x[0] == "up":
                    p = PH[x[1]]
                    with e.Fori(0, p.groups) as g:
                        for k in range(p.kc):
                            s = p.slot0 + k + SPLIT_SLOTS
                            lo(s, g * p.kc + s)
                elif x[0] == "att" and x[1] == "B" and 0 <= x[2] - 1 < STEPS:
                    i, n = x[2] - 1, ((x[2] - 1) // NH + 1) * P
                    e.wait_ge(A["B"]["beta_ready"], i + 1)
                    e.wait_ge(A["B"]["after_ready"], i + 1)
                    w = work[i % 4]
                    e.tensor_tensor(w[:, 0:n], w[:, 0:n], after[i % 2][:, 0:n], ALU.mult).then_inc(A["B"]["p_ready"], 1)
                elif x[0] == "hg_decay":
                    e.wait_ge(x_ready, 3 * DC)
                    link(e.memset(hQ[:, :, :], 0.0))
                    e.memset(hK[:, :, :], 0.0).then_inc(hgs["zero"], 1)
                elif x[0] == "hg_level" and x[1] < 6:
                    m = LEVELS[x[1]]
                    k_, e_, o_ = (t[:, :, :].rearrange("p h (n w) -> p (h n) w", w=2 * m)[:, :, 0:m] for t in (hk, hE, hK))
                    e.wait_ge(hgs["zero"], 1)
                    e.wait_ge(hgs["exp"], x[1] + 1)
                    if x[1]:
                        e.wait_ge(hgs["lev_done"], HH * x[1])
                    e.tensor_tensor(o_, k_, e_, ALU.mult).then_inc(hgs["K"], 1)

        def att_act(e, kind, i):
            a_, ring = A[kind], work[i % 4]
            n = (i // NH + 1) * P
            if i < STEPS and kind == "B":
                e.wait_ge(a_["s_ready"], i + 1)
                if i >= 2:
                    e.wait_ge(a_["after_ready"], i - 1)
                e.activation(keep[i % 2][:, 0:n], ring[:, 0:n], ACT.Sigmoid, scale=-1.0).then_inc(a_["keep_ready"], 1)
                e.activation(ring[:, 0:n], ring[:, 0:n], ACT.Sigmoid).then_inc(a_["beta_ready"], 1)
            elif i < STEPS:
                k = 0 if kind == "A" else 1
                e.wait_ge(a_["s_ready"], i + 1)
                e.activation(ring[:, 0:n], ring[:, 0:n], ACT.Exp, scale=-1.0 if kind == "A" else 1.0,
                             bias=mneg[:, k, i:i + 1], accum_out=rsum[:, k, i:i + 1]).then_inc(a_["p_ready"], 1)
            j = i - 2
            if kind == "F" and 0 <= j < STEPS:
                pt_out(e, kind, j, lambda o, s: e.activation(o, s, ACT.Copy))
            j = i - 4
            if j > 0 and j % NH == 0:
                qb = j // NH - 1
                e.wait_ge(a_["ot_done"], qb + 1)
                b, use = USE[("ot", kind, qb)]
                y = kinds(kind)[3]
                e.activation(y[0][:, :, qb * P:(qb + 1) * P], ps[b][:, :].rearrange("p (c t) -> p c t", c=4),
                             ACT.Copy).then_inc(a_["yhi"], 1)

        def pt_out(e, kind, j, copy):
            a_ = A[kind]
            n = (j // NH + 1) * P
            e.wait_ge(a_["tr_done"], j + 1)
            if j >= 2:
                e.wait_ge(a_["pv_done"], j - 1)
            b, use = USE[("pt", kind, j)]
            copy(work[4 + j % 2][:, 0:n], ps[b][:, 0:n]).then_inc(bank_free[b], 1)

        def conv_col(tap, tile, half):
            return bass.ds(tile + (53 + 44 * tap + FC * half), 1) if not isinstance(tile, int) else \
                slice(53 + 44 * tap + FC * half + tile, 54 + 44 * tap + FC * half + tile)

        def up_act(e, name, hi):
            p, q = PH[name], up_sem[name]

            def group(g, u_):
                banks = 4 * u_
                for k in range(p.kc):
                    s = p.slot0 + k + SPLIT_SLOTS
                    st = s + (g * p.kc if isinstance(g, int) else 0)
                    hi(st if isinstance(g, int) else s, g * p.kc + s, name, g, k)
                if name == "up1":
                    for n in range(4):
                        tile_ready(e, name, g, n)
                        if not isinstance(g, int) or g > 0:
                            e.wait_ge(q["lo"], g * 2)
                        e.activation(acc[:, n, :], ps[banks + n][:, :], ACT.Identity,
                                     bias=vec[:, conv_col(3, g * 2 + n % 2, n // 2)],
                                     scale=vec[:, conv_col(2, g * 2 + n % 2, n // 2)]).then_inc(q["first"], 1)
                    for n in range(2):
                        e.wait_ge(taken["d"], taken_before(name, g, "d") + n + 1)
                        e.activation(acc[:, n, :], acc[:, n, :], ACT.Silu).then_inc(q["silu"], 1)
                else:
                    for n in range(2):
                        tile_ready(e, name, g, n)
                        if not isinstance(g, int) or g > 0:
                            e.wait_ge(q["lo"], g * 2 - 1 + n)
                        e.activation(acc[:, n, :], ps[banks + n][:, :], ACT.Silu).then_inc(taken["a"], 1)
                for n in range(2):
                    e.wait_ge(q["prod"], g * 2 + n + 1)
                    dst = g_hi[:, bass.ds(g * 2 + n, 1), :].rearrange("p a t -> p (a t)")
                    e.wait_ge(const_ready, 2)
                    e.activation(dst, acc[:, n, :], ACT.Copy).then_inc(q["hi"], 1)

            up_groups(e, p, group)

        def up_groups(e, p, group):
            group(0, 0)
            group(1, 1)
            with e.Fori(1, p.groups // 2) as it:
                group(it * 2, 0)
                group(it * 2 + 1, 1)
            group(p.groups - 1, 0)

        @block.scalar
        def _(e):
            seq = [0]

            def link(ins):
                seq[0] += 1
                ins.then_inc(act_seq, 1)
                e.wait_ge(act_seq, seq[0])

            def hi(pos, s, name=None, g=None, k=None):
                r = pos % RAW_SLOTS
                e.wait_ge(raw_full[r], (s - pos) * (32 // RAW_SLOTS) + 32 * (pos // RAW_SLOTS + 1))
                if name:
                    slots_used(e, name, g, k)
                e.activation(w_hi[:, pos % SPLIT_SLOTS, :], w_raw[:, r, :], ACT.Copy).then_inc(hi_full, 1)

            sq_n = [0]

            def square(src, ready=None):
                n = sq_n[0]
                sq_n[0] += 1
                if n >= 2:
                    e.wait_ge(sq_used, n - 1)
                e.activation(sq_ring[n % 2][:, :], src, ACT.Square).then_inc(sq_ready, 1)

            for x in SCHEDULE:
                what = x[0]
                if what == "start":
                    for s in range(SPLIT_SLOTS):
                        hi(s, s)
                elif what == "slot":
                    _, name, g, k = x
                    s = PH[name].slot0 + g * PH[name].kc + k + SPLIT_SLOTS
                    if s < SLOTS:
                        hi(s, s, name, g, k)
                elif what == "sumsq":
                    e.wait_ge(x_ready, x[1] * DC + x[2] + 1)
                    square(xT[:, x[2], :])
                elif what == "norm":
                    e.wait_ge(sq_used, sq_n[0])
                    link(e.activation(work[3][:, :], ps[4][:, :], ACT.Ln, bias=EPS))
                    e.activation(work[2][:, :], work[3][:, :], ACT.Exp, scale=-0.5).then_inc(rstd_ready, 1)
                    for j in range(DC):
                        e.wait_ge(hf_ready, x[1] * DC + j + 1)
                        e.activation(h_hi[:, j, :], work[j % 2][:, :], ACT.Copy).then_inc(hhi_ready, 1)
                elif what == "take":
                    _, name, g = x
                    for n in range(4):
                        own = OWNER[name][n] == "a"
                        if own:
                            tile_ready(e, name, g, n)
                        if not own:
                            pass
                        elif name in ("qB", "kB", "qA", "kA", "fq", "fk"):
                            e.activation(qk1[name][:, n, :], ps[n][:, :], ACT.Copy,
                                         scale=HD ** -0.5 if name == "qB" else 1.0).then_inc(taken["a"], 1)
                        elif name in vtok:
                            e.activation(vtok[name][:, n, :], ps[n][:, :], ACT.Copy).then_inc(taken["a"], 1)
                        elif name in sig:
                            e.activation(sig[name][:, 4 * g + n, :], ps[n][:, :], ACT.Sigmoid).then_inc(taken["a"], 1)
                        elif name in ("hq", "hg"):
                            dst = hq if name == "hq" else hgate
                            e.activation(dst[:, n, :], ps[n][:, :], ACT.Silu).then_inc(taken["a"], 1)
                        elif name == "hf":
                            e.activation(hk[:, n, :], ps[n][:, :], ACT.Sigmoid).then_inc(taken["a"], 1)
                    if name in ("branchA", "branchF"):
                        for n in range(4):
                            j = 4 * g + n
                            e.wait_ge(mix_ready, (DC if name == "branchF" else 0) + j + 1)
                            e.activation(h_hi[:, j, :], sig["gateA" if name == "branchA" else "gateF"][:, j, :],
                                         ACT.Copy).then_inc(mixhi_ready, 1)
                elif what == "qknorm":
                    _, name, n = x
                    tile_taken(e, name, 0, n)
                    n_sq = sq_n[0]
                    sq_n[0] += 1
                    count = {"qA": 0, "kA": 4, "fq": 8, "fk": 12}[name] + n
                    if count:
                        prev = [(m, c) for m in ("qA", "kA", "fq", "fk") for c in range(4)][count - 1]
                        e.wait_ge(qk_ready[prev[0]], prev[1] + 1)
                    e.activation(work[7][:, :], qk1[name][:, n, :], ACT.Square).then_inc(sq_ready, 1)
                    e.wait_ge(sq_used, n_sq + 1)
                    b, use = USE[x]
                    link(e.activation(work[7][:, :], ps[b][:, :], ACT.Ln, bias=EPS))
                    e.nop().then_inc(bank_free[b], 1)
                    e.activation(work[7][:, :], work[7][:, :], ACT.Exp, scale=-0.5).then_inc(qkrs_ready, 1)
                elif what == "att":
                    att_act(e, x[1], x[2])
                elif what == "up":
                    up_act(e, x[1], hi)
                elif what == "foxf":
                    e.wait_ge(small_full, 32)
                    e.activation(wf_hi[:, :, :], wf_raw[:, :, :], ACT.Copy).then_inc(ff["w_hi"], 1)
                    e.wait_ge(ff["x"], 1)
                    link(e.activation(fx[:, 1, :, :], fx[:, 1, :, :], ACT.Exp))
                    e.activation(fx[:, 1, :, :], fx[:, 1, :, :], ACT.Ln, bias=1.0).then_inc(ff["l"], 1)
                elif what == "hg_decay":
                    e.wait_ge(hgs["lb"], 1)
                    e.activation(lb[:, 1:3, :], lb[:, 1:3, :], ACT.Exp).then_inc(hgs["lb_exp"], 1)
                    e.wait_ge(hgs["fg"], 1)
                    e.activation(hE[:, :, :], hE[:, :, :], ACT.Ln).then_inc(hgs["log"], 1)
                elif what == "hg_level" and x[1] < 6:
                    e.wait_ge(hgs["diff"], x[1] + 1)
                    e.activation(hE[:, :, :], hE[:, :, :], ACT.Exp).then_inc(hgs["exp"], 1)
                elif what == "hg_scale":
                    e.wait_ge(hgs["K"], 6)
                    e.wait_ge(hgs["Q"], 6)
                    e.activation(hE[:, :, :], hb[:, :, :], ACT.Exp).then_inc(hgs["eb"], 1)
                    e.wait_ge(hgs["kd"], 1)
                    e.activation(hK[:, :, :], hK[:, :, :], ACT.Exp).then_inc(hgs["el"], 1)
                elif what == "hg_kt":
                    for h in range(HH):
                        e.wait_ge(hgs["kt_done"], h + 1)
                        b, use = USE[("kt", h)]
                        e.activation(hKt[:, h, :], ps[b][:, :], ACT.Copy).then_inc(bank_free[b], 1)
                elif what == "hg_out":
                    if x[1] < TB:
                        pr = x[1]
                        b, use = USE[("ho", pr)]
                        e.wait_ge(hgs["o_done"], pr + 1)
                        if pr:
                            e.wait_ge(hgs["o_ms"], pr)
                        e.activation(work[0][:, :], ps[b][:, :], ACT.Square).then_inc(hgs["o_sq"], 1)
                        e.wait_ge(hgs["o_ms"], pr + 1)
                        link(e.activation(hstat[:, pr, 1, :], hstat[:, pr, 0, :], ACT.Ln, bias=EPS, scale=1.0 / P))
                        e.activation(hstat[:, pr, 2, :], hstat[:, pr, 1, :], ACT.Exp, scale=-0.5).then_inc(hgs["o_rs"], 1)
                    if x[1] > 0:
                        pr = x[1] - 1
                        e.wait_ge(hgs["y"], pr + 1)
                        e.activation(yH[0][:, :, pr * P:(pr + 1) * P], work[2 + pr % 2][:, :].rearrange("p (h t) -> p h t", h=HH),
                                     ACT.Copy).then_inc(hgs["yhi"], 1)
                elif what == "pT":
                    for c in range(2):
                        b, use = USE[("pT", c)]
                        e.wait_ge(p_done, c + 1)
                        e.activation(pT_hi[:, c, :], ps[b][:, :], ACT.Copy).then_inc(p_hi, 1)
                elif what == "finish":
                    pass

        def take_dve(e, name, g, link):
            for n in range(4):
                if OWNER[name][n] != "d":
                    continue
                tile_ready(e, name, g, n)
                j = 4 * g + n
                if name in ("qB", "kB", "qA", "kA", "fq", "fk"):
                    e.tensor_scalar(qk1[name][:, n, :], ps[n][:, :], HD ** -0.5 if name == "qB" else 1.0, None,
                                    ALU.mult).then_inc(taken["d"], 1)
                elif name in vtok:
                    e.tensor_copy(vtok[name][:, n, :], ps[n][:, :]).then_inc(taken["d"], 1)
                elif name in ("branchB", "branchH"):
                    t = sig["gate" + name[-1]][:, j, :]
                    tile_taken(e, "gate" + name[-1], g, n)
                    e.tensor_tensor(t, ps[n][:, :], t, ALU.mult).then_inc(taken["d"], 1)
                elif name in ("branchA", "branchF"):
                    first, second = ("gateB", "gateA") if name == "branchA" else ("gateH", "gateF")
                    t = sig[second][:, j, :]
                    tile_taken(e, second, g, n)
                    e.tensor_tensor(t, ps[n][:, :], t, ALU.mult).then_inc(taken["d"], 1)
                    e.wait_ge(taken["d"], taken_before(name, g, "d") + n + 1)
                    e.tensor_tensor(t, t, sig[first][:, j, :], ALU.add).then_inc(mix_ready, 1)
                elif name in ("out1", "out2", "down1", "down2"):
                    k = {"out1": 1, "down1": 2, "out2": 3, "down2": 4}[name]
                    e.tensor_tensor(xT[:, j, :], ps[n][:, :], xT[:, j, :], ALU.add).then_inc(x_ready, 1)
                    e.wait_ge(x_ready, k * DC + j + 1)
                    e.nop().then_inc(taken["d"], 1)
                elif name == "pproj":
                    t = sig["pgate"][:, j, :]
                    tile_taken(e, "pgate", g, n)
                    e.tensor_tensor(t, ps[n][:, :], t, ALU.mult).then_inc(taken["d"], 1)
                    e.wait_ge(taken["d"], taken_before(name, g, "d") + n + 1)
                    e.tensor_tensor(xT[:, j, :], xT[:, j, :], t, ALU.add).then_inc(x_ready, 1)
            if name in ("branchA", "branchF"):
                for n in range(4):
                    j = 4 * g + n
                    e.wait_ge(mixhi_ready, (DC if name == "branchF" else 0) + j + 1)
                    e.tensor_tensor(h_lo[:, j, :], sig["gateA" if name == "branchA" else "gateF"][:, j, :],
                                    h_hi[:, j, :].bitcast(F32), ALU.subtract).then_inc(mixlo_ready, 1)

        def att_dve(e, kind, i, link):
            a_, ring = A[kind], work[i % 4]
            qb, h = divmod(i, NH)
            n = (qb + 1) * P
            if i < STEPS:
                e.wait_ge(a_["sc_done"], i + 1)
                if i >= 4:
                    e.wait_ge(a_["tr_done"], i - 3)
                b, use = USE[("sc", kind, i)]
                if kind == "B":
                    if qb:
                        e.tensor_copy(ring[:, 0:n - P], ps[b][:, 0:n - P])
                    link(e.tensor_tensor(ring[:, n - P:n], ps[b][:, n - P:n], strict[:, :], ALU.add))
                    e.nop().then_inc(bank_free[b], 1)
                    e.nop().then_inc(a_["s_ready"], 1)
                elif kind == "A":
                    if i == 0:
                        e.wait_ge(bias_ready, NH)
                        link(e.tensor_scalar(bias_mask[0:64, :, S - 64:S], bias_mask[0:64, :, S - 64:S], NEG, None, ALU.add))
                    link(e.tensor_tensor_reduce(out=ring[:, 0:n], in0=ps[b][:, 0:n], in1=bias_mask[:, h, S - n:S],
                                                scale=-1.0, scalar=3e38, op0=ALU.add, op1=ALU.min,
                                                accum_out=mneg[:, 0, i:i + 1]))
                    e.nop().then_inc(bank_free[b], 1)
                    e.nop().then_inc(a_["s_ready"], 1)
                else:
                    link(e.scalar_tensor_tensor(out=ring[:, 0:n], in0=ps[b][:, 0:n], scalar=ctok[:, qb, h:h + 1],
                                                in1=c_rows[:, h, 0:n], op0=ALU.add, op1=ALU.add))
                    e.nop().then_inc(bank_free[b], 1)
                    link(e.tensor_tensor(ring[:, n - P:n], ring[:, n - P:n], causal[:, :], ALU.add))
                    e.tensor_reduce(mneg[:, 1, i:i + 1], ring[:, 0:n], axis=AX.X, op=ALU.max, negate=True).then_inc(a_["s_ready"], 1)
            j = i - 1
            if kind == "B" and 0 <= j < STEPS:
                m = (j // NH + 1) * P
                e.wait_ge(a_["keep_ready"], j + 1)
                if j >= 2:
                    e.wait_ge(a_["p_ready"], j - 1)
                k_, o_ = keep[j % 2], after[j % 2]
                link(e.memset(o_[:, m - 1:m], 1.0))
                rev = lambda t, lo_, hi_: t[:, hi_ - 1:(lo_ - 1 if lo_ else None):-1]
                e.tensor_tensor_scan(rev(o_, 0, m - 1), rev(k_, 1, m), rev(k_, 1, m), 1.0,
                                     ALU.mult, ALU.bypass).then_inc(a_["after_ready"], 1)
            j = i - 2
            if kind != "F" and 0 <= j < STEPS:
                pt_out(e, kind, j, lambda o, s: e.tensor_copy(o, s))
            j = i - 3
            if 0 <= j < STEPS and j % NH == NH - 1:
                q = j // NH
                e.wait_ge(a_["pv_done"], j + 1)
                if q:
                    e.wait_ge(a_["ot_done"], q)
                b, use = USE[("out", kind, q)]
                o3 = work[6][:, :].rearrange("p (h d) -> p h d", h=NH)
                p3 = ps[b][:, :].rearrange("p (h d) -> p h d", h=NH)
                if kind == "B":
                    link(e.tensor_copy(o3, p3))
                else:
                    k = 0 if kind == "A" else 1
                    c = slice(q * NH, (q + 1) * NH)
                    link(e.reciprocal(rinv[:, k, c], rsum[:, k, c]))
                    link(e.tensor_tensor(o3, p3, rinv[:, k, c][:, :, None].to_broadcast([P, NH, HD]), ALU.mult))
                e.nop().then_inc(bank_free[b], 1)
                e.nop().then_inc(a_["ot_ready"], 1)
            j = i - 4
            if j > 0 and j % NH == 0:
                q = j // NH - 1
                e.wait_ge(a_["yhi"], q + 1)
                b, use = USE[("ot", kind, q)]
                y = kinds(kind)[3]
                c = slice(q * P, (q + 1) * P)
                link(e.tensor_tensor(y[1][:, :, c], ps[b][:, :].rearrange("p (c t) -> p c t", c=4),
                                     y[0][:, :, c].bitcast(F32), ALU.subtract))
                e.nop().then_inc(bank_free[b], 1)
                e.nop().then_inc(a_["ylo"], 1)

        def up_dve(e, name):
            p, q = PH[name], up_sem[name]

            def group(g, u_):
                banks = 4 * u_
                if name == "up1":
                    for n in range(4):
                        col = g * 2 + n % 2
                        e.wait_ge(q["first"], g * 4 + n + 1)
                        for shift, tap, s_ in ((1, 1, q["conv1"]), (2, 0, taken["d"])):
                            if shift == 2:
                                e.wait_ge(q["conv1"], g * 4 + n + 1)
                            o = acc[:, n, shift:S]
                            e.scalar_tensor_tensor(out=o, in0=ps[banks + n][:, 0:S - shift],
                                                   scalar=vec[:, conv_col(tap, col, n // 2)], in1=o,
                                                   op0=ALU.mult, op1=ALU.add).then_inc(s_, 1)
                    for n in range(2):
                        e.wait_ge(taken["d"], taken_before(name, g, "d") + n + 3)
                        e.wait_ge(q["silu"], g * 2 + n + 1)
                        e.tensor_tensor(acc[:, n, :], acc[:, n, :], acc[:, n + 2, :], ALU.mult).then_inc(q["prod"], 1)
                else:
                    for n in range(2):
                        tile_ready(e, name, g, n + 2)
                        e.wait_ge(taken["a"], taken_before(name, g, "a") + n + 1)
                        e.tensor_tensor(acc[:, n, :], ps[banks + 2 + n][:, :], acc[:, n, :], ALU.mult).then_inc(taken["d"], 1)
                        e.wait_ge(taken["d"], taken_before(name, g, "d") + n + 1)
                        e.nop().then_inc(q["prod"], 1)
                for n in range(2):
                    e.wait_ge(q["hi"], g * 2 + n + 1)
                    tile = bass.ds(g * 2 + n, 1)
                    dst = g_lo[:, tile, :].rearrange("p a t -> p (a t)")
                    src = g_hi[:, tile, :].rearrange("p a t -> p (a t)").bitcast(F32)
                    e.tensor_tensor(dst, acc[:, n, :], src, ALU.subtract).then_inc(q["lo"], 1)

            up_groups(e, p, group)

        def hg_dve(e, x, link):
            blocks = lambda t, w: t[:, :, :].rearrange("p h (n w) -> p (h n) w", w=w)
            if x[0] == "hg_decay":
                e.wait_ge(hgs["lb_exp"], 1)
                link(e.tensor_tensor(lb[:, 3, :], lb[:, 1, :], lb[:, 2, :], ALU.add))
                link(e.reciprocal(lb[:, 3, :], lb[:, 3, :]))
                link(e.tensor_tensor(lb[:, 4, :], lb[:, 1, :], lb[:, 3, :], ALU.mult))
                link(e.tensor_scalar(lb[:, 5, :], lb[:, 4, :], -1.0, 1.0, ALU.mult, ALU.add))
                tile_taken(e, "hf", 0, 3)
                for h in range(HH):
                    ins = e.tensor_scalar(hE[:, h, :], hk[:, h, :], lb[:, 5, h:h + 1], lb[:, 4, h:h + 1], ALU.mult, ALU.add)
                link(ins)
                link(e.tensor_scalar(hk[:, :, :], hE[:, :, :], -1.0, 1.0, ALU.mult, ALU.add))
                e.nop().then_inc(hgs["fg"], 1)
                e.wait_ge(hgs["log"], 1)
                for h in range(HH):
                    ins = e.tensor_tensor_scan(hb[:, h, :], chunk_start[:, :], hE[:, h, :], 0.0, ALU.mult, ALU.add)
                link(ins)
                link(e.memset(hS[:, :, :], 0.0))
            elif x[0] == "hg_level":
                lev = x[1]
                if lev < 6:
                    m = LEVELS[lev]
                    b_, e_, q_, Q_ = (blocks(t, 2 * m) for t in (hb, hE, hq, hQ))
                    mid = b_[:, :, m - 1:m].to_broadcast([P, HH * S // (2 * m), m])
                    if lev:
                        e.wait_ge(hgs["K"], lev)
                        e.wait_ge(hgs["Q"], lev)
                    e.tensor_tensor(e_[:, :, 0:m], mid, b_[:, :, 0:m], ALU.subtract)
                    link(e.tensor_tensor(e_[:, :, m:], b_[:, :, m:], mid, ALU.subtract))
                    e.nop().then_inc(hgs["diff"], 1)
                    e.wait_ge(hgs["exp"], lev + 1)
                    if lev:
                        e.wait_ge(hgs["lev_done"], HH * lev)
                    else:
                        e.wait_ge(hgs["zero"], 1)
                        tile_taken(e, "hq", 0, 3)
                    e.tensor_tensor(Q_[:, :, m:], q_[:, :, m:], e_[:, :, m:], ALU.mult).then_inc(hgs["Q"], 1)
                for h in range(HH):
                    b, use = USE[("lev", lev, h)]
                    e.wait_ge(hgs["lev_done"], HH * lev + h + 1)
                    o = hS[:, h, :].rearrange("p (n w) -> p n w", w=P)
                    mask = level_mask[:, lev:lev + 1, :].bitcast(U32).to_broadcast([P, TB, P])
                    e.wait_ge(const_ready, 2)
                    e.copy_predicated(o, mask, ps[b][:, :].rearrange("p (n w) -> p n w", w=P)).then_inc(bank_free[b], 1)
            elif x[0] == "hg_scale":
                e.wait_ge(hgs["eb"], 1)
                e.wait_ge(hgs["lev_done"], HH * 7)
                last = lambda t: blocks(t, CH)[:, :, CH - 1:CH]
                e.tensor_tensor(hQ[:, :, :], hq[:, :, :], hE[:, :, :], ALU.mult)
                link(e.tensor_copy(decay[:, :, :].rearrange("p h c -> p (h c)")[:, :, None], last(hE)))
                link(e.tensor_tensor(blocks(hK, CH), last(hb).to_broadcast([P, HH * S // CH, CH]), blocks(hb, CH), ALU.subtract))
                e.nop().then_inc(hgs["kd"], 1)
                e.wait_ge(hgs["el"], 1)
                link(e.tensor_tensor(hK[:, :, :], hK[:, :, :], hk[:, :, :], ALU.mult))
                e.nop().then_inc(hgs["scale"], 1)
            elif x[0] == "hg_state":
                c = x[1]
                b, use = USE[("st", c)]
                e.wait_ge(hgs["u_done"], c + 1)
                if c == 0:
                    link(e.tensor_copy(state[:, 1, :], ps[b][:, :]))
                else:
                    for h in range(HH):
                        v = slice(h * P, (h + 1) * P)
                        ins = e.scalar_tensor_tensor(out=state[:, c + 1, v], in0=state[:, c, v], scalar=decay[:, h, c:c + 1],
                                                     in1=ps[b][:, v], op0=ALU.mult, op1=ALU.add)
                    link(ins)
                e.nop().then_inc(bank_free[b], 1)
                e.nop().then_inc(hgs["state"], 1)
            elif x[0] == "hg_out":
                if x[1] < TB:
                    pr = x[1]
                    b, use = USE[("ho", pr)]
                    e.wait_ge(hgs["o_sq"], pr + 1)
                    e.tensor_reduce(hstat[:, pr, 0, :], work[0][:, :].rearrange("p (h v) -> p h v", h=HH), axis=AX.X, op=ALU.add).then_inc(hgs["o_ms"], 1)
                    e.wait_ge(hgs["o_rs"], pr + 1)
                    if pr:
                        e.wait_ge(hgs["ot_done"], pr)
                    link(e.tensor_tensor(work[1][:, :].rearrange("p (h v) -> p h v", h=HH), ps[b][:, :].rearrange("p (h v) -> p h v", h=HH),
                                         hstat[:, pr, 2, :][:, :, None].to_broadcast([P, HH, P]), ALU.mult))
                    e.nop().then_inc(bank_free[b], 1)
                    e.nop().then_inc(hgs["o_tok"], 1)
                if x[1] > 0:
                    pr = x[1] - 1
                    b, use = USE[("hot", pr)]
                    e.wait_ge(hgs["ot_done"], pr + 1)
                    tile_taken(e, "hg", 0, 3)
                    c = slice(pr * P, (pr + 1) * P)
                    w3 = work[2 + pr % 2][:, :].rearrange("p (h t) -> p h t", h=HH)
                    link(e.scalar_tensor_tensor(out=w3, in0=ps[b][:, :].rearrange("p (h t) -> p h t", h=HH), scalar=vec[:, 44:45],
                                                in1=hgate[:, :, c], op0=ALU.mult, op1=ALU.mult))
                    e.nop().then_inc(bank_free[b], 1)
                    e.nop().then_inc(hgs["y"], 1)
                    e.wait_ge(hgs["yhi"], pr + 1)
                    e.tensor_tensor(yH[1][:, :, c], w3, yH[0][:, :, c].bitcast(F32), ALU.subtract).then_inc(hgs["ylo"], 1)

        @block.vector
        def _(e):
            seq = [0]

            def link(ins):
                seq[0] += 1
                ins.then_inc(dve_seq, 1)
                e.wait_ge(dve_seq, seq[0])

            for x in SCHEDULE:
                what = x[0]
                if what == "start":
                    e.memset(mean_d[:, :], 1.0 / D)
                    link(e.memset(mean_h[:, :], 0.0))
                    e.memset(mean_h[0:64, 0:64], 1.0 / HD)
                    e.memset(mean_h[64:128, 64:128], 1.0 / HD)
                    e.memset(ones[:, :], 1.0)
                    link(e.memset(chunk_start[:, :], 1.0))
                    link(e.memset(chunk_start[:, :].rearrange("p (n w) -> p n w", w=CH)[:, :, 0:1], 0.0))
                    e.nop().then_inc(const_dve, 1)
                    e.wait_ge(vec_done, 1)
                    e.tensor_copy(vec[:, :], ps[7][:, 0:229]).then_inc(vec_ready, 1)
                    for j in range(DC):
                        e.wait_ge(xt_done, j + 1)
                        e.tensor_copy(xT[:, j, :], ps[j][:, :]).then_inc(x_ready, 1)
                    e.wait_ge(x_ready, DC)
                    for b in range(4, 8):
                        e.nop().then_inc(bank_free[b], 1)
                    e.wait_ge(vec_ready, 1)
                    e.tensor_scalar(qk_gain[:, 0:1], vec[:, 40:41], HD ** -0.5, None, ALU.mult)
                    e.tensor_scalar(qk_gain[:, 1:2], vec[:, 42:43], HD ** -0.5, None, ALU.mult)
                    e.wait_ge(rb_full, 16)
                    e.tensor_copy(rb_ext[:, 0:383], rb[:, 256:257].to_broadcast([NH, 383]))
                    link(e.tensor_copy(rb_ext[:, 383:639], rb[:, 256:0:-1]))
                    link(e.memset(rb_ext[:, 639:640], 0.0))
                    e.nop().then_inc(rb_ready, 1)
                    link(e.tensor_tensor(lb[:, 0, :], vec[:, 45:49], vec[:, 49:53], ALU.max))
                    e.tensor_tensor(lb[:, 1, :], vec[:, 45:49], lb[:, 0, :], ALU.subtract)
                    e.tensor_tensor(lb[:, 2, :], vec[:, 49:53], lb[:, 0, :], ALU.subtract).then_inc(hgs["lb"], 1)
                elif what == "norm":
                    e.wait_ge(rstd_ready, x[1] + 1)
                    gain = 8 * x[1]

                    def scaled(j):
                        if j >= 2:
                            e.wait_ge(hlo_ready, x[1] * DC + j - 1)
                        e.scalar_tensor_tensor(out=work[j % 2][:, :], in0=xT[:, j, :], scalar=vec[:, gain + j:gain + j + 1],
                                               in1=work[2][:, :], op0=ALU.mult, op1=ALU.mult).then_inc(hf_ready, 1)
                    scaled(0)
                    for j in range(DC):
                        if j + 1 < DC:
                            scaled(j + 1)
                        e.wait_ge(hhi_ready, x[1] * DC + j + 1)
                        e.tensor_tensor(h_lo[:, j, :], work[j % 2][:, :], h_hi[:, j, :].bitcast(F32), ALU.subtract).then_inc(hlo_ready, 1)
                    e.nop().then_inc(bank_free[4], 1)
                elif what == "take":
                    take_dve(e, x[1], x[2], link)
                elif what == "qknorm":
                    _, name, n = x
                    count = {"qA": 0, "kA": 4, "fq": 8, "fk": 12}[name] + n
                    e.wait_ge(qkrs_ready, count + 1)
                    t = qk1[name][:, n, :]
                    g = {"qA": qk_gain[:, 0:1], "kA": vec[:, 41:42], "fq": qk_gain[:, 1:2], "fk": vec[:, 43:44]}[name]
                    e.scalar_tensor_tensor(out=t, in0=t, scalar=g, in1=work[7][:, :], op0=ALU.mult, op1=ALU.mult).then_inc(qk_ready[name], 1)
                elif what == "att":
                    att_dve(e, x[1], x[2], link)
                elif what == "up":
                    up_dve(e, x[1])
                elif what == "foxf":
                    e.wait_ge(ff["w_hi"], 1)
                    e.tensor_tensor(wf_lo[:, :, :], wf_raw[:, :, :], wf_hi[:, :, :].bitcast(F32), ALU.subtract).then_inc(ff["w_lo"], 1)
                    e.wait_ge(ff["mm"], 1)
                    b, use = USE[("foxf", 0)]
                    link(e.tensor_tensor(fx[:, 0, :, :], ps[b][:, 0:32].rearrange("p (t h) -> p t h", h=NH),
                                         fbias[:, None, :].to_broadcast([P, TB, NH]), ALU.add))
                    e.nop().then_inc(bank_free[b], 1)
                    e.scalar_tensor_tensor(out=fx[:, 1, :, :], in0=fx[:, 0, :, :], scalar=-1.0, in1=fx[:, 0, :, :],
                                           op0=ALU.mult, op1=ALU.min).then_inc(ff["x"], 1)
                    e.wait_ge(ff["l"], 1)
                    e.scalar_tensor_tensor(out=fx[:, 2, :, :], in0=fx[:, 0, :, :], scalar=0.0, in1=fx[:, 1, :, :],
                                           op0=ALU.min, op1=ALU.subtract).then_inc(ff["logf"], 1)
                    e.wait_ge(ff["cmm"], 1)
                    b, use = USE[("foxf", 1)]
                    e.tensor_copy(ctok[:, :, :], ps[b][:, 0:32].rearrange("p (t h) -> p t h", h=NH)).then_inc(bank_free[b], 1)
                    e.wait_ge(ff["ct"], 1)
                    b, use = USE[("foxf", 2)]
                    link(e.tensor_scalar(cT[0:NH, :], ps[b][0:NH, :], -1.0, None, ALU.mult))
                    e.nop().then_inc(bank_free[b], 1)
                    e.nop().then_inc(ff["ctsb"], 1)
                elif what == "foxc":
                    h = x[1]
                    e.wait_ge(ff["row_mm"], h + 1)
                    b, use = USE[x]
                    e.tensor_copy(c_rows[:, h, :], ps[b][:, :]).then_inc(bank_free[b], 1)
                elif what == "bias":
                    b, use = USE[x]
                    e.wait_ge(bias_mm, x[1] + 1)
                    link(e.tensor_copy(bias_mask[:, x[1], :], ps[b][:, :]))
                    e.nop().then_inc(bank_free[b], 1)
                    e.nop().then_inc(bias_ready, 1)
                elif what in ("hg_decay", "hg_level", "hg_scale", "hg_state", "hg_out"):
                    hg_dve(e, x, link)
                elif what == "pT":
                    for c in range(2):
                        b, use = USE[("pT", c)]
                        e.wait_ge(p_hi, c + 1)
                        link(e.tensor_tensor(pT_lo[:, c, :], ps[b][:, :], pT_hi[:, c, :].bitcast(F32), ALU.subtract))
                        e.nop().then_inc(bank_free[b], 1)
                    e.nop().then_inc(p_lo, 1)
                elif what == "finish":
                    for j in range(8):
                        half, tb = j // 4, j % 4
                        e.wait_ge(fin_done, j + 1)
                        b, use = USE[("fin", j)]
                        link(e.tensor_copy(otok[:, tb, half * 512:(half + 1) * 512], ps[b][:, :]))
                        e.nop().then_inc(bank_free[b], 1)
                        e.nop().then_inc(fin_copied, 1)

        def att_pe(e, kind, i):
            a_ = A[kind]
            qn, kn, vn, _ = kinds(kind)
            if i < STEPS:
                qb, h = divmod(i, NH)
                if i == 0:
                    if kind == "B":
                        for nm in (qn, kn, vn):
                            tile_taken(e, nm, 0, 2)
                            tile_taken(e, nm, 0, 3)
                    else:
                        e.wait_ge(qk_ready[qn], 4)
                        e.wait_ge(qk_ready[kn], 4)
                r = slice(64 * (h % 2), 64 * (h % 2) + 64)
                n = (qb + 1) * P
                bank = bank_wait(e, ("sc", kind, i))
                e.matmul(bank[:, 0:n], qk1[qn][r, h // 2, qb * P:n], qk1[kn][r, h // 2, 0:n], start=True, stop=True).then_inc(a_["sc_done"], 1)
            j = i - 2
            if 0 <= j < STEPS:
                bank = bank_wait(e, ("pt", kind, j))
                e.wait_ge(a_["p_ready"], j + 1)
                for c in range(j // NH + 1):
                    mm = e.transpose(bank[:, c * P:(c + 1) * P], work[j % 4][:, c * P:(c + 1) * P], ident[:, :])
                mm.then_inc(a_["tr_done"], 1)
            j = i - 3
            if 0 <= j < STEPS:
                qb, h = divmod(j, NH)
                if h == 0:
                    bank_wait(e, ("out", kind, qb))
                if j == 0:
                    tile_taken(e, vn, 0, 2)
                    tile_taken(e, vn, 0, 3)
                b, use = USE[("pt", kind, j)]
                e.wait_ge(bank_free[b], use + 1)
                for c in range(qb + 1):
                    mm = e.matmul(ps[7][:, h * HD:(h + 1) * HD], work[4 + j % 2][:, c * P:(c + 1) * P],
                                  vtok[vn][:, c, h * HD:(h + 1) * HD], start=c == 0, stop=c == qb)
                mm.then_inc(a_["pv_done"], 1)
            j = i - 4
            if j > 0 and j % NH == 0:
                q = j // NH - 1
                bank = bank_wait(e, ("ot", kind, q))
                e.wait_ge(a_["ot_ready"], q + 1)
                for c in range(4):
                    mm = e.transpose(bank[:, c * P:(c + 1) * P], work[6][:, c * P:(c + 1) * P], ident[:, :])
                mm.then_inc(a_["ot_done"], 1)

        @block.tensor
        def _(e):
            def operand(name, k):
                if name.startswith("branch"):
                    y = {"B": yB, "A": yA, "H": yH, "F": yF}[name[-1]]
                    return y[0][:, k, :], y[1][:, k, :]
                if name.startswith("down"):
                    return g_hi[:, k, :], g_lo[:, k, :]
                if name == "pproj":
                    return pT_hi[:, k, :], pT_lo[:, k, :]
                return h_hi[:, k, :], h_lo[:, k, :]

            norm_of = {"qB": 0, "kB": 0, "vB": 0, "qA": 0, "kA": 0, "vA": 0, "gateB": 0, "gateA": 0,
                       "up1": 1, "hq": 2, "hf": 2, "hi": 2, "hg": 2, "fq": 2, "fk": 2, "fv": 2,
                       "gateH": 2, "gateF": 2, "up2": 3, "pgate": 4}

            def activations_ready(name, g, k):
                first = isinstance(g, int) and g == 0
                if not first:
                    return
                if name in norm_of and name in ("qB", "up1", "hq", "up2", "pgate"):
                    e.wait_ge(hlo_ready, norm_of[name] * DC + k + 1)
                elif name in ("out1", "out2"):
                    e.wait_ge(mixlo_ready, (DC if name == "out2" else 0) + k + 1)
                elif name.startswith("down") and k % 2 == 0:
                    e.wait_ge(up_sem["up" + name[-1]]["lo"], k + 2)
                elif name.startswith("branch") and k == 0:
                    if name == "branchH":
                        e.wait_ge(hgs["ylo"], TB)
                    else:
                        e.wait_ge(A[name[-1]]["ylo"], TB)
                elif name == "pproj" and k == 0:
                    e.wait_ge(p_lo, 1)

            def slot(name, g, k, banks, bank_check):
                p = PH[name]
                static = p.slot0 + (g * p.kc if isinstance(g, int) else 0) + k
                pos = static % SPLIT_SLOTS
                activations_ready(name, g, k)
                e.wait_ge(lo_full, g * p.kc + (p.slot0 + k + 1))
                x_hi, x_lo = operand(name, k)
                for n in range(4):
                    if k == 0:
                        bank_check(n)
                    c = slice(n * P, (n + 1) * P)
                    if name in ("vB", "vA", "fv", "hi"):
                        ops = [(x_hi[:, c], w_lo[:, pos, :]), (x_lo[:, c], w_hi[:, pos, :]), (x_hi[:, c], w_hi[:, pos, :])]
                    else:
                        ops = [(w_lo[:, pos, c], x_hi), (w_hi[:, pos, c], x_lo), (w_hi[:, pos, c], x_hi)]
                    for i, (l, r) in enumerate(ops):
                        mm = e.matmul(ps[banks + n][:, :], l, r, start=k == 0 and i == 0, stop=k == p.kc - 1 and i == 2)
                    if k == p.kc - 1:
                        mm.then_inc(tile_done, 1)
                if k < p.kc - 1:
                    mm.then_inc(slot_used, 1)

            sq_n = [0]

            def sum_squares(bank, weights, start, stop):
                n = sq_n[0]
                sq_n[0] += 1
                e.wait_ge(sq_ready, n + 1)
                e.matmul(bank[:, :], weights[:, :], sq_src[0], start=start, stop=stop).then_inc(sq_used, 1)

            sq_src = [None]
            for x in SCHEDULE:
                what = x[0]
                if what == "start":
                    e.wait_ge(const_ready, 1)
                    e.wait_ge(vec_full, 16 * 19)
                    for i, (n, c) in enumerate(((53, 0), (88, 53), (88, 141))):
                        mm = e.transpose(ps[7][:, c:c + n], vrows[0:n, i, :], ident[0:n, 0:n])
                    mm.then_inc(vec_done, 1)
                    e.wait_ge(x_full, 64)
                    for j in range(DC):
                        if j == 7:
                            e.wait_ge(vec_ready, 1)
                        for tb in range(TB):
                            mm = e.transpose(ps[j][:, tb * P:(tb + 1) * P], xtok[:, tb, j * P:(j + 1) * P], ident[:, :])
                        mm.then_inc(xt_done, 1)
                    e.wait_ge(const_dve, 1)
                elif what == "sumsq":
                    if x[2] == 0:
                        bank_wait(e, ("norm", x[1]))
                    sq_src[0] = sq_ring[sq_n[0] % 2][:, :]
                    sum_squares(ps[4], mean_d, x[2] == 0, x[2] == DC - 1)
                elif what == "slot":
                    _, name, g, k = x

                    def check(n):
                        prev = previous_group(name, g)
                        if prev is None:
                            e.wait_ge(x_ready, DC)
                        else:
                            tile_taken(e, *prev, n)
                    slot(name, g, k, 0, check)
                elif what == "up":
                    name = x[1]
                    p = PH[name]

                    def group(g, u_):
                        def check(n):
                            if isinstance(g, int) and g == 0:
                                tile_taken(e, *previous_group(name, 0), n)
                            elif isinstance(g, int) and g == 1:
                                b, use = USE[(name, 4 + n)]
                                e.wait_ge(bank_free[b], use)
                            else:
                                tile_taken(e, name, g - 2, n)
                        for k in range(p.kc):
                            slot(name, g, k, 4 * u_, check)

                    up_groups(e, p, group)
                elif what == "qknorm":
                    _, name, n = x
                    bank = bank_wait(e, x)
                    sq_src[0] = work[7][:, :]
                    sum_squares(bank, mean_h, True, True)
                elif what == "att":
                    att_pe(e, x[1], x[2])
                elif what == "bias":
                    e.wait_ge(bias_full, 16)
                    e.wait_ge(const_ready, 1)
                    bank = bank_wait(e, x)
                    e.matmul(bank[:, :], reverse[:, :], bias_up[:, x[1], :], start=True, stop=True).then_inc(bias_mm, 1)
                elif what == "foxf":
                    bank = bank_wait(e, ("foxf", 0))
                    e.wait_ge(ff["w_lo"], 1)
                    for tb in range(TB):
                        c = slice(tb * P, (tb + 1) * P)
                        for k in range(DC):
                            for i, (l, r) in enumerate(((h_hi, wf_lo), (h_lo, wf_hi), (h_hi, wf_hi))):
                                mm = e.matmul(bank[:, tb * NH:(tb + 1) * NH], l[:, k, c], r[:, k, :],
                                              start=k == 0 and i == 0, stop=k == DC - 1 and i == 2)
                    mm.then_inc(ff["mm"], 1)
                    bank = bank_wait(e, ("foxf", 1))
                    e.wait_ge(ff["logf"], 1)
                    e.wait_ge(const_ready, 2)
                    for tb in range(TB):
                        for t in range(tb + 1):
                            mm = e.matmul(bank[:, tb * NH:(tb + 1) * NH], (tri if t == tb else ones)[:, :],
                                          fx[:, 2, t, :], start=t == 0, stop=t == tb)
                    mm.then_inc(ff["cmm"], 1)
                    bank = bank_wait(e, ("foxf", 2))
                    for tb in range(TB):
                        mm = e.transpose(bank[0:NH, tb * P:(tb + 1) * P], ctok[:, tb, :], ident[:, :])
                    mm.then_inc(ff["ct"], 1)
                elif what == "foxc":
                    h = x[1]
                    if h == 0:
                        e.wait_ge(ff["ctsb"], 1)
                    bank = bank_wait(e, x)
                    e.matmul(bank[:, :], ident[0:NH, h:h + 1].to_broadcast([NH, P]), cT[0:NH, :], start=True, stop=True).then_inc(ff["row_mm"], 1)
                elif what == "hg_level":
                    lev = x[1]
                    if lev < 6:
                        e.wait_ge(hgs["Q"], lev + 1)
                        e.wait_ge(hgs["K"], lev + 1)
                    q_, k_ = (hQ, hK) if lev < 6 else (hq, hk)
                    for h in range(HH):
                        bank = bank_wait(e, ("lev", lev, h))
                        for pr in range(TB):
                            c = slice(pr * P, (pr + 1) * P)
                            mm = e.matmul(bank[:, c], k_[:, h, c], q_[:, h, c], start=True, stop=True)
                        mm.then_inc(hgs["lev_done"], 1)
                elif what == "hg_kt":
                    e.wait_ge(hgs["scale"], 1)
                    for h in range(HH):
                        bank = bank_wait(e, ("kt", h))
                        for pr in range(TB):
                            c = slice(pr * P, (pr + 1) * P)
                            mm = e.transpose(bank[:, c], hK[:, h, c], ident[:, :])
                        mm.then_inc(hgs["kt_done"], 1)
                elif what == "hg_state":
                    c = x[1]
                    pr, r = c // 2, slice(64 * (c % 2), 64 * (c % 2) + 64)
                    bank = bank_wait(e, ("st", c))
                    if c == 0:
                        for h in range(HH):
                            b, use = USE[("kt", h)]
                            e.wait_ge(bank_free[b], use + 1)
                        tile_taken(e, "hi", 0, 2)
                        tile_taken(e, "hi", 0, 3)
                    for h in range(HH):
                        mm = e.matmul(bank[:, h * P:(h + 1) * P], hKt[r, h, pr * P:(pr + 1) * P], hv[r, pr, h * P:(h + 1) * P],
                                      start=True, stop=True)
                    mm.then_inc(hgs["u_done"], 1)
                elif what == "hg_out":
                    if x[1] < TB:
                        pr = x[1]
                        bank = bank_wait(e, ("ho", pr))
                        e.wait_ge(hgs["state"], min(2 * pr + 1, 7))
                        for h in range(HH):
                            v = slice(h * P, (h + 1) * P)
                            e.matmul(bank[:, v], hS[:, h, pr * P:(pr + 1) * P], hv[:, pr, v], start=True, stop=False, skip_group_check=True)
                            for half in range(2):
                                c = 2 * pr + half
                                if c:
                                    mm = e.matmul(bank[64 * half:64 * half + 64, v], hQ[:, h, c * CH:(c + 1) * CH], state[:, c, v],
                                                  start=False, stop=True, skip_group_check=True)
                        mm.then_inc(hgs["o_done"], 1)
                    if x[1] > 0:
                        pr = x[1] - 1
                        bank = bank_wait(e, ("hot", pr))
                        e.wait_ge(hgs["o_tok"], pr + 1)
                        for h in range(HH):
                            mm = e.transpose(bank[:, h * P:(h + 1) * P], work[1][:, h * P:(h + 1) * P], ident[:, :])
                        mm.then_inc(hgs["ot_done"], 1)
                elif what == "pT":
                    e.wait_ge(p_full, 16)
                    for c in range(2):
                        bank = bank_wait(e, ("pT", c))
                        for tb in range(TB):
                            mm = e.transpose(bank[:, tb * P:(tb + 1) * P], ptok[:, tb, c * P:(c + 1) * P], ident[:, :])
                        mm.then_inc(p_done, 1)
                elif what == "finish":
                    for j in range(8):
                        half, tb = j // 4, j % 4
                        e.wait_ge(x_ready, 5 * DC + 4 * half + 4)
                        bank = bank_wait(e, ("fin", j))
                        for c in range(4):
                            mm = e.transpose(bank[:, c * P:(c + 1) * P], xT[:, 4 * half + c, tb * P:(tb + 1) * P], ident[:, :])
                        mm.then_inc(fin_done, 1)



_INS = ['x', 'norm1_g', 'w_in', 'q_norm_g', 'k_norm_g', 'rel_bias', 'w_branch_a', 'w_branch_b', 'w_out',
        'norm2_g', 'w_ffn_up', 'ffn_conv_w', 'ffn_conv_b', 'w_ffn_down', 'p_2', 'norm_mix_g_2', 'w_in_2',
        'hg_lb_logits_2', 'hg_onorm_g_2', 'fox_f_bias_2', 'fox_q_norm_g_2', 'fox_k_norm_g_2',
        'w_branch_a_2', 'w_branch_b_2', 'w_out_2', 'norm_ffn_g_2', 'w_ffn_gate_2', 'w_ffn_up_2',
        'w_ffn_down_2', 'norm_ple_g_2', 'w_ple_gate_2', 'w_ple_proj_2']


def kernel(**inputs):
    import numpy as np
    import concourse.bacc as bacc
    from concourse.bass_utils import run_bass_kernel_spmd

    nc = bacc.Bacc("TRN2", target_bir_lowering=False, num_devices=1, dynamic_dma_scratch_size=1024)
    arrays, aps = {}, {}
    for name in _INS:
        v = np.ascontiguousarray(inputs[name])
        arrays[f"in_{name}"] = v
        aps[name] = nc.dram_tensor(f"in_{name}", v.shape, mybir.dt.from_np(v.dtype), kind="ExternalInput").ap()
    out = nc.dram_tensor("out_x", (1, S, D), F32, kind="ExternalOutput").ap()
    two_block_kernel(nc, aps, out)
    r = run_bass_kernel_spmd(nc, [arrays], core_ids=[0])
    return r.results[0]["out_x"]
```

```python
import concourse.bass as bass
from concourse import mybir
from contextlib import ExitStack

F32 = mybir.dt.float32
F32R = mybir.dt.float32r
U32 = mybir.dt.uint32
ALU = mybir.AluOpType
ACT = mybir.ActivationFunctionType
AX = mybir.AxisListType

P = 128
S = 512
TB = S // P
D = 1024
DC = D // P
FF = 2816
FC = FF // P
NH = 8
HD = 64
HH = 4
CH = 64
NREL = 257
EPS = 1e-6
NEG = -1e30
SPLIT_SLOTS = 8
RAW_SLOTS = 4
LEVELS = (32, 16, 8, 4, 2, 1)
STEPS = TB * NH
LAG = 3


class Phase:

    def __init__(self, name, kc, groups):
        self.name, self.kc, self.groups = name, kc, groups


PHASES = [Phase(*a) for a in (
    ("qB", 8, 1), ("kB", 8, 1), ("vB", 8, 1), ("qA", 8, 1), ("kA", 8, 1), ("vA", 8, 1),
    ("gateB", 8, 2), ("branchB", 4, 2), ("gateA", 8, 2), ("branchA", 4, 2), ("out1", 8, 2),
    ("up1", 8, 11), ("down1", 22, 2),
    ("hf", 8, 1), ("hq", 8, 1), ("hi", 8, 1), ("hg", 8, 1), ("fq", 8, 1), ("fk", 8, 1), ("fv", 8, 1),
    ("gateH", 8, 2), ("branchH", 4, 2), ("gateF", 8, 2), ("branchF", 4, 2), ("out2", 8, 2),
    ("up2", 8, 11), ("down2", 22, 2), ("pgate", 8, 2), ("pproj", 2, 2))]
PH = {}
_slot = _group = 0
for _p in PHASES:
    _p.slot0, _p.group0 = _slot, _group
    _slot += _p.kc * _p.groups
    _group += _p.groups
    PH[_p.name] = _p
SLOTS = _slot
OWNER = {name: "adad" for name in ("qB", "kB", "vB", "qA", "kA", "vA", "hi", "fq", "fk", "fv")}
OWNER |= {name: "aaaa" for name in ("gateB", "gateA", "gateH", "gateF", "pgate", "hq", "hf", "hg")}
OWNER |= {name: "dddd" for name in ("branchB", "branchA", "branchH", "branchF", "out1", "out2",
                                    "down1", "down2", "pproj", "up1")}
OWNER["up2"] = "aadd"


def taken_before(name, g, who):
    total = 0
    for p in PHASES:
        per = OWNER[p.name].count(who)
        if p.name == name:
            return g * per + total if per else total
        total += per * p.groups
    raise KeyError(name)


def previous_group(name, g):
    if g:
        return name, g - 1
    i = PHASES.index(PH[name])
    return (PHASES[i - 1].name, PHASES[i - 1].groups - 1) if i else None



def make_schedule():
    s = []

    def run(names, plan=()):
        behind = {}
        for at, step in plan:
            behind.setdefault(at, []).append(step)
        n = 0
        for name in names:
            name, _, only = name.partition(":")
            p = PH[name]
            for g in range(p.groups) if not only else [int(only)]:
                for k in range(p.kc):
                    s.append(("slot", name, g, k))
                    if k == p.kc - 1:
                        s.append(("take", name, g))
                    s.extend(behind.pop(n, ()))
                    n += 1
        assert not behind, behind

    def spread(steps, first, last):
        n = len(steps)
        return [(first + i * (last - first + 1) // n, x) for i, x in enumerate(steps)]

    def attention(kind, first, last):
        return spread([("att", kind, i) for i in range(STEPS + LAG + 3)], first, last)

    def head_norms(q, k, first):
        plan = []
        for i, (name, n) in enumerate([(x, n) for x in (q, k) for n in range(4)]):
            plan += [(first + i, ("square", name, n)), (first + i + 1, ("scale", name, n))]
        return sorted(plan, key=lambda x: (x[0], x[1][0] == "scale"))

    def residual(name, norm):
        run([name + ":0"])
        run([name + ":1"], [(PH[name].kc - 4 + j, ("sumsq", norm, j)) for j in range(4)])
        s.extend(("sumsq", norm, j) for j in range(4, 8))
        s.append(("norm", norm))

    s.append(("start",))
    s.extend(("sumsq", 0, j) for j in range(DC))
    s.append(("norm", 0))
    run(["qB", "kB", "vB"], [(8 + h, ("bias", h)) for h in range(NH)])
    run(["qA", "kA", "vA", "gateB", "branchB", "gateA"],
        attention("B", 0, 23) + head_norms("qA", "kA", 24) + attention("A", 34, 62))
    run(["branchA"])
    residual("out1", 1)
    s.append(("up", "up1"))
    residual("down1", 2)
    levels = []
    for x in range(7):
        levels.append((2 + 3 * x, ("hg_mm", x)))
        if x < 5:
            levels.append((2 + 3 * x, ("hg_prep", x + 1)))
        levels.append((2 + 3 * x, ("hg_merge", x)))
        if x < 5:
            levels.append((2 + 3 * x, ("hg_qk", x + 1)))
    run(["hf", "hq"], [(7, ("hg_decay",)), (15, ("hg_prep", 0)), (15, ("hg_qk", 0))])
    run(["hi", "hg", "fq", "fk", "fv", "gateH", "branchH", "gateF"],
        levels + [(1, ("foxf", 0)), (3, ("foxf", 1)), (4, ("foxf", 2))]
        + [(21, ("hg_scale",)), (24, ("hg_kt",))] + [(26 + c, ("hg_state", c)) for c in range(7)]
        + [(33 + 2 * p, ("hg_out", p)) for p in range(TB + 1)]
        + head_norms("fq", "fk", 34) + [(42 + h // 2, ("foxc", h)) for h in range(NH)]
        + attention("F", 46, 79))
    run(["branchF"])
    residual("out2", 3)
    s.append(("up", "up2"))
    residual("down2", 4)
    run(["pgate"], [(8, ("pT",))])
    run(["pproj"])
    s.append(("finish",))
    return s


SCHEDULE = make_schedule()


def bank_uses():
    use, count = {}, [0] * 8

    def take(key, bank):
        use[key] = (bank, count[bank])
        count[bank] += 1

    for x in SCHEDULE:
        if x[0] == "start":
            for j in range(4, 8):
                take(("x", j), j)
        elif x[0] == "sumsq" and x[2] == 0:
            take(("norm", x[1]), 4)
        elif x[0] == "scale":
            take(x, 4 + x[2] % 2)
        elif x[0] == "bias":
            take(x, 4 + x[1] % 2)
        elif x[0] == "foxf":
            take(x, 5)
        elif x[0] == "foxc":
            take(x, 4 + x[1] % 2)
        elif x[0] == "att":
            kind, i = x[1:]
            if i < STEPS:
                take(("sc", kind, i), 4 + i % 2)
            if 0 <= i - LAG < STEPS:
                take(("pt", kind, i - LAG), 6)
            j = i - LAG - 1
            if 0 <= j < STEPS and j % NH == 0:
                take(("out", kind, j // NH), 7)
            j = i - LAG - 2
            if j > 0 and j % NH == 0:
                take(("ot", kind, j // NH - 1), 6)
        elif x[0] == "hg_mm":
            for h in range(HH):
                take(("lev", x[1], h), 4 + h)
        elif x[0] == "hg_kt":
            for h in range(HH):
                take(("kt", h), 4 + h)
        elif x[0] == "hg_state":
            take(("st", x[1]), 4 + x[1] % 2)
        elif x[0] == "hg_out":
            if x[1] < TB:
                take(("ho", x[1]), 4 + x[1] % 2)
            if x[1] > 0:
                take(("hot", x[1] - 1), 6)
        elif x[0] == "up":
            for j in range(4, 8):
                use[(x[1], j)] = (j, count[j])
        elif x[0] == "pT":
            take(("pT", 0), 4)
            take(("pT", 1), 5)
        elif x[0] == "finish":
            for j in range(8):
                take(("fin", j), 4 + j % 4)
    return use


USE = bank_uses()


def two_block_kernel(nc, a, out):
    ctx = ExitStack()
    with ctx:
        KB = 1024
        base = nc.sbuf_base + 64
        base += -base % 64
        at = [base]

        def place(name, shape, dt=F32, offset=None):
            n = 4
            for d in shape[1:]:
                n *= d
            if offset is None:
                offset = at[0]
                at[0] += n + (-n % 64)
            return nc.alloc_sbuf_tensor_at(name, shape, dt, offset=offset)

        xT = place("xT", [P, DC, S])
        h_hi = place("h_hi", [P, DC, S], F32R)
        h_lo = place("h_lo", [P, DC, S], F32R)
        w_raw = place("w_raw", [P, RAW_SLOTS, S])
        w_hi = place("w_hi", [P, SPLIT_SLOTS, S], F32R)
        w_lo = place("w_lo", [P, SPLIT_SLOTS, S], F32R)
        ident = place("ident", [P, P])
        mean_d = place("mean_d", [P, P])
        mean_h = place("mean_h", [P, P])
        ones = place("ones", [P, P])
        reverse = place("reverse", [P, P])
        tri = place("tri", [P, P])
        strict = place("strict", [P, P])
        causal = place("causal", [P, P])
        level_mask = place("level_mask", [P, 7, P])
        chunk_start = place("chunk_start", [P, S])
        vec = place("vec", [P, 53 + 176])
        qk_gain = place("qk_gain", [P, 2])
        lb = place("lb", [P, 6, HH])
        mneg = place("mneg", [P, 2, STEPS])
        rsum = place("rsum", [P, 2, STEPS])
        rinv = place("rinv", [P, 2, STEPS])
        fbias = place("fbias", [P, NH])
        fx = place("fx", [P, 3, TB, NH])
        ctok = place("ctok", [P, TB, NH])
        decay = place("decay", [P, HH, NH])
        hstat = place("hstat", [P, TB, 3, HH])
        wf_raw = place("wf_raw", [P, DC, NH])
        wf_hi = place("wf_hi", [P, DC, NH], F32R)
        wf_lo = place("wf_lo", [P, DC, NH], F32R)
        cT = place("cT", [NH, S])
        U = at[0]
        assert U + 112 * KB <= nc.sbuf_usable_end, (U, nc.sbuf_usable_end)

        def u(name, kb, shape, dt=F32):
            return place(name, shape, dt, offset=U + kb * KB)

        work = [u(f"work{i}", 96 + 2 * i, [P, S]) for i in range(8)]
        sq_ring = [work[6], work[7]]
        xtok = u("xtok", 0, [P, TB, D])
        vrows = u("vrows", 16, [P, 3, P])
        rb = u("rb", 88, [NH, NREL])
        rb_ext = u("rb_ext", 90, [NH, 640])
        qk1 = {"qB": u("qB", 0, [P, 4, S]), "kB": u("kB", 8, [P, 4, S]), "qA": u("qA", 24, [P, 4, S]),
               "kA": u("kA", 32, [P, 4, S]), "fq": u("fq", 72, [P, 4, S]), "fk": u("fk", 80, [P, 4, S])}
        vtok = {"vB": u("vB", 16, [P, 4, S]), "vA": u("vA", 40, [P, 4, S]),
                "fv": u("fv", 88, [P, 4, S]), "hi": u("hv", 24, [P, 4, S])}
        bias_mask = u("bias_mask", 48, [P, NH, S])
        bias_up = u("bias_up", 64, [P, NH, S])
        yB = (u("yB_hi", 64, [P, 4, S], F32R), u("yB_lo", 72, [P, 4, S], F32R))
        yA = (u("yA_hi", 80, [P, 4, S], F32R), u("yA_lo", 88, [P, 4, S], F32R))
        keep = [u(f"keep{i}", 80 + 2 * i, [P, S]) for i in range(2)]
        after = [u(f"after{i}", 84 + 2 * i, [P, S]) for i in range(2)]
        sig_halves = {"gateB": (0, 8), "gateA": (16, 24), "gateH": (56, 64), "gateF": (40, 72), "pgate": (16, 24)}
        sig = {name: [u(f"{name}{i}", kb, [P, 4, S]) for i, kb in enumerate(v)] for name, v in sig_halves.items()}
        g_hi = u("g_hi", 0, [P, FC, S], F32R)
        g_lo = u("g_lo", 44, [P, FC, S], F32R)
        acc = u("acc", 88, [P, 4, S])
        hq = u("hq", 0, [P, HH, S])
        hk = u("hk", 8, [P, HH, S])
        hb = u("hb", 16, [P, HH, S])
        hv = vtok["hi"]
        hgate = u("hgate", 32, [P, HH, S])
        hS = u("hS", 40, [P, HH, S])
        hE = u("hE", 48, [P, HH, S])
        hQ = u("hQ", 56, [P, HH, S])
        hK = u("hK", 64, [P, HH, S])
        state = u("state", 0, [P, NH, S])
        hKt = u("hKt", 16, [P, HH, S])
        yH = (u("yH_hi", 48, [P, 4, S], F32R), u("yH_lo", 16, [P, 4, S], F32R))
        yF = (u("yF_hi", 0, [P, 4, S], F32R), u("yF_lo", 8, [P, 4, S], F32R))
        c_rows = u("c_rows", 24, [P, NH, S])
        ptok = u("ptok", 0, [P, TB, 256])
        pT_hi = u("pT_hi", 4, [P, 2, S], F32R)
        pT_lo = u("pT_lo", 8, [P, 2, S], F32R)
        otok = u("otok", 32, [P, TB, D])

        ps = [ctx.enter_context(nc.psum_tensor(f"bank{i}", [P, S], F32)) for i in range(8)]
        bias_dram = nc.dram_tensor("bias_ext", (NH, 640), F32, kind="Internal").ap()

        def sem(name):
            return ctx.enter_context(nc.semaphore(name))

        raw_full = [sem(f"raw_full{i}") for i in range(RAW_SLOTS)]
        hi_full, lo_full = sem("hi_full"), sem("lo_full")
        slot_used = sem("slot_used")
        tile_done = sem("tile_done")
        taken = {"a": sem("taken_act"), "d": sem("taken_dve")}
        act_seq, dve_seq, pool_seq = sem("act_seq"), sem("dve_seq"), sem("pool_seq")
        bank_free = {b: sem(f"bank_free{b}") for b in range(4, 8)}
        const_ready = sem("const_ready")
        const_dve = sem("const_dve")
        x_full, vec_full, rb_full, bias_full, small_full = (sem(n) for n in (
            "x_full", "vec_full", "rb_full", "bias_full", "small_full"))
        vec_done, vec_ready, rb_ready, scratch_full = (sem(n) for n in (
            "vec_done", "vec_ready", "rb_ready", "scratch_full"))
        xt_done = sem("xt_done")
        x_ready = sem("x_ready")
        sq_ready, sq_used = sem("sq_ready"), sem("sq_used")
        rstd_ready = sem("rstd_ready")
        hf_ready, hhi_ready, hlo_ready = sem("hf_ready"), sem("hhi_ready"), sem("hlo_ready")
        qkrs_ready = sem("qkrs_ready")
        qk_ready = {n: sem(f"{n}_ready") for n in ("qA", "kA", "fq", "fk")}
        A = {}
        for kind in "BAF":
            A[kind] = {n: sem(f"{n}{kind}") for n in (
                "sc_done", "s_ready", "p_ready", "tr_done", "pv_done", "ot_ready", "ot_done",
                "yhi", "ylo", "keep_ready", "beta_ready", "after_ready")}
        mix_ready, mixhi_ready, mixlo_ready = sem("mix_ready"), sem("mixhi_ready"), sem("mixlo_ready")
        up_sem = {n: {k: sem(f"{n}_{k}") for k in (
            "first", "conv1", "conv2", "silu", "prod", "hi", "lo")} for n in ("up1", "up2")}
        hgs = {n: sem(f"hg_{n}") for n in (
            "lb", "lb_exp", "fg", "k", "log", "b", "diff", "exp", "Q", "K", "lev_done", "merged", "zero",
            "eb", "el", "kt_done", "kt", "u_done", "state", "o_done", "o_sq", "o_ms", "o_rs",
            "o_tok", "ot_done", "y", "yhi", "ylo", "scale", "kd")}
        ff = {n: sem(f"fox_{n}") for n in (
            "w_hi", "w_lo", "mm", "x", "e", "l", "logf", "cmm", "c", "ct", "ctsb", "row_mm", "rows")}
        p_full, p_done, p_hi, p_lo = (sem(n) for n in ("p_full", "p_done", "p_hi", "p_lo"))
        fin_done, fin_copied, out_full = sem("fin_done"), sem("fin_copied"), sem("out_full")
        bias_mm, bias_ready = sem("bias_mm"), sem("bias_ready")

        def gate(name, j):
            return sig[name][j // 4][:, j % 4, :]

        def kinds(kind):
            return {"B": ("qB", "kB", "vB", yB), "A": ("qA", "kA", "vA", yA), "F": ("fq", "fk", "fv", yF)}[kind]


        def slots_used(e, name, g, k):
            p = PH[name]
            if k == p.kc - 1:
                e.wait_ge(tile_done, (g + (p.group0 + 1)) * 4)
            else:
                before = p.slot0 - p.group0
                e.wait_ge(slot_used, g * (p.kc - 1) + (before + k + 1))

        def tile_ready(e, name, g, n):
            e.wait_ge(tile_done, g * 4 + (PH[name].group0 * 4 + n + 1))

        def tile_taken(e, name, g, n):
            who = OWNER[name][n]
            e.wait_ge(taken[who], taken_before(name, g, who) + (OWNER[name][:n + 1].count(who)))

        def bank_wait(e, key):
            b, n = USE[key]
            if n:
                e.wait_ge(bank_free[b], n)
            return ps[b]

        def source(name, k, cols):
            r = slice(k * P, (k + 1) * P)
            win = {"qA": 0, "kA": 512, "vA": 1024, "qB": 1536, "kB": 2048, "vB": 2560,
                   "gateA": 3072, "gateB": 4096}
            win2 = {"hq": 0, "hf": 512, "hi": 1024, "hg": 1536, "fq": 2048, "fk": 2560, "fv": 3072,
                    "gateH": 3592, "gateF": 4616}
            rest = {"branchA": "w_branch_a", "branchB": "w_branch_b", "out1": "w_out",
                    "down1": "w_ffn_down", "branchH": "w_branch_a_2", "branchF": "w_branch_b_2",
                    "out2": "w_out_2", "down2": "w_ffn_down_2", "pgate": "w_ple_gate_2",
                    "pproj": "w_ple_proj_2"}
            if name == "up1":
                w = a["w_ffn_up"][0].rearrange("k (t c) -> k t c", t=2)
                return [(slice(0, 512), w[r, :, bass.ds(cols * 256, 256)])]
            if name == "up2":
                return [(slice(0, 256), a["w_ffn_gate_2"][0][r, bass.ds(cols * 256, 256)]),
                        (slice(256, 512), a["w_ffn_up_2"][0][r, bass.ds(cols * 256, 256)])]
            if name in win:
                w, c0 = a["w_in"][0], win[name]
            elif name in win2:
                w, c0 = a["w_in_2"][0], win2[name]
            else:
                w, c0 = a[rest[name]][0], 0
            return [(slice(0, 512), w[r, c0 + cols * 512:c0 + (cols + 1) * 512])]

        block = ctx.enter_context(nc.Block())

        @block.sync
        def _(e):
            for tb in range(TB):
                e.dma_start(xtok[:, tb, :], a["x"][0, tb * P:(tb + 1) * P, :]).then_inc(x_full, 16)
            gains = ("norm1_g", "norm2_g", "norm_mix_g_2", "norm_ffn_g_2", "norm_ple_g_2")
            for i, n in enumerate(gains):
                e.dma_start(vrows[8 * i:8 * i + 8, 0, :], a[n].rearrange("a (r c) -> (a r) c", c=P)).then_inc(vec_full, 16)
            for i, n in enumerate(("q_norm_g", "k_norm_g", "fox_q_norm_g_2", "fox_k_norm_g_2")):
                for half in range(2):
                    e.dma_start(vrows[40 + i:41 + i, 0, 64 * half:64 * half + 64], a[n]).then_inc(vec_full, 16)
            e.dma_start(vrows[44:45, 0, :], a["hg_onorm_g_2"]).then_inc(vec_full, 16)
            e.dma_start(vrows[45:53, 0, :], a["hg_lb_logits_2"].rearrange("a (r c) -> (a r) c", c=P)).then_inc(vec_full, 16)
            cw = a["ffn_conv_w"][0].rearrange("t (r c) -> t r c", c=P)
            for t in range(3):
                row = 44 * (t % 2)
                e.dma_start(vrows[row:row + 44, 1 + t // 2, :], cw[t]).then_inc(vec_full, 16)
            e.dma_start(vrows[44:88, 2, :], a["ffn_conv_b"][0].rearrange("(r c) -> r c", c=P)).then_inc(vec_full, 16)
            e.dma_start(rb[:, :], a["rel_bias"][0]).then_inc(rb_full, 16)
            e.dma_start(fbias[:, :], a["fox_f_bias_2"].to_broadcast([P, NH])).then_inc(small_full, 16)
            with nc.allow_non_contiguous_dma(reason="eight columns of the fused input projection"):
                e.dma_start(wf_raw[:, :, :], a["w_in_2"][0][:, 3584:3592].rearrange("(k p) c -> p k c", p=P)).then_inc(small_full, 16)

            def load(name, g, k, s):
                pos = (PH[name].slot0 + (g * PH[name].kc if isinstance(g, int) else 0) + k)
                if not (isinstance(g, int) and pos < RAW_SLOTS):
                    e.wait_ge(hi_full, s - (RAW_SLOTS - 1))
                    e.wait_ge(lo_full, s - (RAW_SLOTS - 1))
                pos %= RAW_SLOTS
                parts = source(name, k, g)
                for cols, src in parts:
                    dst = w_raw[:, pos, cols]
                    if name == "up1":
                        dst = dst.rearrange("p (t c) -> p t c", t=2)
                    e.dma_start(dst, src).then_inc(raw_full[pos], 32 // len(parts))

            for i, p in enumerate(PHASES):
                if p.name in ("up1", "up2"):
                    with e.Fori(0, p.groups) as g:
                        for k in range(p.kc):
                            load(p.name, g, k, g * p.kc + (p.slot0 + k))
                else:
                    for g in range(p.groups):
                        for k in range(p.kc):
                            load(p.name, g, k, p.slot0 + g * p.kc + k)
                if p.name == "qB":
                    e.wait_ge(rb_ready, 1)
                    e.dma_start(bias_dram, rb_ext[:, :]).then_inc(scratch_full, 16)
                    e.wait_ge(scratch_full, 16)
                    e.dma_start(bias_up[:, :, :], bass.AP(bias_dram.tensor, 0, [[1, P], [640, NH], [1, S]])).then_inc(bias_full, 16)
                if p.name == "pgate":
                    e.wait_ge(x_ready, 5 * DC)
                    e.dma_start(ptok[:, :, :], a["p_2"][0, 0].rearrange("(t p) c -> p t c", p=P)).then_inc(p_full, 16)
            for half in range(2):
                for tb in range(TB):
                    e.wait_ge(fin_copied, half * TB + tb + 1)
                    e.dma_start(out[0, tb * P:(tb + 1) * P, half * 512:(half + 1) * 512],
                                otok[:, tb, half * 512:(half + 1) * 512]).then_inc(out_full, 16)
            e.wait_ge(out_full, 2 * TB * 16)

        @block.gpsimd
        def _(e):
            seq = [0]

            def link(ins):
                seq[0] += 1
                ins.then_inc(pool_seq, 1)
                e.wait_ge(pool_seq, seq[0])

            def lo(pos, s):
                e.wait_ge(hi_full, s + 1)
                e.tensor_tensor(w_lo[:, pos % SPLIT_SLOTS, :], w_raw[:, pos % RAW_SLOTS, :],
                                w_hi[:, pos % SPLIT_SLOTS, :].bitcast(F32), ALU.subtract).then_inc(lo_full, 1)

            link(e.memset(ident[:, :], 0.0))
            link(e.affine_select(out=ident[:, :], in_=ident[:, :], compare_op=ALU.not_equal, fill=1.0,
                                 base=0, pattern=[[-1, P]], channel_multiplier=1))
            link(e.memset(reverse[:, :], 0.0))
            link(e.affine_select(out=reverse[:, :], in_=reverse[:, :], compare_op=ALU.not_equal, fill=1.0,
                                 base=1 - P, pattern=[[1, P]], channel_multiplier=1))
            e.nop().then_inc(const_ready, 1)
            link(e.memset(strict[:, :], 0.0))
            link(e.affine_select(out=strict[:, :], in_=strict[:, :], compare_op=ALU.is_gt, fill=NEG,
                                 base=0, pattern=[[-1, P]], channel_multiplier=1))
            link(e.memset(causal[:, :], 0.0))
            link(e.affine_select(out=causal[:, :], in_=causal[:, :], compare_op=ALU.is_ge, fill=NEG,
                                 base=0, pattern=[[-1, P]], channel_multiplier=1))
            link(e.memset(tri[:, :], 1.0))
            link(e.affine_select(out=tri[:, :], in_=tri[:, :], compare_op=ALU.is_ge, fill=0.0,
                                 base=0, pattern=[[1, P]], channel_multiplier=-1))
            for x in SCHEDULE:
                if x[0] == "start":
                    for s in range(SPLIT_SLOTS):
                        lo(s, s)
                    link(e.memset(level_mask[:, :, :], 0.0))
                    for x, m in enumerate(LEVELS):
                        v = level_mask[:, x, :].rearrange("p (n w) -> p n w", w=2 * m)[:, :, m:]
                        n = P // (2 * m)
                        link(e.memset(v, 1.0))
                        link(e.affine_select(out=v, in_=v, compare_op=ALU.is_ge, fill=0.0, base=0,
                                             pattern=[[-2 * m, n], [0, m]], channel_multiplier=1))
                        link(e.affine_select(out=v, in_=v, compare_op=ALU.is_ge, fill=0.0, base=m - 1,
                                             pattern=[[2 * m, n], [0, m]], channel_multiplier=-1))
                    link(e.affine_select(out=level_mask[:, 6, :], in_=level_mask[:, 6, :], compare_op=ALU.not_equal,
                                         fill=1.0, base=0, pattern=[[-1, P]], channel_multiplier=1))
                    e.nop().then_inc(const_ready, 1)
                elif x[0] == "slot":
                    s = PH[x[1]].slot0 + x[2] * PH[x[1]].kc + x[3] + SPLIT_SLOTS
                    if s < SLOTS:
                        lo(s, s)
                elif x[0] == "up":
                    p = PH[x[1]]
                    with e.Fori(0, p.groups) as g:
                        for k in range(p.kc):
                            s = p.slot0 + k + SPLIT_SLOTS
                            lo(s, g * p.kc + s)
                elif x[0] == "att" and x[1] == "B" and 0 <= x[2] - 1 < STEPS:
                    i, n = x[2] - 1, ((x[2] - 1) // NH + 1) * P
                    e.wait_ge(A["B"]["beta_ready"], i + 1)
                    e.wait_ge(A["B"]["after_ready"], i + 1)
                    w = work[i % 4]
                    e.tensor_tensor(w[:, 0:n], w[:, 0:n], after[i % 2][:, 0:n], ALU.mult).then_inc(A["B"]["p_ready"], 1)
                elif x[0] == "hg_decay":
                    e.wait_ge(x_ready, 3 * DC)
                    link(e.memset(hQ[:, :, :], 0.0))
                    e.memset(hK[:, :, :], 0.0).then_inc(hgs["zero"], 1)
                elif x[0] == "hg_qk":
                    m = LEVELS[x[1]]
                    k_, e_, o_ = (t[:, :, :].rearrange("p h (n w) -> p (h n) w", w=2 * m)[:, :, 0:m] for t in (hk, hE, hK))
                    e.wait_ge(hgs["zero"], 1)
                    e.wait_ge(hgs["exp"], x[1] + 1)
                    if x[1]:
                        e.wait_ge(hgs["lev_done"], HH * x[1])
                    e.tensor_tensor(o_, k_, e_, ALU.mult).then_inc(hgs["K"], 1)

        def att_act(e, kind, i):
            a_, ring = A[kind], work[i % 4]
            n = (i // NH + 1) * P
            if i < STEPS and kind == "B":
                e.wait_ge(a_["s_ready"], i + 1)
                if i >= 2:
                    e.wait_ge(a_["after_ready"], i - 1)
                e.activation(keep[i % 2][:, 0:n], ring[:, 0:n], ACT.Sigmoid, scale=-1.0).then_inc(a_["keep_ready"], 1)
                e.activation(ring[:, 0:n], ring[:, 0:n], ACT.Sigmoid).then_inc(a_["beta_ready"], 1)
            elif i < STEPS:
                k = 0 if kind == "A" else 1
                e.wait_ge(a_["s_ready"], i + 1)
                e.activation(ring[:, 0:n], ring[:, 0:n], ACT.Exp, scale=-1.0 if kind == "A" else 1.0,
                             bias=mneg[:, k, i:i + 1], accum_out=rsum[:, k, i:i + 1]).then_inc(a_["p_ready"], 1)
            j = i - LAG
            if kind == "F" and 0 <= j < STEPS:
                pt_out(e, kind, j, lambda o, s: e.activation(o, s, ACT.Copy))
            j = i - LAG - 2
            if j > 0 and j % NH == 0:
                qb = j // NH - 1
                e.wait_ge(a_["ot_done"], qb + 1)
                b, use = USE[("ot", kind, qb)]
                y = kinds(kind)[3]
                e.activation(y[0][:, :, qb * P:(qb + 1) * P], ps[b][:, :].rearrange("p (c t) -> p c t", c=4),
                             ACT.Copy).then_inc(a_["yhi"], 1)

        def pt_out(e, kind, j, copy):
            a_ = A[kind]
            n = (j // NH + 1) * P
            e.wait_ge(a_["tr_done"], j + 1)
            if j >= 2:
                e.wait_ge(a_["pv_done"], j - 1)
            b, use = USE[("pt", kind, j)]
            copy(work[4 + j % 2][:, 0:n], ps[b][:, 0:n]).then_inc(bank_free[b], 1)

        def conv_col(tap, tile, half):
            return bass.ds(tile + (53 + 44 * tap + FC * half), 1) if not isinstance(tile, int) else \
                slice(53 + 44 * tap + FC * half + tile, 54 + 44 * tap + FC * half + tile)

        def up_act(e, name, hi):
            p, q = PH[name], up_sem[name]

            def group(g, u_):
                banks = 4 * u_
                for k in range(p.kc):
                    s = p.slot0 + k + SPLIT_SLOTS
                    st = s + (g * p.kc if isinstance(g, int) else 0)
                    hi(st if isinstance(g, int) else s, g * p.kc + s, name, g, k)
                if name == "up1":
                    for n in range(4):
                        tile_ready(e, name, g, n)
                        if not isinstance(g, int) or g > 0:
                            e.wait_ge(q["lo"], g * 2)
                        e.activation(acc[:, n, :], ps[banks + n][:, :], ACT.Identity,
                                     bias=vec[:, conv_col(3, g * 2 + n % 2, n // 2)],
                                     scale=vec[:, conv_col(2, g * 2 + n % 2, n // 2)]).then_inc(q["first"], 1)
                    for n in range(2):
                        e.wait_ge(taken["d"], taken_before(name, g, "d") + n + 1)
                        e.activation(acc[:, n, :], acc[:, n, :], ACT.Silu).then_inc(q["silu"], 1)
                else:
                    for n in range(2):
                        tile_ready(e, name, g, n)
                        if not isinstance(g, int) or g > 0:
                            e.wait_ge(q["lo"], g * 2 - 1 + n)
                        e.activation(acc[:, n, :], ps[banks + n][:, :], ACT.Silu).then_inc(taken["a"], 1)
                for n in range(2):
                    e.wait_ge(q["prod"], g * 2 + n + 1)
                    dst = g_hi[:, bass.ds(g * 2 + n, 1), :].rearrange("p a t -> p (a t)")
                    e.wait_ge(const_ready, 2)
                    e.activation(dst, acc[:, n, :], ACT.Copy).then_inc(q["hi"], 1)

            up_groups(e, p, group)

        def up_groups(e, p, group):
            group(0, 0)
            group(1, 1)
            with e.Fori(1, p.groups // 2) as it:
                group(it * 2, 0)
                group(it * 2 + 1, 1)
            group(p.groups - 1, 0)

        @block.scalar
        def _(e):
            seq = [0]

            def link(ins):
                seq[0] += 1
                ins.then_inc(act_seq, 1)
                e.wait_ge(act_seq, seq[0])

            def hi(pos, s, name=None, g=None, k=None):
                r = pos % RAW_SLOTS
                e.wait_ge(raw_full[r], (s - pos) * (32 // RAW_SLOTS) + 32 * (pos // RAW_SLOTS + 1))
                if name:
                    slots_used(e, name, g, k)
                e.activation(w_hi[:, pos % SPLIT_SLOTS, :], w_raw[:, r, :], ACT.Copy).then_inc(hi_full, 1)

            table = [None]

            def uses(name):
                if name == "ln_exp" and table[0] != name:
                    e.preload_act_table_set("natural_log_exp_and_others")
                table[0] = name

            sq_n, sum_n = [0], [0]

            def square(src):
                n = sq_n[0]
                sq_n[0] += 1
                if n >= 2:
                    e.wait_ge(sq_used, n - 1)
                e.activation(sq_ring[n % 2][:, :], src, ACT.Square).then_inc(sq_ready, 1)

            for x in SCHEDULE:
                what = x[0]
                if what == "start":
                    for s in range(SPLIT_SLOTS):
                        hi(s, s)
                elif what == "slot":
                    _, name, g, k = x
                    s = PH[name].slot0 + g * PH[name].kc + k + SPLIT_SLOTS
                    if s < SLOTS:
                        hi(s, s, name, g, k)
                elif what == "sumsq":
                    e.wait_ge(x_ready, x[1] * DC + x[2] + 1)
                    square(xT[:, x[2], :])
                    sum_n[0] += 1
                elif what == "norm":
                    uses("ln_exp")
                    e.wait_ge(sq_used, sum_n[0])
                    link(e.activation(work[3][:, :], ps[4][:, :], ACT.Ln, bias=EPS))
                    e.activation(work[2][:, :], work[3][:, :], ACT.Exp, scale=-0.5).then_inc(rstd_ready, 1)
                    for j in range(DC):
                        e.wait_ge(hf_ready, x[1] * DC + j + 1)
                        e.activation(h_hi[:, j, :], work[j % 2][:, :], ACT.Copy).then_inc(hhi_ready, 1)
                elif what == "take":
                    _, name, g = x
                    for n in range(4):
                        own = OWNER[name][n] == "a"
                        if own:
                            tile_ready(e, name, g, n)
                        if not own:
                            pass
                        elif name in ("qB", "kB", "qA", "kA", "fq", "fk"):
                            e.activation(qk1[name][:, n, :], ps[n][:, :], ACT.Copy,
                                         scale=HD ** -0.5 if name == "qB" else 1.0).then_inc(taken["a"], 1)
                        elif name in vtok:
                            e.activation(vtok[name][:, n, :], ps[n][:, :], ACT.Copy).then_inc(taken["a"], 1)
                        elif name in sig:
                            uses("sigmoid")
                            e.activation(gate(name, 4 * g + n), ps[n][:, :], ACT.Sigmoid).then_inc(taken["a"], 1)
                        elif name in ("hq", "hg"):
                            dst = hq if name == "hq" else hgate
                            uses("silu")
                            e.activation(dst[:, n, :], ps[n][:, :], ACT.Silu).then_inc(taken["a"], 1)
                        elif name == "hf":
                            uses("sigmoid")
                            e.activation(hk[:, n, :], ps[n][:, :], ACT.Sigmoid).then_inc(taken["a"], 1)
                    if name in ("branchA", "branchF"):
                        for n in range(4):
                            j = 4 * g + n
                            e.wait_ge(mix_ready, (DC if name == "branchF" else 0) + j + 1)
                            e.activation(h_hi[:, j, :], gate("gateA" if name == "branchA" else "gateF", j), ACT.Copy).then_inc(mixhi_ready, 1)
                elif what == "square":
                    tile_taken(e, x[1], 0, x[2])
                    square(qk1[x[1]][:, x[2], :])
                elif what == "scale":
                    _, name, n = x
                    uses("ln_exp")
                    b, use = USE[x]
                    count = {"qA": 0, "kA": 4, "fq": 8, "fk": 12}[name] + n
                    t = work[4 + n % 2]
                    if count >= 2:
                        prev = [(m, c) for m in ("qA", "kA", "fq", "fk") for c in range(4)][count - 2]
                        e.wait_ge(qk_ready[prev[0]], prev[1] + 1)
                    sum_n[0] += 1
                    e.wait_ge(sq_used, sum_n[0])
                    link(e.activation(t[:, :], ps[b][:, :], ACT.Ln, bias=EPS))
                    e.nop().then_inc(bank_free[b], 1)
                    e.activation(t[:, :], t[:, :], ACT.Exp, scale=-0.5).then_inc(qkrs_ready, 1)
                elif what == "att":
                    uses("sigmoid" if x[1] == "B" else "ln_exp")
                    att_act(e, x[1], x[2])
                elif what == "up":
                    uses("silu")
                    up_act(e, x[1], hi)
                elif x == ("foxf", 0):
                    e.wait_ge(small_full, 32)
                    e.activation(wf_hi[:, :, :], wf_raw[:, :, :], ACT.Copy).then_inc(ff["w_hi"], 1)
                elif x == ("foxf", 1):
                    uses("ln_exp")
                    e.wait_ge(ff["x"], 1)
                    link(e.activation(fx[:, 1, :, :], fx[:, 1, :, :], ACT.Exp))
                    e.activation(fx[:, 1, :, :], fx[:, 1, :, :], ACT.Ln, bias=1.0).then_inc(ff["l"], 1)
                elif what == "hg_decay":
                    uses("ln_exp")
                    e.wait_ge(hgs["lb"], 1)
                    e.activation(lb[:, 1:3, :], lb[:, 1:3, :], ACT.Exp).then_inc(hgs["lb_exp"], 1)
                    e.wait_ge(hgs["fg"], 1)
                    e.activation(hE[:, :, :], hE[:, :, :], ACT.Ln).then_inc(hgs["log"], 1)
                elif what == "hg_prep":
                    uses("ln_exp")
                    e.wait_ge(hgs["diff"], x[1] + 1)
                    e.activation(hE[:, :, :], hE[:, :, :], ACT.Exp).then_inc(hgs["exp"], 1)
                elif what == "hg_scale":
                    uses("ln_exp")
                    e.wait_ge(hgs["K"], 6)
                    e.wait_ge(hgs["Q"], 6)
                    e.activation(hE[:, :, :], hb[:, :, :], ACT.Exp).then_inc(hgs["eb"], 1)
                    e.wait_ge(hgs["kd"], 1)
                    e.activation(hK[:, :, :], hK[:, :, :], ACT.Exp).then_inc(hgs["el"], 1)
                elif what == "hg_kt":
                    for h in range(HH):
                        e.wait_ge(hgs["kt_done"], h + 1)
                        b, use = USE[("kt", h)]
                        e.activation(hKt[:, h, :], ps[b][:, :], ACT.Copy).then_inc(bank_free[b], 1)
                elif what == "hg_out":
                    if x[1] < TB:
                        uses("ln_exp")
                        pr = x[1]
                        b, use = USE[("ho", pr)]
                        e.wait_ge(hgs["o_done"], pr + 1)
                        if pr:
                            e.wait_ge(hgs["o_ms"], pr)
                        e.activation(work[0][:, :], ps[b][:, :], ACT.Square).then_inc(hgs["o_sq"], 1)
                        e.wait_ge(hgs["o_ms"], pr + 1)
                        link(e.activation(hstat[:, pr, 1, :], hstat[:, pr, 0, :], ACT.Ln, bias=EPS, scale=1.0 / P))
                        e.activation(hstat[:, pr, 2, :], hstat[:, pr, 1, :], ACT.Exp, scale=-0.5).then_inc(hgs["o_rs"], 1)
                    if x[1] > 0:
                        pr = x[1] - 1
                        e.wait_ge(hgs["y"], pr + 1)
                        e.activation(yH[0][:, :, pr * P:(pr + 1) * P], work[2 + pr % 2][:, :].rearrange("p (h t) -> p h t", h=HH),
                                     ACT.Copy).then_inc(hgs["yhi"], 1)
                elif what == "pT":
                    for c in range(2):
                        b, use = USE[("pT", c)]
                        e.wait_ge(p_done, c + 1)
                        e.activation(pT_hi[:, c, :], ps[b][:, :], ACT.Copy).then_inc(p_hi, 1)
                elif what == "finish":
                    pass

        def take_dve(e, name, g, link):
            for n in range(4):
                if OWNER[name][n] != "d":
                    continue
                tile_ready(e, name, g, n)
                j = 4 * g + n
                if name in ("qB", "kB", "qA", "kA", "fq", "fk"):
                    e.tensor_scalar(qk1[name][:, n, :], ps[n][:, :], HD ** -0.5 if name == "qB" else 1.0, None,
                                    ALU.mult).then_inc(taken["d"], 1)
                elif name in vtok:
                    e.tensor_copy(vtok[name][:, n, :], ps[n][:, :]).then_inc(taken["d"], 1)
                elif name in ("branchB", "branchH"):
                    t = gate("gate" + name[-1], j)
                    tile_taken(e, "gate" + name[-1], g, n)
                    e.tensor_tensor(t, ps[n][:, :], t, ALU.mult).then_inc(taken["d"], 1)
                elif name in ("branchA", "branchF"):
                    first, second = ("gateB", "gateA") if name == "branchA" else ("gateH", "gateF")
                    t = gate(second, j)
                    tile_taken(e, second, g, n)
                    e.tensor_tensor(t, ps[n][:, :], t, ALU.mult).then_inc(taken["d"], 1)
                    e.wait_ge(taken["d"], taken_before(name, g, "d") + n + 1)
                    e.tensor_tensor(t, t, gate(first, j), ALU.add).then_inc(mix_ready, 1)
                elif name in ("out1", "out2", "down1", "down2"):
                    k = {"out1": 1, "down1": 2, "out2": 3, "down2": 4}[name]
                    e.tensor_tensor(xT[:, j, :], ps[n][:, :], xT[:, j, :], ALU.add).then_inc(x_ready, 1)
                    e.wait_ge(x_ready, k * DC + j + 1)
                    e.nop().then_inc(taken["d"], 1)
                elif name == "pproj":
                    t = gate("pgate", j)
                    tile_taken(e, "pgate", g, n)
                    e.tensor_tensor(t, ps[n][:, :], t, ALU.mult).then_inc(taken["d"], 1)
                    e.wait_ge(taken["d"], taken_before(name, g, "d") + n + 1)
                    e.tensor_tensor(xT[:, j, :], xT[:, j, :], t, ALU.add).then_inc(x_ready, 1)
            if name in ("branchA", "branchF"):
                for n in range(4):
                    j = 4 * g + n
                    e.wait_ge(mixhi_ready, (DC if name == "branchF" else 0) + j + 1)
                    e.tensor_tensor(h_lo[:, j, :], gate("gateA" if name == "branchA" else "gateF", j),
                                    h_hi[:, j, :].bitcast(F32), ALU.subtract).then_inc(mixlo_ready, 1)

        def att_dve(e, kind, i, link):
            a_, ring = A[kind], work[i % 4]
            qb, h = divmod(i, NH)
            n = (qb + 1) * P
            j = i - 1
            if kind == "B" and 0 <= j < STEPS:
                m = (j // NH + 1) * P
                e.wait_ge(a_["keep_ready"], j + 1)
                if j >= 2:
                    e.wait_ge(a_["p_ready"], j - 1)
                k_, o_ = keep[j % 2], after[j % 2]
                link(e.memset(o_[:, m - 1:m], 1.0))
                rev = lambda t, lo_, hi_: t[:, hi_ - 1:(lo_ - 1 if lo_ else None):-1]
                e.tensor_tensor_scan(rev(o_, 0, m - 1), rev(k_, 1, m), rev(k_, 1, m), 1.0,
                                     ALU.mult, ALU.bypass).then_inc(a_["after_ready"], 1)
            if i < STEPS:
                e.wait_ge(a_["sc_done"], i + 1)
                if i >= 4:
                    e.wait_ge(a_["tr_done"], i - 3)
                b, use = USE[("sc", kind, i)]
                if kind == "B":
                    if qb:
                        e.tensor_copy(ring[:, 0:n - P], ps[b][:, 0:n - P])
                    link(e.tensor_tensor(ring[:, n - P:n], ps[b][:, n - P:n], strict[:, :], ALU.add))
                    e.nop().then_inc(bank_free[b], 1)
                    e.nop().then_inc(a_["s_ready"], 1)
                elif kind == "A":
                    if i == 0:
                        e.wait_ge(bias_ready, NH)
                        link(e.tensor_scalar(bias_mask[0:64, :, S - 64:S], bias_mask[0:64, :, S - 64:S], NEG, None, ALU.add))
                    link(e.tensor_tensor_reduce(out=ring[:, 0:n], in0=ps[b][:, 0:n], in1=bias_mask[:, h, S - n:S],
                                                scale=-1.0, scalar=3e38, op0=ALU.add, op1=ALU.min,
                                                accum_out=mneg[:, 0, i:i + 1]))
                    e.nop().then_inc(bank_free[b], 1)
                    e.nop().then_inc(a_["s_ready"], 1)
                else:
                    link(e.scalar_tensor_tensor(out=ring[:, 0:n], in0=ps[b][:, 0:n], scalar=ctok[:, qb, h:h + 1],
                                                in1=c_rows[:, h, 0:n], op0=ALU.add, op1=ALU.add))
                    e.nop().then_inc(bank_free[b], 1)
                    link(e.tensor_tensor(ring[:, n - P:n], ring[:, n - P:n], causal[:, :], ALU.add))
                    e.tensor_reduce(mneg[:, 1, i:i + 1], ring[:, 0:n], axis=AX.X, op=ALU.max, negate=True).then_inc(a_["s_ready"], 1)
            j = i - LAG
            if kind != "F" and 0 <= j < STEPS:
                pt_out(e, kind, j, lambda o, s: e.tensor_copy(o, s))
            j = i - LAG - 1
            if 0 <= j < STEPS and j % NH == NH - 1:
                q = j // NH
                e.wait_ge(a_["pv_done"], j + 1)
                if q:
                    e.wait_ge(a_["ot_done"], q)
                b, use = USE[("out", kind, q)]
                o3 = work[6][:, :].rearrange("p (h d) -> p h d", h=NH)
                p3 = ps[b][:, :].rearrange("p (h d) -> p h d", h=NH)
                if kind == "B":
                    link(e.tensor_copy(o3, p3))
                else:
                    k = 0 if kind == "A" else 1
                    c = slice(q * NH, (q + 1) * NH)
                    link(e.reciprocal(rinv[:, k, c], rsum[:, k, c]))
                    link(e.tensor_tensor(o3, p3, rinv[:, k, c][:, :, None].to_broadcast([P, NH, HD]), ALU.mult))
                e.nop().then_inc(bank_free[b], 1)
                e.nop().then_inc(a_["ot_ready"], 1)
            j = i - LAG - 2
            if j > 0 and j % NH == 0:
                q = j // NH - 1
                e.wait_ge(a_["yhi"], q + 1)
                b, use = USE[("ot", kind, q)]
                y = kinds(kind)[3]
                c = slice(q * P, (q + 1) * P)
                link(e.tensor_tensor(y[1][:, :, c], ps[b][:, :].rearrange("p (c t) -> p c t", c=4),
                                     y[0][:, :, c].bitcast(F32), ALU.subtract))
                e.nop().then_inc(bank_free[b], 1)
                e.nop().then_inc(a_["ylo"], 1)

        def up_dve(e, name):
            p, q = PH[name], up_sem[name]

            def group(g, u_):
                banks = 4 * u_
                if name == "up1":
                    for n in range(4):
                        col = g * 2 + n % 2
                        e.wait_ge(q["first"], g * 4 + n + 1)
                        for shift, tap, s_ in ((1, 1, q["conv1"]), (2, 0, taken["d"])):
                            if shift == 2:
                                e.wait_ge(q["conv1"], g * 4 + n + 1)
                            o = acc[:, n, shift:S]
                            e.scalar_tensor_tensor(out=o, in0=ps[banks + n][:, 0:S - shift],
                                                   scalar=vec[:, conv_col(tap, col, n // 2)], in1=o,
                                                   op0=ALU.mult, op1=ALU.add).then_inc(s_, 1)
                    for n in range(2):
                        e.wait_ge(taken["d"], taken_before(name, g, "d") + n + 3)
                        e.wait_ge(q["silu"], g * 2 + n + 1)
                        e.tensor_tensor(acc[:, n, :], acc[:, n, :], acc[:, n + 2, :], ALU.mult).then_inc(q["prod"], 1)
                else:
                    for n in range(2):
                        tile_ready(e, name, g, n + 2)
                        e.wait_ge(taken["a"], taken_before(name, g, "a") + n + 1)
                        e.tensor_tensor(acc[:, n, :], ps[banks + 2 + n][:, :], acc[:, n, :], ALU.mult).then_inc(taken["d"], 1)
                        e.wait_ge(taken["d"], taken_before(name, g, "d") + n + 1)
                        e.nop().then_inc(q["prod"], 1)
                for n in range(2):
                    e.wait_ge(q["hi"], g * 2 + n + 1)
                    tile = bass.ds(g * 2 + n, 1)
                    dst = g_lo[:, tile, :].rearrange("p a t -> p (a t)")
                    src = g_hi[:, tile, :].rearrange("p a t -> p (a t)").bitcast(F32)
                    e.tensor_tensor(dst, acc[:, n, :], src, ALU.subtract).then_inc(q["lo"], 1)

            up_groups(e, p, group)

        def hg_dve(e, x, link):
            blocks = lambda t, w: t[:, :, :].rearrange("p h (n w) -> p (h n) w", w=w)
            if x[0] == "hg_decay":
                e.wait_ge(hgs["lb_exp"], 1)
                link(e.tensor_tensor(lb[:, 3, :], lb[:, 1, :], lb[:, 2, :], ALU.add))
                link(e.reciprocal(lb[:, 3, :], lb[:, 3, :]))
                link(e.tensor_tensor(lb[:, 4, :], lb[:, 1, :], lb[:, 3, :], ALU.mult))
                link(e.tensor_scalar(lb[:, 5, :], lb[:, 4, :], -1.0, 1.0, ALU.mult, ALU.add))
                tile_taken(e, "hf", 0, 3)
                for h in range(HH):
                    ins = e.tensor_scalar(hE[:, h, :], hk[:, h, :], lb[:, 5, h:h + 1], lb[:, 4, h:h + 1], ALU.mult, ALU.add)
                link(ins)
                link(e.tensor_scalar(hk[:, :, :], hE[:, :, :], -1.0, 1.0, ALU.mult, ALU.add))
                e.nop().then_inc(hgs["fg"], 1)
                e.wait_ge(hgs["log"], 1)
                for h in range(HH):
                    ins = e.tensor_tensor_scan(hb[:, h, :], chunk_start[:, :], hE[:, h, :], 0.0, ALU.mult, ALU.add)
                link(ins)
                link(e.memset(hS[:, :, :], 0.0))
            elif x[0] == "hg_prep":
                lev, m = x[1], LEVELS[x[1]]
                b_, e_ = blocks(hb, 2 * m), blocks(hE, 2 * m)
                mid = b_[:, :, m - 1:m].to_broadcast([P, HH * S // (2 * m), m])
                if lev:
                    e.wait_ge(hgs["K"], lev)
                    e.wait_ge(hgs["Q"], lev)
                e.tensor_tensor(e_[:, :, 0:m], mid, b_[:, :, 0:m], ALU.subtract)
                link(e.tensor_tensor(e_[:, :, m:], b_[:, :, m:], mid, ALU.subtract))
                e.nop().then_inc(hgs["diff"], 1)
            elif x[0] == "hg_qk":
                lev, m = x[1], LEVELS[x[1]]
                q_, e_, Q_ = (blocks(t, 2 * m) for t in (hq, hE, hQ))
                e.wait_ge(hgs["exp"], lev + 1)
                if lev:
                    e.wait_ge(hgs["lev_done"], HH * lev)
                else:
                    e.wait_ge(hgs["zero"], 1)
                    tile_taken(e, "hq", 0, 3)
                e.tensor_tensor(Q_[:, :, m:], q_[:, :, m:], e_[:, :, m:], ALU.mult).then_inc(hgs["Q"], 1)
            elif x[0] == "hg_merge":
                lev = x[1]
                for h in range(HH):
                    b, use = USE[("lev", lev, h)]
                    e.wait_ge(hgs["lev_done"], HH * lev + h + 1)
                    o = hS[:, h, :].rearrange("p (n w) -> p n w", w=P)
                    mask = level_mask[:, lev:lev + 1, :].bitcast(U32).to_broadcast([P, TB, P])
                    e.wait_ge(const_ready, 2)
                    e.copy_predicated(o, mask, ps[b][:, :].rearrange("p (n w) -> p n w", w=P)).then_inc(bank_free[b], 1)
            elif x[0] == "hg_scale":
                e.wait_ge(hgs["eb"], 1)
                e.wait_ge(hgs["lev_done"], HH * 7)
                last = lambda t: blocks(t, CH)[:, :, CH - 1:CH]
                e.tensor_tensor(hQ[:, :, :], hq[:, :, :], hE[:, :, :], ALU.mult)
                link(e.tensor_copy(decay[:, :, :].rearrange("p h c -> p (h c)")[:, :, None], last(hE)))
                link(e.tensor_tensor(blocks(hK, CH), last(hb).to_broadcast([P, HH * S // CH, CH]), blocks(hb, CH), ALU.subtract))
                e.nop().then_inc(hgs["kd"], 1)
                e.wait_ge(hgs["el"], 1)
                link(e.tensor_tensor(hK[:, :, :], hK[:, :, :], hk[:, :, :], ALU.mult))
                e.nop().then_inc(hgs["scale"], 1)
            elif x[0] == "hg_state":
                c = x[1]
                b, use = USE[("st", c)]
                e.wait_ge(hgs["u_done"], c + 1)
                if c == 0:
                    link(e.tensor_copy(state[:, 1, :], ps[b][:, :]))
                else:
                    for h in range(HH):
                        v = slice(h * P, (h + 1) * P)
                        ins = e.scalar_tensor_tensor(out=state[:, c + 1, v], in0=state[:, c, v], scalar=decay[:, h, c:c + 1],
                                                     in1=ps[b][:, v], op0=ALU.mult, op1=ALU.add)
                    link(ins)
                e.nop().then_inc(bank_free[b], 1)
                e.nop().then_inc(hgs["state"], 1)
            elif x[0] == "hg_out":
                if x[1] < TB:
                    pr = x[1]
                    b, use = USE[("ho", pr)]
                    e.wait_ge(hgs["o_sq"], pr + 1)
                    e.tensor_reduce(hstat[:, pr, 0, :], work[0][:, :].rearrange("p (h v) -> p h v", h=HH), axis=AX.X, op=ALU.add).then_inc(hgs["o_ms"], 1)
                    e.wait_ge(hgs["o_rs"], pr + 1)
                    if pr:
                        e.wait_ge(hgs["ot_done"], pr)
                    link(e.tensor_tensor(work[1][:, :].rearrange("p (h v) -> p h v", h=HH), ps[b][:, :].rearrange("p (h v) -> p h v", h=HH),
                                         hstat[:, pr, 2, :][:, :, None].to_broadcast([P, HH, P]), ALU.mult))
                    e.nop().then_inc(bank_free[b], 1)
                    e.nop().then_inc(hgs["o_tok"], 1)
                if x[1] > 0:
                    pr = x[1] - 1
                    b, use = USE[("hot", pr)]
                    e.wait_ge(hgs["ot_done"], pr + 1)
                    tile_taken(e, "hg", 0, 3)
                    c = slice(pr * P, (pr + 1) * P)
                    w3 = work[2 + pr % 2][:, :].rearrange("p (h t) -> p h t", h=HH)
                    link(e.scalar_tensor_tensor(out=w3, in0=ps[b][:, :].rearrange("p (h t) -> p h t", h=HH), scalar=vec[:, 44:45],
                                                in1=hgate[:, :, c], op0=ALU.mult, op1=ALU.mult))
                    e.nop().then_inc(bank_free[b], 1)
                    e.nop().then_inc(hgs["y"], 1)
                    e.wait_ge(hgs["yhi"], pr + 1)
                    e.tensor_tensor(yH[1][:, :, c], w3, yH[0][:, :, c].bitcast(F32), ALU.subtract).then_inc(hgs["ylo"], 1)

        @block.vector
        def _(e):
            seq = [0]

            def link(ins):
                seq[0] += 1
                ins.then_inc(dve_seq, 1)
                e.wait_ge(dve_seq, seq[0])

            for x in SCHEDULE:
                what = x[0]
                if what == "start":
                    e.memset(mean_d[:, :], 1.0 / D)
                    link(e.memset(mean_h[:, :], 0.0))
                    e.memset(mean_h[0:64, 0:64], 1.0 / HD)
                    e.memset(mean_h[64:128, 64:128], 1.0 / HD)
                    e.memset(ones[:, :], 1.0)
                    link(e.memset(chunk_start[:, :], 1.0))
                    link(e.memset(chunk_start[:, :].rearrange("p (n w) -> p n w", w=CH)[:, :, 0:1], 0.0))
                    e.nop().then_inc(const_dve, 1)
                    e.wait_ge(vec_done, 1)
                    e.tensor_copy(vec[:, :], ps[7][:, 0:229]).then_inc(vec_ready, 1)
                    for j in range(DC):
                        e.wait_ge(xt_done, j + 1)
                        e.tensor_copy(xT[:, j, :], ps[j][:, :]).then_inc(x_ready, 1)
                    e.wait_ge(x_ready, DC)
                    for b in range(4, 8):
                        e.nop().then_inc(bank_free[b], 1)
                    e.wait_ge(vec_ready, 1)
                    e.tensor_scalar(qk_gain[:, 0:1], vec[:, 40:41], HD ** -0.5, None, ALU.mult)
                    e.tensor_scalar(qk_gain[:, 1:2], vec[:, 42:43], HD ** -0.5, None, ALU.mult)
                    e.wait_ge(rb_full, 16)
                    e.tensor_copy(rb_ext[:, 0:383], rb[:, 256:257].to_broadcast([NH, 383]))
                    link(e.tensor_copy(rb_ext[:, 383:639], rb[:, 256:0:-1]))
                    link(e.memset(rb_ext[:, 639:640], 0.0))
                    e.nop().then_inc(rb_ready, 1)
                    link(e.tensor_tensor(lb[:, 0, :], vec[:, 45:49], vec[:, 49:53], ALU.max))
                    e.tensor_tensor(lb[:, 1, :], vec[:, 45:49], lb[:, 0, :], ALU.subtract)
                    e.tensor_tensor(lb[:, 2, :], vec[:, 49:53], lb[:, 0, :], ALU.subtract).then_inc(hgs["lb"], 1)
                elif what == "norm":
                    e.wait_ge(rstd_ready, x[1] + 1)
                    gain = 8 * x[1]

                    def scaled(j):
                        if j >= 2:
                            e.wait_ge(hlo_ready, x[1] * DC + j - 1)
                        e.scalar_tensor_tensor(out=work[j % 2][:, :], in0=xT[:, j, :], scalar=vec[:, gain + j:gain + j + 1],
                                               in1=work[2][:, :], op0=ALU.mult, op1=ALU.mult).then_inc(hf_ready, 1)
                    scaled(0)
                    for j in range(DC):
                        if j + 1 < DC:
                            scaled(j + 1)
                        e.wait_ge(hhi_ready, x[1] * DC + j + 1)
                        e.tensor_tensor(h_lo[:, j, :], work[j % 2][:, :], h_hi[:, j, :].bitcast(F32), ALU.subtract).then_inc(hlo_ready, 1)
                    e.nop().then_inc(bank_free[4], 1)
                elif what == "take":
                    take_dve(e, x[1], x[2], link)
                elif what == "scale":
                    _, name, n = x
                    count = {"qA": 0, "kA": 4, "fq": 8, "fk": 12}[name] + n
                    e.wait_ge(qkrs_ready, count + 1)
                    t = qk1[name][:, n, :]
                    g = {"qA": qk_gain[:, 0:1], "kA": vec[:, 41:42], "fq": qk_gain[:, 1:2], "fk": vec[:, 43:44]}[name]
                    e.scalar_tensor_tensor(out=t, in0=t, scalar=g, in1=work[4 + n % 2][:, :], op0=ALU.mult, op1=ALU.mult).then_inc(qk_ready[name], 1)
                elif what == "att":
                    att_dve(e, x[1], x[2], link)
                elif what == "up":
                    up_dve(e, x[1])
                elif x == ("foxf", 0):
                    e.wait_ge(ff["w_hi"], 1)
                    e.tensor_tensor(wf_lo[:, :, :], wf_raw[:, :, :], wf_hi[:, :, :].bitcast(F32), ALU.subtract).then_inc(ff["w_lo"], 1)
                    e.wait_ge(ff["mm"], 1)
                    b, use = USE[x]
                    link(e.tensor_tensor(fx[:, 0, :, :], ps[b][:, 0:32].rearrange("p (t h) -> p t h", h=NH),
                                         fbias[:, None, :].to_broadcast([P, TB, NH]), ALU.add))
                    e.nop().then_inc(bank_free[b], 1)
                    e.scalar_tensor_tensor(out=fx[:, 1, :, :], in0=fx[:, 0, :, :], scalar=-1.0, in1=fx[:, 0, :, :],
                                           op0=ALU.mult, op1=ALU.min).then_inc(ff["x"], 1)
                elif x == ("foxf", 1):
                    e.wait_ge(ff["l"], 1)
                    e.scalar_tensor_tensor(out=fx[:, 2, :, :], in0=fx[:, 0, :, :], scalar=0.0, in1=fx[:, 1, :, :],
                                           op0=ALU.min, op1=ALU.subtract).then_inc(ff["logf"], 1)
                    e.wait_ge(ff["cmm"], 1)
                    b, use = USE[x]
                    link(e.tensor_copy(ctok[:, :, :], ps[b][:, 0:32].rearrange("p (t h) -> p t h", h=NH)))
                    e.nop().then_inc(bank_free[b], 1)
                elif x == ("foxf", 2):
                    e.wait_ge(ff["ct"], 1)
                    b, use = USE[x]
                    link(e.tensor_scalar(cT[:, :], ps[b][0:NH, :], -1.0, None, ALU.mult))
                    e.nop().then_inc(bank_free[b], 1)
                    e.nop().then_inc(ff["ctsb"], 1)
                elif what == "foxc":
                    h = x[1]
                    e.wait_ge(ff["row_mm"], h + 1)
                    b, use = USE[x]
                    e.tensor_copy(c_rows[:, h, :], ps[b][:, :]).then_inc(bank_free[b], 1)
                elif what == "bias":
                    b, use = USE[x]
                    e.wait_ge(bias_mm, x[1] + 1)
                    link(e.tensor_copy(bias_mask[:, x[1], :], ps[b][:, :]))
                    e.nop().then_inc(bank_free[b], 1)
                    e.nop().then_inc(bias_ready, 1)
                elif what in ("hg_decay", "hg_prep", "hg_qk", "hg_merge", "hg_scale", "hg_state", "hg_out"):
                    hg_dve(e, x, link)
                elif what == "pT":
                    for c in range(2):
                        b, use = USE[("pT", c)]
                        e.wait_ge(p_hi, c + 1)
                        link(e.tensor_tensor(pT_lo[:, c, :], ps[b][:, :], pT_hi[:, c, :].bitcast(F32), ALU.subtract))
                        e.nop().then_inc(bank_free[b], 1)
                    e.nop().then_inc(p_lo, 1)
                elif what == "finish":
                    for j in range(8):
                        half, tb = j // 4, j % 4
                        e.wait_ge(fin_done, j + 1)
                        b, use = USE[("fin", j)]
                        link(e.tensor_copy(otok[:, tb, half * 512:(half + 1) * 512], ps[b][:, :]))
                        e.nop().then_inc(bank_free[b], 1)
                        e.nop().then_inc(fin_copied, 1)

        def att_pe(e, kind, i):
            a_ = A[kind]
            qn, kn, vn, _ = kinds(kind)
            if i < STEPS:
                qb, h = divmod(i, NH)
                if i == 0:
                    if kind == "B":
                        for nm in (qn, kn, vn):
                            tile_taken(e, nm, 0, 2)
                            tile_taken(e, nm, 0, 3)
                    else:
                        e.wait_ge(qk_ready[qn], 4)
                        e.wait_ge(qk_ready[kn], 4)
                r = slice(64 * (h % 2), 64 * (h % 2) + 64)
                n = (qb + 1) * P
                bank = bank_wait(e, ("sc", kind, i))
                e.matmul(bank[:, 0:n], qk1[qn][r, h // 2, qb * P:n], qk1[kn][r, h // 2, 0:n], start=True, stop=True).then_inc(a_["sc_done"], 1)
            j = i - LAG
            if 0 <= j < STEPS:
                bank = bank_wait(e, ("pt", kind, j))
                e.wait_ge(a_["p_ready"], j + 1)
                for c in range(j // NH + 1):
                    mm = e.transpose(bank[:, c * P:(c + 1) * P], work[j % 4][:, c * P:(c + 1) * P], ident[:, :])
                mm.then_inc(a_["tr_done"], 1)
            j = i - LAG - 1
            if 0 <= j < STEPS:
                qb, h = divmod(j, NH)
                if h == 0:
                    bank_wait(e, ("out", kind, qb))
                if j == 0:
                    tile_taken(e, vn, 0, 2)
                    tile_taken(e, vn, 0, 3)
                b, use = USE[("pt", kind, j)]
                e.wait_ge(bank_free[b], use + 1)
                for c in range(qb + 1):
                    mm = e.matmul(ps[7][:, h * HD:(h + 1) * HD], work[4 + j % 2][:, c * P:(c + 1) * P],
                                  vtok[vn][:, c, h * HD:(h + 1) * HD], start=c == 0, stop=c == qb)
                mm.then_inc(a_["pv_done"], 1)
            j = i - LAG - 2
            if j > 0 and j % NH == 0:
                q = j // NH - 1
                bank = bank_wait(e, ("ot", kind, q))
                e.wait_ge(a_["ot_ready"], q + 1)
                for c in range(4):
                    mm = e.transpose(bank[:, c * P:(c + 1) * P], work[6][:, c * P:(c + 1) * P], ident[:, :])
                mm.then_inc(a_["ot_done"], 1)

        @block.tensor
        def _(e):
            def operand(name, k):
                if name.startswith("branch"):
                    y = {"B": yB, "A": yA, "H": yH, "F": yF}[name[-1]]
                    return y[0][:, k, :], y[1][:, k, :]
                if name.startswith("down"):
                    return g_hi[:, k, :], g_lo[:, k, :]
                if name == "pproj":
                    return pT_hi[:, k, :], pT_lo[:, k, :]
                return h_hi[:, k, :], h_lo[:, k, :]

            norm_of = {"qB": 0, "kB": 0, "vB": 0, "qA": 0, "kA": 0, "vA": 0, "gateB": 0, "gateA": 0,
                       "up1": 1, "hq": 2, "hf": 2, "hi": 2, "hg": 2, "fq": 2, "fk": 2, "fv": 2,
                       "gateH": 2, "gateF": 2, "up2": 3, "pgate": 4}

            def activations_ready(name, g, k):
                first = isinstance(g, int) and g == 0
                if not first:
                    return
                if name in norm_of and name in ("qB", "up1", "hf", "up2", "pgate"):
                    e.wait_ge(hlo_ready, norm_of[name] * DC + k + 1)
                elif name in ("out1", "out2"):
                    e.wait_ge(mixlo_ready, (DC if name == "out2" else 0) + k + 1)
                elif name.startswith("down") and k % 2 == 0:
                    e.wait_ge(up_sem["up" + name[-1]]["lo"], k + 2)
                elif name.startswith("branch") and k == 0:
                    if name == "branchH":
                        e.wait_ge(hgs["ylo"], TB)
                    else:
                        e.wait_ge(A[name[-1]]["ylo"], TB)
                elif name == "pproj" and k == 0:
                    e.wait_ge(p_lo, 1)

            def slot(name, g, k, banks, bank_check):
                p = PH[name]
                static = p.slot0 + (g * p.kc if isinstance(g, int) else 0) + k
                pos = static % SPLIT_SLOTS
                activations_ready(name, g, k)
                e.wait_ge(lo_full, g * p.kc + (p.slot0 + k + 1))
                x_hi, x_lo = operand(name, k)
                for n in range(4):
                    if k == 0:
                        bank_check(n)
                    c = slice(n * P, (n + 1) * P)
                    if name in ("vB", "vA", "fv", "hi"):
                        ops = [(x_hi[:, c], w_lo[:, pos, :]), (x_lo[:, c], w_hi[:, pos, :]), (x_hi[:, c], w_hi[:, pos, :])]
                    else:
                        ops = [(w_lo[:, pos, c], x_hi), (w_hi[:, pos, c], x_lo), (w_hi[:, pos, c], x_hi)]
                    for i, (l, r) in enumerate(ops):
                        mm = e.matmul(ps[banks + n][:, :], l, r, start=k == 0 and i == 0, stop=k == p.kc - 1 and i == 2)
                    if k == p.kc - 1:
                        mm.then_inc(tile_done, 1)
                if k < p.kc - 1:
                    mm.then_inc(slot_used, 1)

            sq_n = [0]

            def sum_squares(bank, weights, start, stop):
                n = sq_n[0]
                sq_n[0] += 1
                e.wait_ge(sq_ready, n + 1)
                e.matmul(bank[:, :], weights[:, :], sq_ring[n % 2][:, :], start=start, stop=stop).then_inc(sq_used, 1)

            for x in SCHEDULE:
                what = x[0]
                if what == "start":
                    e.wait_ge(const_ready, 1)
                    e.wait_ge(vec_full, 16 * 19)
                    for i, (n, c) in enumerate(((53, 0), (88, 53), (88, 141))):
                        mm = e.transpose(ps[7][:, c:c + n], vrows[0:n, i, :], ident[0:n, 0:n])
                    mm.then_inc(vec_done, 1)
                    e.wait_ge(x_full, 64)
                    for j in range(DC):
                        if j == 7:
                            e.wait_ge(vec_ready, 1)
                        for tb in range(TB):
                            mm = e.transpose(ps[j][:, tb * P:(tb + 1) * P], xtok[:, tb, j * P:(j + 1) * P], ident[:, :])
                        mm.then_inc(xt_done, 1)
                    e.wait_ge(const_dve, 1)
                elif what == "sumsq":
                    if x[2] == 0:
                        bank_wait(e, ("norm", x[1]))
                    sum_squares(ps[4], mean_d, x[2] == 0, x[2] == DC - 1)
                elif what == "slot":
                    _, name, g, k = x

                    def check(n):
                        prev = previous_group(name, g)
                        if prev is None:
                            e.wait_ge(x_ready, DC)
                        else:
                            tile_taken(e, *prev, n)
                    slot(name, g, k, 0, check)
                elif what == "up":
                    name = x[1]
                    p = PH[name]

                    def group(g, u_):
                        def check(n):
                            if isinstance(g, int) and g == 0:
                                tile_taken(e, *previous_group(name, 0), n)
                            elif isinstance(g, int) and g == 1:
                                b, use = USE[(name, 4 + n)]
                                e.wait_ge(bank_free[b], use)
                            else:
                                tile_taken(e, name, g - 2, n)
                        for k in range(p.kc):
                            slot(name, g, k, 4 * u_, check)

                    up_groups(e, p, group)
                elif what == "scale":
                    sum_squares(bank_wait(e, x), mean_h, True, True)
                elif what == "att":
                    att_pe(e, x[1], x[2])
                elif what == "bias":
                    e.wait_ge(bias_full, 16)
                    e.wait_ge(const_ready, 1)
                    bank = bank_wait(e, x)
                    e.matmul(bank[:, :], reverse[:, :], bias_up[:, x[1], :], start=True, stop=True).then_inc(bias_mm, 1)
                elif x == ("foxf", 0):
                    bank = bank_wait(e, x)
                    e.wait_ge(ff["w_lo"], 1)
                    for tb in range(TB):
                        c = slice(tb * P, (tb + 1) * P)
                        for k in range(DC):
                            for i, (l, r) in enumerate(((h_hi, wf_lo), (h_lo, wf_hi), (h_hi, wf_hi))):
                                mm = e.matmul(bank[:, tb * NH:(tb + 1) * NH], l[:, k, c], r[:, k, :],
                                              start=k == 0 and i == 0, stop=k == DC - 1 and i == 2)
                    mm.then_inc(ff["mm"], 1)
                elif x == ("foxf", 1):
                    bank = bank_wait(e, x)
                    e.wait_ge(ff["logf"], 1)
                    e.wait_ge(const_ready, 2)
                    for tb in range(TB):
                        for t in range(tb + 1):
                            mm = e.matmul(bank[:, tb * NH:(tb + 1) * NH], (tri if t == tb else ones)[:, :],
                                          fx[:, 2, t, :], start=t == 0, stop=t == tb)
                    mm.then_inc(ff["cmm"], 1)
                elif x == ("foxf", 2):
                    bank = bank_wait(e, x)
                    for tb in range(TB):
                        mm = e.transpose(bank[0:NH, tb * P:(tb + 1) * P], ctok[:, tb, :], ident[:, :])
                    mm.then_inc(ff["ct"], 1)
                elif what == "foxc":
                    h = x[1]
                    if h == 0:
                        e.wait_ge(ff["ctsb"], 1)
                    bank = bank_wait(e, x)
                    e.matmul(bank[:, :], ident[0:NH, h:h + 1].to_broadcast([NH, P]), cT[0:NH, :], start=True, stop=True).then_inc(ff["row_mm"], 1)
                elif what == "hg_mm":
                    lev = x[1]
                    if lev < 6:
                        e.wait_ge(hgs["Q"], lev + 1)
                        e.wait_ge(hgs["K"], lev + 1)
                    q_, k_ = (hQ, hK) if lev < 6 else (hq, hk)
                    for h in range(HH):
                        bank = bank_wait(e, ("lev", lev, h))
                        for pr in range(TB):
                            c = slice(pr * P, (pr + 1) * P)
                            mm = e.matmul(bank[:, c], k_[:, h, c], q_[:, h, c], start=True, stop=True)
                        mm.then_inc(hgs["lev_done"], 1)
                elif what == "hg_kt":
                    e.wait_ge(hgs["scale"], 1)
                    for h in range(HH):
                        bank = bank_wait(e, ("kt", h))
                        for pr in range(TB):
                            c = slice(pr * P, (pr + 1) * P)
                            mm = e.transpose(bank[:, c], hK[:, h, c], ident[:, :])
                        mm.then_inc(hgs["kt_done"], 1)
                elif what == "hg_state":
                    c = x[1]
                    pr, r = c // 2, slice(64 * (c % 2), 64 * (c % 2) + 64)
                    bank = bank_wait(e, ("st", c))
                    if c == 0:
                        for h in range(HH):
                            b, use = USE[("kt", h)]
                            e.wait_ge(bank_free[b], use + 1)
                        tile_taken(e, "hi", 0, 2)
                        tile_taken(e, "hi", 0, 3)
                    for h in range(HH):
                        mm = e.matmul(bank[:, h * P:(h + 1) * P], hKt[r, h, pr * P:(pr + 1) * P], hv[r, pr, h * P:(h + 1) * P],
                                      start=True, stop=True)
                    mm.then_inc(hgs["u_done"], 1)
                elif what == "hg_out":
                    if x[1] < TB:
                        pr = x[1]
                        bank = bank_wait(e, ("ho", pr))
                        e.wait_ge(hgs["state"], min(2 * pr + 1, 7))
                        for h in range(HH):
                            v = slice(h * P, (h + 1) * P)
                            e.matmul(bank[:, v], hS[:, h, pr * P:(pr + 1) * P], hv[:, pr, v], start=True, stop=False, skip_group_check=True)
                            for half in range(2):
                                c = 2 * pr + half
                                if c:
                                    mm = e.matmul(bank[64 * half:64 * half + 64, v], hQ[:, h, c * CH:(c + 1) * CH], state[:, c, v],
                                                  start=False, stop=True, skip_group_check=True)
                        mm.then_inc(hgs["o_done"], 1)
                    if x[1] > 0:
                        pr = x[1] - 1
                        bank = bank_wait(e, ("hot", pr))
                        e.wait_ge(hgs["o_tok"], pr + 1)
                        for h in range(HH):
                            mm = e.transpose(bank[:, h * P:(h + 1) * P], work[1][:, h * P:(h + 1) * P], ident[:, :])
                        mm.then_inc(hgs["ot_done"], 1)
                elif what == "pT":
                    e.wait_ge(p_full, 16)
                    for c in range(2):
                        bank = bank_wait(e, ("pT", c))
                        for tb in range(TB):
                            mm = e.transpose(bank[:, tb * P:(tb + 1) * P], ptok[:, tb, c * P:(c + 1) * P], ident[:, :])
                        mm.then_inc(p_done, 1)
                elif what == "finish":
                    for j in range(8):
                        half, tb = j // 4, j % 4
                        e.wait_ge(x_ready, 5 * DC + 4 * half + 4)
                        bank = bank_wait(e, ("fin", j))
                        for c in range(4):
                            mm = e.transpose(bank[:, c * P:(c + 1) * P], xT[:, 4 * half + c, tb * P:(tb + 1) * P], ident[:, :])
                        mm.then_inc(fin_done, 1)



_INS = ['x', 'norm1_g', 'w_in', 'q_norm_g', 'k_norm_g', 'rel_bias', 'w_branch_a', 'w_branch_b', 'w_out',
        'norm2_g', 'w_ffn_up', 'ffn_conv_w', 'ffn_conv_b', 'w_ffn_down', 'p_2', 'norm_mix_g_2', 'w_in_2',
        'hg_lb_logits_2', 'hg_onorm_g_2', 'fox_f_bias_2', 'fox_q_norm_g_2', 'fox_k_norm_g_2',
        'w_branch_a_2', 'w_branch_b_2', 'w_out_2', 'norm_ffn_g_2', 'w_ffn_gate_2', 'w_ffn_up_2',
        'w_ffn_down_2', 'norm_ple_g_2', 'w_ple_gate_2', 'w_ple_proj_2']


def kernel(**inputs):
    import numpy as np
    import concourse.bacc as bacc
    from concourse.bass_utils import run_bass_kernel_spmd

    nc = bacc.Bacc("TRN2", target_bir_lowering=False, num_devices=1, dynamic_dma_scratch_size=1024)
    arrays, aps = {}, {}
    for name in _INS:
        v = np.ascontiguousarray(inputs[name])
        arrays[f"in_{name}"] = v
        aps[name] = nc.dram_tensor(f"in_{name}", v.shape, mybir.dt.from_np(v.dtype), kind="ExternalInput").ap()
    out = nc.dram_tensor("out_x", (1, S, D), F32, kind="ExternalOutput").ap()
    two_block_kernel(nc, aps, out)
    r = run_bass_kernel_spmd(nc, [arrays], core_ids=[0])
    return r.results[0]["out_x"]
```

```python
import concourse.bass as bass
from concourse import mybir
from contextlib import ExitStack

F32 = mybir.dt.float32
F32R = mybir.dt.float32r
U32 = mybir.dt.uint32
ALU = mybir.AluOpType
ACT = mybir.ActivationFunctionType
AX = mybir.AxisListType

P = 128
S = 512
TB = S // P
D = 1024
DC = D // P
FF = 2816
FC = FF // P
NH = 8
HD = 64
HH = 4
CH = 64
NREL = 257
EPS = 1e-6
NEG = -1e30
SPLIT_SLOTS = 8
RAW_SLOTS = 4
LEVELS = (32, 16, 8, 4, 2, 1)
STEPS = TB * NH
ADDED = 6
LAG = 3


class Phase:

    def __init__(self, name, kc, groups):
        self.name, self.kc, self.groups = name, kc, groups


PHASES = [Phase(*a) for a in (
    ("qB", 8, 1), ("kB", 8, 1), ("vB", 8, 1), ("qA", 8, 1), ("kA", 8, 1), ("vA", 8, 1),
    ("gateB", 8, 2), ("branchB", 4, 2), ("gateA", 8, 2), ("branchA", 4, 2), ("out1", 8, 2),
    ("up1", 8, 11), ("down1", 22, 2),
    ("hf", 8, 1), ("hq", 8, 1), ("hi", 8, 1), ("hg", 8, 1), ("fq", 8, 1), ("fk", 8, 1), ("fv", 8, 1),
    ("gateH", 8, 2), ("branchH", 4, 2), ("gateF", 8, 2), ("branchF", 4, 2), ("out2", 8, 2),
    ("up2", 8, 11), ("down2", 22, 2), ("pproj", 2, 2), ("pgate", 8, 2))]
PH = {}
_slot = _group = 0
for _p in PHASES:
    _p.slot0, _p.group0 = _slot, _group
    _slot += _p.kc * _p.groups
    _group += _p.groups
    PH[_p.name] = _p
SLOTS = _slot
OWNER = {name: "adad" for name in ("qB", "kB", "vB", "qA", "kA", "vA", "hi", "fq", "fk", "fv")}
OWNER |= {name: "aaaa" for name in ("gateB", "gateA", "gateH", "gateF", "pgate", "hq", "hf", "hg")}
OWNER |= {name: "dddd" for name in ("branchB", "branchA", "branchH", "branchF", "out1", "out2",
                                    "down1", "down2", "up1")}
OWNER["up2"] = "aadd"
OWNER["pproj"] = "adad"


def taken_before(name, g, who):
    total = 0
    for p in PHASES:
        per = OWNER[p.name].count(who)
        if p.name == name:
            return g * per + total if per else total
        total += per * p.groups
    raise KeyError(name)


def previous_group(name, g):
    if g:
        return name, g - 1
    i = PHASES.index(PH[name])
    return (PHASES[i - 1].name, PHASES[i - 1].groups - 1) if i else None



def first_bank(name, g):
    return 4 if (name, g) in (("down1", 0), ("down2", 0), ("pproj", 1)) else 0


def by_tile(name, g):
    return 4 if name in ("out1", "out2", "down1", "down2", "pgate") and g == 1 else 1


def make_schedule():
    s = []

    def run(names, plan=(), fill=True):
        behind = {}
        for at, step in plan:
            behind.setdefault(at, []).append(step)
        n = 0
        for name in names:
            name, _, only = name.partition(":")
            p = PH[name]
            for g in range(p.groups) if not only else [int(only)]:
                for k in range(p.kc):
                    s.append(("slot", name, g, k))
                    if fill and k < p.kc - by_tile(name, g):
                        s.append(("fill", name, g, k))
                    if k == p.kc - 1 and (by_tile(name, g) == 1 or name == "pgate"):
                        s.append(("take", name, g, 0, 4))
                        if fill:
                            s.append(("fill", name, g, k))
                    s.extend(behind.pop(n, ()))
                    n += 1
        assert not behind, behind

    def attention(kind, first, last):
        room = [min(i, STEPS - 1) // NH + 3 for i in range(STEPS + LAG + 3)]
        return [(first + sum(room[:i]) * (last - first + 1) // sum(room), ("att", kind, i))
                for i in range(len(room))]

    def head_norms(q, k, first, first_k):
        tiles = [(at + n, x, n) for x, at in ((q, first), (k, first_k)) for n in range(4)]
        return sorted([(at + 2, ("scale", x, n)) for at, x, n in tiles]
                      + [(at, ("square", x, n)) for at, x, n in tiles], key=lambda x: x[0])

    def residual(name, norm, plan=(), meanwhile=None):
        run([name + ":0"])
        run([name + ":1"], [(1 + j // 2, (what, norm, j)) for j in range(4) for what in ("x_square", "x_add")]
            + list(plan))
        s.extend([("take", name, 1, 0, 1), ("x_square", norm, 4),
                  ("take", name, 1, 1, 2), ("x_square", norm, 5), ("x_add", norm, 4),
                  ("take", name, 1, 2, 3), ("x_square", norm, 6), ("x_add", norm, 5),
                  ("take", name, 1, 3, 4), ("sumsq", norm, 0), ("x_square", norm, 7),
                  ("sumsq", norm, 6), ("sumsq", norm, 7)] + [("warm", norm)] * (meanwhile is None))
        fills = [("fill", name, 1, k) for k in range(PH[name].kc - by_tile(name, 1), PH[name].kc)]
        s.append(("norm", norm, 0))
        if meanwhile:
            run([meanwhile], fill=False)
            name, _, g = meanwhile.partition(":")
            fills += [("fill", name, int(g), k) for k in range(PH[name].kc)]
        s.extend([*fills[:2], ("norm", norm, 1), *fills[2:]])

    s.append(("start",))
    s.extend([("sumsq", 0, 0), ("vec", 0), ("warm", 0), ("norm", 0, 0), ("prefill", 4), ("prefill", 5),
              ("norm", 0, 1), ("prefill", 6), ("prefill", 7)])
    run(["qB", "kB", "vB", "qA", "kA", "vA", "gateB", "branchB", "gateA"],
        [(16, ("vec", 1))] + attention("B", 22, 48) + head_norms("qA", "kA", 49, 53) + attention("A", 59, 85))
    run(["branchA"])
    residual("out1", 1)
    s.append(("up", "up1"))
    residual("down1", 2, [(4, ("foxw",))])
    levels = []
    for x in range(7):
        levels.append((2 + 3 * x, ("hg_mm", x)))
        if x < 5:
            levels.append((2 + 3 * x, ("hg_prep", x + 1)))
        levels.append((2 + 3 * x, ("hg_merge", x)))
        if x < 5:
            levels.append((2 + 3 * x, ("hg_qk", x + 1)))
    run(["hf", "hq"], [(7, ("hg_decay",)), (15, ("hg_prep", 0)), (15, ("hg_qk", 0))])
    run(["hi", "hg", "fq", "fk", "fv", "gateH", "branchH", "gateF"],
        [(0, ("foxf", 0)), (1, ("foxf", 1)), (5, ("foxf", 2))] + levels
        + [(19 + i, ("hg_scale", i)) for i in range(4)] + [(24, ("hg_kt",))]
        + [(25 + c, ("hg_state", c)) for c in range(7)]
        + [(33 + 2 * p, ("hg_out", p)) for p in range(TB + 1)]
        + head_norms("fq", "fk", 25, 34) + [(42, ("foxc",))]
        + attention("F", 48, 79))
    run(["branchF"])
    residual("out2", 3)
    s.append(("up", "up2"))
    residual("down2", 4, [(4, ("pT",))], "pproj:0")
    run(["pproj:1", "pgate"], [(5 + j, ("xback", j)) for j in range(8)])
    return s


SCHEDULE = make_schedule()


def bank_uses():
    use, count = {}, [0] * 8

    def take(key, bank):
        use[key] = (bank, count[bank])
        count[bank] += 1

    for x in SCHEDULE:
        if x[0] == "start":
            for j in range(4, 8):
                take(("x", j), j)
        elif x[0] in ("vec", "warm"):
            take(x, 5)
        elif x[0] == "sumsq" and x[2] == 0:
            take(("norm", x[1]), 4)
        elif x[0] == "scale":
            take(x, 6)
        elif x[0] == "foxf" and x[1] != 1:
            take(x, 5)
        elif x[0] == "att":
            kind, i = x[1:]
            if i < STEPS:
                take(("sc", kind, i), 4 + i % 2)
            if 0 <= i - LAG < STEPS:
                take(("pt", kind, i - LAG), 6)
            j = i - LAG - 1
            if 0 <= j < STEPS and j % NH == 0:
                take(("out", kind, j // NH), 7)
            j = i - LAG - 2
            if j > 0 and j % NH == 0:
                take(("ot", kind, j // NH - 1), 4 + (i + 1) % 2)
        elif x[0] == "hg_mm":
            for h in range(HH):
                take(("lev", x[1], h), 4 + h)
        elif x[0] == "hg_kt":
            for h in range(HH):
                take(("kt", h), 4 + h)
        elif x[0] == "hg_state":
            take(("st", x[1]), 4 + x[1] % 2)
        elif x[0] == "hg_out":
            if x[1] < TB:
                take(("ho", x[1]), 4 + x[1] % 2)
            if x[1] > 0:
                take(("hot", x[1] - 1), 7)
        elif x[0] == "up":
            for j in range(4, 8):
                use[(x[1], j)] = (j, count[j])
        elif x[0] == "take" and first_bank(x[1], x[2]) == 4:
            for n in range(4):
                take((x[1], n), 4 + n)
        elif x[0] == "pT":
            take(("pT", 0), 5)
            take(("pT", 1), 6)
        elif x[0] == "xback":
            take(x, 4 + (x[1] + 3) % 4)
    return use


USE = bank_uses()


def square_indices():
    index, n = {}, 0
    for x in SCHEDULE:
        if x[0] == "x_square" and x[2] > 0:
            n += 1
            index[("x_add" if x[2] < ADDED else "sumsq", *x[1:])] = n
        elif x[0] == "square":
            n += 1
            index[("scale", *x[1:])] = n
    return index


SQUARE = square_indices()
CONSUMER = {n: step for step, n in SQUARE.items()}
SUMMED = [step for step in SQUARE if step[0] != "x_add"]


def two_block_kernel(nc, a, out):
    ctx = ExitStack()
    with ctx:
        KB = 1024
        base = nc.sbuf_base + 64
        base += -base % 64
        at = [base]

        def place(name, shape, dt=F32, offset=None):
            n = 4
            for d in shape[1:]:
                n *= d
            if offset is None:
                offset = at[0]
                at[0] += n + (-n % 64)
            return nc.alloc_sbuf_tensor_at(name, shape, dt, offset=offset)

        xT = place("xT", [P, DC, S])
        h_hi = place("h_hi", [P, DC, S], F32R)
        h_lo = place("h_lo", [P, DC, S], F32R)
        w_raw = place("w_raw", [P, RAW_SLOTS, S])
        w_hi = place("w_hi", [P, SPLIT_SLOTS, S], F32R)
        w_lo = place("w_lo", [P, SPLIT_SLOTS, S], F32R)
        ident = place("ident", [P, P])
        mean_d = place("mean_d", [P, P])
        mean_h = place("mean_h", [P, P])
        strict = place("strict", [P, P])
        causal = place("causal", [P, P])
        level_mask = place("level_mask", [P, 7, P])
        chunk_start = place("chunk_start", [P, S])
        vec = place("vec", [P, 53 + 176])
        qk_gain = place("qk_gain", [P, 2])
        lb = place("lb", [P, 6, HH])
        mneg = place("mneg", [P, 2, STEPS])
        rsum = place("rsum", [P, 2, STEPS])
        rinv = place("rinv", [P, 2, STEPS])
        fbias = place("fbias", [NH, 1])
        fx = place("fx", [NH, 3, S])
        ctok = place("ctok", [P, TB, NH])
        decay = place("decay", [P, HH, NH])
        xstat = place("xstat", [P, TB])
        hstat = place("hstat", [P, TB, 3, HH])
        wf_raw = place("wf_raw", [P, DC, NH])
        wf_hi = place("wf_hi", [P, DC, NH], F32R)
        wf_lo = place("wf_lo", [P, DC, NH], F32R)
        cT = place("cT", [NH, S])
        U = at[0]
        assert U + 112 * KB <= nc.sbuf_usable_end, (U, nc.sbuf_usable_end)

        def u(name, kb, shape, dt=F32):
            return place(name, shape, dt, offset=U + kb * KB)

        work = [u(f"work{i}", 96 + 2 * i, [P, S]) for i in range(8)]
        sq_ring = [work[6], work[7]]
        sq_sum = work[4]
        xtok = u("xtok", 0, [P, TB, D])
        x_squares = u("x_squares", 48, [P, TB, D])
        vrows = u("vrows", 16, [P, 3, P])
        rb = u("rb", 88, [NH, NREL])
        rb_ext = u("rb_ext", 90, [NH, 640])
        qk1 = {"qB": u("qB", 0, [P, 4, S]), "kB": u("kB", 8, [P, 4, S]), "qA": u("qA", 24, [P, 4, S]),
               "kA": u("kA", 32, [P, 4, S]), "fq": u("fq", 72, [P, 4, S]), "fk": u("fk", 80, [P, 4, S])}
        vtok = {"vB": u("vB", 16, [P, 4, S]), "vA": u("vA", 40, [P, 4, S]),
                "fv": u("fv", 88, [P, 4, S]), "hi": u("hv", 24, [P, 4, S])}
        bias_mask = u("bias_mask", 48, [P, NH, S])
        yB = (u("yB_hi", 64, [P, 4, S], F32R), u("yB_lo", 72, [P, 4, S], F32R))
        yA = (u("yA_hi", 80, [P, 4, S], F32R), u("yA_lo", 88, [P, 4, S], F32R))
        keep = [u(f"keep{i}", 80 + 2 * i, [P, S]) for i in range(2)]
        after = [u(f"after{i}", 84 + 2 * i, [P, S]) for i in range(2)]
        sig_halves = {"gateB": (0, 8), "gateA": (16, 24), "gateH": (56, 64), "gateF": (40, 72), "pgate": (16, 24)}
        sig = {name: [u(f"{name}{i}", kb, [P, 4, S]) for i, kb in enumerate(v)] for name, v in sig_halves.items()}
        g_hi = u("g_hi", 0, [P, FC, S], F32R)
        g_lo = u("g_lo", 44, [P, FC, S], F32R)
        acc = u("acc", 88, [P, 4, S])
        hq = u("hq", 0, [P, HH, S])
        hk = u("hk", 8, [P, HH, S])
        hb = u("hb", 16, [P, HH, S])
        hv = vtok["hi"]
        hgate = u("hgate", 32, [P, HH, S])
        hS = u("hS", 40, [P, HH, S])
        hE = u("hE", 48, [P, HH, S])
        hQ = u("hQ", 56, [P, HH, S])
        hK = u("hK", 64, [P, HH, S])
        state = u("state", 0, [P, NH, S])
        hKt = u("hKt", 16, [P, HH, S])
        yH = (u("yH_hi", 48, [P, 4, S], F32R), u("yH_lo", 16, [P, 4, S], F32R))
        yF = (u("yF_hi", 0, [P, 4, S], F32R), u("yF_lo", 8, [P, 4, S], F32R))
        c_rows = u("c_rows", 24, [P, NH, S])
        ptok = u("ptok", 100, [P, TB, 256])
        pT_hi = u("pT_hi", 88, [P, 2, S], F32R)
        pT_lo = u("pT_lo", 92, [P, 2, S], F32R)
        pproj = u("pproj", 0, [P, 8, S])
        xback = u("xback", 48, [P, 8, S])
        otok = u("otok", 32, [P, 8, S])

        ps = [ctx.enter_context(nc.psum_tensor(f"bank{i}", [P, S], F32)) for i in range(8)]
        bias_dram = nc.dram_tensor("bias_ext", (NH, 640), F32, kind="Internal").ap()
        c_dram = nc.dram_tensor("c_neg", (NH, S), F32, kind="Internal").ap()

        def sem(name):
            return ctx.enter_context(nc.semaphore(name))

        raw_full = [sem(f"raw_full{i}") for i in range(RAW_SLOTS)]
        hi_full, lo_full = sem("hi_full"), sem("lo_full")
        slot_used = sem("slot_used")
        tile_done = sem("tile_done")
        taken = {"a": sem("taken_act"), "d": sem("taken_dve")}
        act_seq, dve_seq, pool_seq = sem("act_seq"), sem("dve_seq"), sem("pool_seq")
        bank_free = {b: sem(f"bank_free{b}") for b in range(4, 8)}
        const_ready = sem("const_ready")
        const_dve = sem("const_dve")
        x_full = [sem(f"x_full{tb}") for tb in range(TB)]
        gain_full = sem("gain_full")
        vec_full, rb_full, bias_full, small_full = (sem(n) for n in (
            "vec_full", "rb_full", "bias_full", "small_full"))
        vec_done, x_odd, rb_ready, scratch_full = (sem(n) for n in (
            "vec_done", "x_odd", "rb_ready", "scratch_full"))
        xt_done = sem("xt_done")
        x_ready = sem("x_ready")
        sq_ready, sq_used = sem("sq_ready"), sem("sq_used")
        added = sem("added")
        diag_ready, x_sums = sem("diag_ready"), sem("x_sums")
        x_mean, rstd_ready = sem("x_mean"), sem("rstd_ready")
        hf_ready, hhi_ready = sem("hf_ready"), sem("hhi_ready")
        hlo_ready = [sem("hlo_even"), sem("hlo_odd")]
        qkrs_ready = sem("qkrs_ready")
        qk_ready = {n: sem(f"{n}_ready") for n in ("qA", "kA", "fq", "fk")}
        A = {kind: {n: sem(f"{n}{kind}") for n in (
            "sc_done", "s_ready", "p_ready", "tr_done", "pv_done", "ot_ready", "ot_done", "yhi", "ylo")}
            for kind in "BAF"}
        A["B"] |= {n: sem(f"{n}B") for n in ("keep_ready", "beta_ready", "after_ready")}
        mix_ready, mixhi_ready, mixlo_ready = sem("mix_ready"), sem("mixhi_ready"), sem("mixlo_ready")
        up_sem = {n: {k: sem(f"{n}_{k}") for k in (
            "first", "conv1", "conv2", "silu", "prod", "hi", "lo")} for n in ("up1", "up2")}
        hgs = {n: sem(f"hg_{n}") for n in (
            "lb", "lb_exp", "fg", "log", "diff", "exp", "Q", "K", "lev_done", "zero", "eb",
            "el", "kt_done", "u_done", "state", "o_done", "o_sq", "o_ms", "o_rs", "o_tok",
            "ot_done", "y", "yhi", "ylo", "scale", "kd")}
        ff = {n: sem(f"fox_{n}") for n in (
            "w_hi", "w_lo", "mm", "x", "l", "c", "ct", "saved", "rows")}
        p_full, p_done, p_hi, p_lo = (sem(n) for n in ("p_full", "p_done", "p_hi", "p_lo"))
        xback_done, xback_ready = sem("xback_done"), sem("xback_ready")
        out_ready, out_full = sem("out_ready"), sem("out_full")

        def gate(name, j):
            return sig[name][j // 4][:, j % 4, :]

        def of_level(lev, t):
            if lev == 6:
                return t
            m = LEVELS[lev]
            return t.rearrange("p (n w) -> p n w", w=2 * m)[:, :, m:]

        def in_query_order(name, n, bank):
            if name != "qA":
                return qk1[name][:, n, :], bank
            return (qk1[name][:, n, :].rearrange("p (b t) -> p b t", t=P)[:, :, ::-1],
                    bank.rearrange("p (b t) -> p b t", t=P))

        def x_out(e, odd, copy):
            for j in (4 + odd, odd, 2 + odd, 6 + odd):
                e.wait_ge(xt_done, j + 1)
                copy(xT[:, j, :], ps[j][:, :])
                if j >= 4:
                    e.nop().then_inc(bank_free[j], 1)

        def h_rest(e, norm, j):
            e.wait_ge(hhi_ready, norm * DC + j + 1)
            e.tensor_tensor(h_lo[:, j, :], work[j % 2][:, :], h_hi[:, j, :].bitcast(F32), ALU.subtract).then_inc(hlo_ready[j % 2], 1)

        def h_done(e, norm, j):
            e.wait_ge(hlo_ready[j % 2], (norm * DC + j) // 2 + 1)

        def kinds(kind):
            return {"B": ("qB", "kB", "vB", yB), "A": ("qA", "kA", "vA", yA), "F": ("fq", "fk", "fv", yF)}[kind]


        def slots_used(e, name, g, k):
            p = PH[name]
            if k == p.kc - 1:
                e.wait_ge(tile_done, (g + (p.group0 + 1)) * 4)
            else:
                before = p.slot0 - p.group0
                e.wait_ge(slot_used, g * (p.kc - 1) + (before + k + 1))

        def tile_ready(e, name, g, n):
            e.wait_ge(tile_done, g * 4 + (PH[name].group0 * 4 + n + 1))

        def tile_taken(e, name, g, n):
            who = OWNER[name][n]
            e.wait_ge(taken[who], taken_before(name, g, who) + (OWNER[name][:n + 1].count(who)))

        def bank_wait(e, key):
            b, n = USE[key]
            if n:
                e.wait_ge(bank_free[b], n)
            return ps[b]

        def source(name, k, cols):
            r = slice(k * P, (k + 1) * P)
            win = {"qA": 0, "kA": 512, "vA": 1024, "qB": 1536, "kB": 2048, "vB": 2560,
                   "gateA": 3072, "gateB": 4096}
            win2 = {"hq": 0, "hf": 512, "hi": 1024, "hg": 1536, "fq": 2048, "fk": 2560, "fv": 3072,
                    "gateH": 3592, "gateF": 4616}
            rest = {"branchA": "w_branch_a", "branchB": "w_branch_b", "out1": "w_out",
                    "down1": "w_ffn_down", "branchH": "w_branch_a_2", "branchF": "w_branch_b_2",
                    "out2": "w_out_2", "down2": "w_ffn_down_2", "pgate": "w_ple_gate_2",
                    "pproj": "w_ple_proj_2"}
            if name == "up1":
                w = a["w_ffn_up"][0].rearrange("k (t c) -> k t c", t=2)
                return [(slice(0, 512), w[r, :, bass.ds(cols * 256, 256)])]
            if name == "up2":
                return [(slice(0, 256), a["w_ffn_gate_2"][0][r, bass.ds(cols * 256, 256)]),
                        (slice(256, 512), a["w_ffn_up_2"][0][r, bass.ds(cols * 256, 256)])]
            if name in win:
                w, c0 = a["w_in"][0], win[name]
            elif name in win2:
                w, c0 = a["w_in_2"][0], win2[name]
            else:
                w, c0 = a[rest[name]][0], 0
            return [(slice(0, 512), w[r, c0 + cols * 512:c0 + (cols + 1) * 512])]

        block = ctx.enter_context(nc.Block())

        @block.sync
        def _(e):
            for tb in range(TB):
                e.dma_start(xtok[:, tb, :], a["x"][0, tb * P:(tb + 1) * P, :]).then_inc(x_full[tb], 16)
            e.dma_start(vrows[0:8, 0, :], a["norm1_g"].rearrange("a (r c) -> (a r) c", c=P)).then_inc(gain_full, 16)

            def small_loads():
                gains = ("norm2_g", "norm_mix_g_2", "norm_ffn_g_2", "norm_ple_g_2")
                for i, n in enumerate(gains, 1):
                    yield e.dma_start(vrows[8 * i:8 * i + 8, 0, :], a[n].rearrange("a (r c) -> (a r) c", c=P)).then_inc(vec_full, 16)
                for i, n in enumerate(("q_norm_g", "k_norm_g", "fox_q_norm_g_2", "fox_k_norm_g_2")):
                    yield e.dma_start(vrows[40 + i:41 + i, 0, :].rearrange("a (t c) -> a t c", t=2),
                                a[n][:, None, :].to_broadcast([1, 2, HD])).then_inc(vec_full, 16)
                yield e.dma_start(vrows[44:45, 0, :], a["hg_onorm_g_2"]).then_inc(vec_full, 16)
                yield e.dma_start(vrows[45:53, 0, :], a["hg_lb_logits_2"].rearrange("a (r c) -> (a r) c", c=P)).then_inc(vec_full, 16)
                cw = a["ffn_conv_w"][0].rearrange("t (r c) -> t r c", c=P)
                for t in range(3):
                    row = 44 * (t % 2)
                    yield e.dma_start(vrows[row:row + 44, 1 + t // 2, :], cw[t]).then_inc(vec_full, 16)
                yield e.dma_start(vrows[44:88, 2, :], a["ffn_conv_b"][0].rearrange("(r c) -> r c", c=P)).then_inc(vec_full, 16)
                yield e.dma_start(rb[:, :], a["rel_bias"][0]).then_inc(rb_full, 16)
                yield e.dma_start(fbias[:, :], a["fox_f_bias_2"].rearrange("a h -> h a")).then_inc(small_full, 16)
                with nc.allow_non_contiguous_dma(reason="eight columns of the fused input projection"):
                    yield e.dma_start(wf_raw[:, :, :], a["w_in_2"][0][:, 3584:3592].rearrange("(k p) c -> p k c", p=P)).then_inc(small_full, 16)

            small = small_loads()

            def load(name, g, k, s):
                pos = (PH[name].slot0 + (g * PH[name].kc if isinstance(g, int) else 0) + k)
                if not (isinstance(g, int) and pos < RAW_SLOTS):
                    e.wait_ge(hi_full, s - (RAW_SLOTS - 1))
                    e.wait_ge(lo_full, s - (RAW_SLOTS - 1))
                pos %= RAW_SLOTS
                parts = source(name, k, g)
                for cols, src in parts:
                    dst = w_raw[:, pos, cols]
                    if name == "up1":
                        dst = dst.rearrange("p (t c) -> p t c", t=2)
                    e.dma_start(dst, src).then_inc(raw_full[pos], 32 // len(parts))

            for i, p in enumerate(PHASES):
                if p.name in ("up1", "up2"):
                    with e.Fori(0, p.groups) as g:
                        for k in range(p.kc):
                            load(p.name, g, k, g * p.kc + (p.slot0 + k))
                else:
                    for g in range(p.groups):
                        for k in range(p.kc):
                            load(p.name, g, k, p.slot0 + g * p.kc + k)
                            if p.name == "kB" or p.name == "vB" or (p.name == "qB" and k >= RAW_SLOTS):
                                next(small, None)
                if p.name == "qA":
                    e.wait_ge(rb_ready, 1)
                    e.dma_start(bias_dram, rb_ext[:, :]).then_inc(scratch_full, 16)
                    e.wait_ge(scratch_full, 16)
                    e.dma_start(bias_mask[:, :, :], bass.AP(bias_dram.tensor, 0, [[1, P], [640, NH], [1, S]])).then_inc(bias_full, 16)
                if p.name == "up2":
                    h_done(e, 3, DC - 2)
                    h_done(e, 3, DC - 1)
                    e.dma_start(ptok[:, :, :], a["p_2"][0, 0].rearrange("(t p) c -> p t c", p=P)).then_inc(p_full, 16)
            for j in range(8):
                half, tb = j // TB, j % TB
                e.wait_ge(out_ready, j + 1)
                e.dma_start(out[0, tb * P:(tb + 1) * P, half * 512:(half + 1) * 512], otok[:, j, :]).then_inc(out_full, 16)
            e.wait_ge(out_full, 2 * TB * 16)

        @block.gpsimd
        def _(e):
            seq = [0]

            def link(ins):
                seq[0] += 1
                ins.then_inc(pool_seq, 1)
                e.wait_ge(pool_seq, seq[0])

            def lo(pos, s):
                e.wait_ge(hi_full, s + 1)
                e.tensor_tensor(w_lo[:, pos % SPLIT_SLOTS, :], w_raw[:, pos % RAW_SLOTS, :],
                                w_hi[:, pos % SPLIT_SLOTS, :].bitcast(F32), ALU.subtract).then_inc(lo_full, 1)

            link(e.memset(ident[:, :], 0.0))
            link(e.affine_select(out=ident[:, :], in_=ident[:, :], compare_op=ALU.not_equal, fill=1.0,
                                 base=0, pattern=[[-1, P]], channel_multiplier=1))
            e.nop().then_inc(const_ready, 1)
            link(e.memset(strict[:, :], 0.0))
            link(e.affine_select(out=strict[:, :], in_=strict[:, :], compare_op=ALU.is_gt, fill=NEG,
                                 base=0, pattern=[[-1, P]], channel_multiplier=1))
            link(e.memset(causal[:, :], 0.0))
            link(e.affine_select(out=causal[:, :], in_=causal[:, :], compare_op=ALU.is_ge, fill=NEG,
                                 base=0, pattern=[[-1, P]], channel_multiplier=1))
            link(e.memset(level_mask[:, :, :], 0.0))
            for level, m in enumerate(LEVELS):
                v = level_mask[:, level, :].rearrange("p (n w) -> p n w", w=2 * m)[:, :, m:]
                n = P // (2 * m)
                link(e.memset(v, 1.0))
                link(e.affine_select(out=v, in_=v, compare_op=ALU.is_ge, fill=0.0, base=0,
                                     pattern=[[-2 * m, n], [0, m]], channel_multiplier=1))
                link(e.affine_select(out=v, in_=v, compare_op=ALU.is_ge, fill=0.0, base=m - 1,
                                     pattern=[[2 * m, n], [0, m]], channel_multiplier=-1))
            link(e.affine_select(out=level_mask[:, 6, :], in_=level_mask[:, 6, :], compare_op=ALU.not_equal,
                                 fill=1.0, base=0, pattern=[[-1, P]], channel_multiplier=1))
            e.nop().then_inc(const_ready, 1)
            for x in SCHEDULE:
                if x[0] == "start":
                    for s in range(RAW_SLOTS):
                        lo(s, s)
                elif x[0] == "prefill":
                    lo(x[1], x[1])
                elif x[0] == "norm":
                    for j in (1, 3) if x[2] == 0 else (5, 7):
                        h_rest(e, x[1], j)
                elif x[0] == "fill":
                    s = PH[x[1]].slot0 + x[2] * PH[x[1]].kc + x[3] + SPLIT_SLOTS
                    if s < SLOTS:
                        lo(s, s)
                elif x[0] == "up":
                    p = PH[x[1]]
                    with e.Fori(0, p.groups) as g:
                        for k in range(p.kc):
                            s = p.slot0 + k + SPLIT_SLOTS
                            lo(s, g * p.kc + s)
                elif x[0] == "att" and x[1] == "B" and 0 <= x[2] - 1 < STEPS:
                    i, n = x[2] - 1, ((x[2] - 1) // NH + 1) * P
                    e.wait_ge(A["B"]["beta_ready"], i + 1)
                    e.wait_ge(A["B"]["after_ready"], i + 1)
                    w = work[i % 4]
                    e.tensor_tensor(w[:, 0:n], w[:, 0:n], after[i % 2][:, 0:n], ALU.mult).then_inc(A["B"]["p_ready"], 1)
                elif x[0] == "hg_decay":
                    e.wait_ge(x_ready, 3 * DC)
                    e.memset(hK[:, :, :], 0.0).then_inc(hgs["zero"], 1)
                elif x[0] == "hg_qk":
                    m = LEVELS[x[1]]
                    k_, e_, o_ = (t[:, :, :].rearrange("p h (n w) -> p (h n) w", w=2 * m)[:, :, 0:m] for t in (hk, hE, hK))
                    e.wait_ge(hgs["zero"], 1)
                    e.wait_ge(hgs["exp"], x[1] + 1)
                    if x[1]:
                        e.wait_ge(hgs["lev_done"], HH * x[1])
                    e.tensor_tensor(o_, k_, e_, ALU.mult).then_inc(hgs["K"], 1)

        def tokens_of(y, kind, qb):
            first = qb * P
            if kind == "A":
                return y[:, :, first + P - 1:(first - 1 if first else None):-1]
            return y[:, :, first:first + P]

        def att_act(e, kind, i):
            a_, ring = A[kind], work[i % 4]
            n = (i // NH + 1) * P
            if i < STEPS and kind == "B":
                e.wait_ge(a_["s_ready"], i + 1)
                if i >= 2:
                    e.wait_ge(a_["after_ready"], i - 1)
                e.activation(keep[i % 2][:, 0:n], ring[:, 0:n], ACT.Sigmoid, scale=-1.0).then_inc(a_["keep_ready"], 1)
                e.activation(ring[:, 0:n], ring[:, 0:n], ACT.Sigmoid).then_inc(a_["beta_ready"], 1)
            elif i < STEPS:
                k = 0 if kind == "A" else 1
                e.wait_ge(a_["s_ready"], i + 1)
                e.activation(ring[:, 0:n], ring[:, 0:n], ACT.Exp, scale=-1.0 if kind == "A" else 1.0,
                             bias=mneg[:, k, i:i + 1], accum_out=rsum[:, k, i:i + 1]).then_inc(a_["p_ready"], 1)
            j = i - LAG - 2
            if j > 0 and j % NH == 0:
                qb = j // NH - 1
                e.wait_ge(a_["ot_done"], qb + 1)
                b, use = USE[("ot", kind, qb)]
                y = kinds(kind)[3]
                e.activation(tokens_of(y[0], kind, qb), ps[b][:, :].rearrange("p (c t) -> p c t", c=4),
                             ACT.Copy).then_inc(a_["yhi"], 1)

        def pt_out(e, kind, j, copy):
            a_ = A[kind]
            n = (j // NH + 1) * P
            e.wait_ge(a_["tr_done"], j + 1)
            if j >= 2:
                e.wait_ge(a_["pv_done"], j - 1)
            b, use = USE[("pt", kind, j)]
            copy(work[4 + j % 2][:, 0:n], ps[b][:, 0:n]).then_inc(bank_free[b], 1)

        def conv_col(tap, tile, half):
            return bass.ds(tile + (53 + 44 * tap + FC * half), 1) if not isinstance(tile, int) else \
                slice(53 + 44 * tap + FC * half + tile, 54 + 44 * tap + FC * half + tile)

        def up_act(e, name, hi):
            p, q = PH[name], up_sem[name]

            def group(g, u_):
                banks = 4 * u_
                for k in range(p.kc):
                    s = p.slot0 + k + SPLIT_SLOTS
                    st = s + (g * p.kc if isinstance(g, int) else 0)
                    hi(st if isinstance(g, int) else s, g * p.kc + s, name, g, k)
                if name == "up1":
                    for n in range(4):
                        tile_ready(e, name, g, n)
                        if not isinstance(g, int) or g > 0:
                            e.wait_ge(q["lo"], g * 2)
                        e.activation(acc[:, n, :], ps[banks + n][:, :], ACT.Identity,
                                     bias=vec[:, conv_col(3, g * 2 + n % 2, n // 2)],
                                     scale=vec[:, conv_col(2, g * 2 + n % 2, n // 2)]).then_inc(q["first"], 1)
                    for n in range(2):
                        e.wait_ge(taken["d"], taken_before(name, g, "d") + n + 1)
                        e.activation(acc[:, n, :], acc[:, n, :], ACT.Silu).then_inc(q["silu"], 1)
                else:
                    for n in range(2):
                        tile_ready(e, name, g, n)
                        if not isinstance(g, int) or g > 0:
                            e.wait_ge(q["lo"], g * 2 - 1 + n)
                        e.activation(acc[:, n, :], ps[banks + n][:, :], ACT.Silu).then_inc(taken["a"], 1)
                for n in range(2):
                    e.wait_ge(q["prod"], g * 2 + n + 1)
                    dst = g_hi[:, bass.ds(g * 2 + n, 1), :].rearrange("p a t -> p (a t)")
                    e.wait_ge(const_ready, 2)
                    e.activation(dst, acc[:, n, :], ACT.Copy).then_inc(q["hi"], 1)

            up_groups(e, p, group)

        def up_groups(e, p, group):
            group(0, 0)
            group(1, 1)
            with e.Fori(1, p.groups // 2) as it:
                group(it * 2, 0)
                group(it * 2 + 1, 1)
            group(p.groups - 1, 0)

        @block.scalar
        def _(e):
            seq = [0]

            def link(ins):
                seq[0] += 1
                ins.then_inc(act_seq, 1)
                e.wait_ge(act_seq, seq[0])

            def hi(pos, s, name=None, g=None, k=None):
                r = pos % RAW_SLOTS
                e.wait_ge(raw_full[r], (s - pos) * (32 // RAW_SLOTS) + 32 * (pos // RAW_SLOTS + 1))
                if name:
                    slots_used(e, name, g, k)
                e.activation(w_hi[:, pos % SPLIT_SLOTS, :], w_raw[:, r, :], ACT.Copy).then_inc(hi_full, 1)

            table = [None]

            def uses(name):
                if table[0] != name:
                    e.preload_act_table_set(name + "_and_others")
                table[0] = name

            sq_n = [0]

            def squares_used(n):
                step = CONSUMER[n]
                if step[0] == "x_add":
                    e.wait_ge(added, step[2] + ADDED * (step[1] - 1) + 1)
                else:
                    e.wait_ge(sq_used, SUMMED.index(step) + 1)

            def square(src):
                n = sq_n[0]
                sq_n[0] += 1
                if n >= 2:
                    squares_used(n - 1)
                e.activation(sq_ring[n % 2][:, :], src, ACT.Square).then_inc(sq_ready, 1)

            for x in SCHEDULE:
                what = x[0]
                if what == "start":
                    uses("natural_log_exp")
                    for tb in range(TB):
                        e.wait_ge(x_full[tb], 16)
                        e.activation(x_squares[:, tb, :], xtok[:, tb, :], ACT.Square, accum_out=xstat[:, tb:tb + 1]).then_inc(x_sums, 1)
                    x_out(e, 1, lambda o, i_: link(e.activation(o, i_, ACT.Copy)))
                    e.nop().then_inc(x_odd, DC // 2)
                    for s in range(RAW_SLOTS):
                        hi(s, s)
                elif what == "prefill":
                    hi(x[1], x[1])
                elif what == "fill":
                    _, name, g, k = x
                    s = PH[name].slot0 + g * PH[name].kc + k + SPLIT_SLOTS
                    if s < SLOTS:
                        hi(s, s, name, g, k)
                elif what == "x_square":
                    _, norm, j = x
                    e.wait_ge(x_ready, norm * DC + j + 1)
                    if j == 0:
                        e.activation(sq_sum[:, :], xT[:, j, :], ACT.Square).then_inc(added, 1)
                    else:
                        square(xT[:, j, :])
                elif what == "norm":
                    if x[2] == 0:
                        uses("natural_log_exp")
                        if x[1]:
                            e.wait_ge(sq_used, SUMMED.index(("sumsq", x[1], DC - 1)) + 1)
                        else:
                            e.wait_ge(x_mean, 1)
                        link(e.activation(work[3][:, :], ps[4][:, :], ACT.Ln, bias=EPS))
                        e.nop().then_inc(bank_free[4], 1)
                        e.activation(work[2][:, :], work[3][:, :], ACT.Exp, scale=-0.5).then_inc(rstd_ready, 1)
                    for j in range(4 * x[2], 4 * x[2] + 4):
                        e.wait_ge(hf_ready, x[1] * DC + j + 1)
                        e.activation(h_hi[:, j, :], work[j % 2][:, :], ACT.Copy).then_inc(hhi_ready, 1)
                elif what == "take":
                    _, name, g, first, end = x
                    if name in sig or name == "hf":
                        uses("sigmoid")
                    elif name in ("hq", "hg"):
                        uses("silu")
                    for n in range(first, end):
                        if OWNER[name][n] != "a":
                            continue
                        tile_ready(e, name, g, n)
                        bank = ps[first_bank(name, g) + n][:, :]
                        if name in ("qB", "kB", "qA", "kA", "fq", "fk"):
                            o, i_ = in_query_order(name, n, bank)
                            e.activation(o, i_, ACT.Copy, scale=HD ** -0.5 if name == "qB" else 1.0).then_inc(taken["a"], 1)
                        elif name in vtok:
                            e.activation(vtok[name][:, n, :], bank, ACT.Copy).then_inc(taken["a"], 1)
                        elif name in sig:
                            e.activation(gate(name, 4 * g + n), bank, ACT.Sigmoid).then_inc(taken["a"], 1)
                        elif name in ("hq", "hg"):
                            dst = hq if name == "hq" else hgate
                            e.activation(dst[:, n, :], bank, ACT.Silu).then_inc(taken["a"], 1)
                        elif name == "hf":
                            e.activation(hk[:, n, :], bank, ACT.Sigmoid).then_inc(taken["a"], 1)
                        elif name == "pproj":
                            link(e.activation(pproj[:, 4 * g + n, :], bank, ACT.Copy))
                            e.nop().then_inc(taken["a"], 1)
                            if first_bank(name, g) == 4:
                                e.nop().then_inc(bank_free[4 + n], 1)
                    if name in ("branchA", "branchF"):
                        for n in range(4):
                            j = 4 * g + n
                            e.wait_ge(mix_ready, (DC if name == "branchF" else 0) + j + 1)
                            e.activation(h_hi[:, j, :], gate("gateA" if name == "branchA" else "gateF", j), ACT.Copy).then_inc(mixhi_ready, 1)
                elif what == "square":
                    tile_taken(e, x[1], 0, x[2])
                    square(qk1[x[1]][:, x[2], :])
                elif what == "scale":
                    _, name, n = x
                    uses("natural_log_exp")
                    b, use = USE[x]
                    count = {"qA": 0, "kA": 4, "fq": 8, "fk": 12}[name] + n
                    t = work[4 + n % 2]
                    if count >= 2:
                        prev = [(m, c) for m in ("qA", "kA", "fq", "fk") for c in range(4)][count - 2]
                        e.wait_ge(qk_ready[prev[0]], prev[1] + 1)
                    e.wait_ge(sq_used, SUMMED.index(x) + 1)
                    link(e.activation(t[:, :], ps[b][:, :], ACT.Ln, bias=EPS))
                    e.nop().then_inc(bank_free[b], 1)
                    e.activation(t[:, :], t[:, :], ACT.Exp, scale=-0.5).then_inc(qkrs_ready, 1)
                elif what == "att":
                    uses("sigmoid" if x[1] == "B" else "natural_log_exp")
                    att_act(e, x[1], x[2])
                elif what == "up":
                    uses("silu")
                    up_act(e, x[1], hi)
                elif what == "foxw":
                    e.wait_ge(small_full, 32)
                    e.activation(wf_hi[:, :, :], wf_raw[:, :, :], ACT.Copy).then_inc(ff["w_hi"], 1)
                elif x == ("foxf", 1):
                    uses("natural_log_exp")
                    e.wait_ge(ff["x"], 1)
                    link(e.activation(fx[:, 1, :], fx[:, 1, :], ACT.Exp))
                    e.activation(fx[:, 1, :], fx[:, 1, :], ACT.Ln, bias=1.0).then_inc(ff["l"], 1)
                elif x == ("foxf", 2):
                    e.wait_ge(ff["c"], 1)
                    e.dma_start(c_dram, cT[:, :]).then_inc(ff["saved"], 16)
                elif what == "foxc":
                    e.wait_ge(ff["saved"], 16)
                    e.wait_ge(hgs["ylo"], TB)
                    e.dma_start(c_rows[:, :, :], bass.AP(c_dram.tensor, 0, [[0, P], [S, NH], [1, S]])).then_inc(ff["rows"], 16)
                elif what == "hg_decay":
                    uses("natural_log_exp")
                    e.wait_ge(hgs["lb"], 1)
                    e.activation(lb[:, 1:3, :], lb[:, 1:3, :], ACT.Exp).then_inc(hgs["lb_exp"], 1)
                    e.wait_ge(hgs["fg"], 1)
                    e.activation(hE[:, :, :], hE[:, :, :], ACT.Ln).then_inc(hgs["log"], 1)
                elif what == "hg_prep":
                    uses("natural_log_exp")
                    e.wait_ge(hgs["diff"], x[1] + 1)
                    e.activation(hE[:, :, :], hE[:, :, :], ACT.Exp).then_inc(hgs["exp"], 1)
                elif what == "hg_scale" and x[1] == 0:
                    uses("natural_log_exp")
                    e.wait_ge(hgs["K"], 6)
                    e.wait_ge(hgs["Q"], 6)
                    e.activation(hE[:, :, :], hb[:, :, :], ACT.Exp).then_inc(hgs["eb"], 1)
                elif what == "hg_scale" and x[1] == 1:
                    e.wait_ge(hgs["kd"], 1)
                    e.activation(hK[:, :, :], hK[:, :, :], ACT.Exp).then_inc(hgs["el"], 1)
                elif what == "hg_kt":
                    for h in range(HH):
                        e.wait_ge(hgs["kt_done"], h + 1)
                        b, use = USE[("kt", h)]
                        e.activation(hKt[:, h, :], ps[b][:, :], ACT.Copy).then_inc(bank_free[b], 1)
                elif what == "hg_out":
                    if x[1] < TB:
                        uses("natural_log_exp")
                        pr = x[1]
                        b, use = USE[("ho", pr)]
                        e.wait_ge(hgs["o_done"], pr + 1)
                        if pr:
                            e.wait_ge(hgs["o_ms"], pr)
                        e.activation(work[0][:, :], ps[b][:, :], ACT.Square).then_inc(hgs["o_sq"], 1)
                        e.wait_ge(hgs["o_ms"], pr + 1)
                        link(e.activation(hstat[:, pr, 1, :], hstat[:, pr, 0, :], ACT.Ln, bias=EPS, scale=1.0 / P))
                        e.activation(hstat[:, pr, 2, :], hstat[:, pr, 1, :], ACT.Exp, scale=-0.5).then_inc(hgs["o_rs"], 1)
                    if x[1] > 0:
                        pr = x[1] - 1
                        e.wait_ge(hgs["y"], pr + 1)
                        e.activation(yH[0][:, :, pr * P:(pr + 1) * P], work[2 + pr % 2][:, :].rearrange("p (h t) -> p h t", h=HH),
                                     ACT.Copy).then_inc(hgs["yhi"], 1)
                elif what == "pT":
                    for c in range(2):
                        b, use = USE[("pT", c)]
                        e.wait_ge(p_done, c + 1)
                        e.activation(pT_hi[:, c, :], ps[b][:, :], ACT.Copy).then_inc(p_hi, 1)

        def take_dve(e, name, g, first, end, link):
            if name == "pgate":
                for n in range(4):
                    j = 4 * g + n
                    tile_taken(e, "pgate", g, n)
                    tile_taken(e, "pproj", g, n)
                    e.wait_ge(xback_ready, j + 1)
                    link(e.tensor_tensor(otok[:, j, :], pproj[:, j, :], gate("pgate", j), ALU.mult))
                    e.tensor_tensor(otok[:, j, :], otok[:, j, :], xback[:, j, :], ALU.add).then_inc(out_ready, 1)
                return
            for n in range(first, end):
                if OWNER[name][n] != "d":
                    continue
                tile_ready(e, name, g, n)
                j = 4 * g + n
                bank = ps[first_bank(name, g) + n][:, :]
                if name in ("qB", "kB", "qA", "kA", "fq", "fk"):
                    o, i_ = in_query_order(name, n, bank)
                    e.tensor_scalar(o, i_, HD ** -0.5 if name == "qB" else 1.0, None,
                                    ALU.mult).then_inc(taken["d"], 1)
                elif name in vtok:
                    e.tensor_copy(vtok[name][:, n, :], ps[n][:, :]).then_inc(taken["d"], 1)
                elif name == "pproj":
                    link(e.tensor_copy(pproj[:, j, :], bank))
                    e.nop().then_inc(taken["d"], 1)
                    if first_bank(name, g) == 4:
                        e.nop().then_inc(bank_free[4 + n], 1)
                elif name in ("branchB", "branchH"):
                    t = gate("gate" + name[-1], j)
                    tile_taken(e, "gate" + name[-1], g, n)
                    e.tensor_tensor(t, ps[n][:, :], t, ALU.mult).then_inc(taken["d"], 1)
                elif name in ("branchA", "branchF"):
                    first, second = ("gateB", "gateA") if name == "branchA" else ("gateH", "gateF")
                    t = gate(second, j)
                    tile_taken(e, second, g, n)
                    e.tensor_tensor(t, ps[n][:, :], t, ALU.mult).then_inc(taken["d"], 1)
                    e.wait_ge(taken["d"], taken_before(name, g, "d") + n + 1)
                    e.tensor_tensor(t, t, gate(first, j), ALU.add).then_inc(mix_ready, 1)
                elif name in ("out1", "out2", "down1", "down2"):
                    k = {"out1": 1, "down1": 2, "out2": 3, "down2": 4}[name]
                    e.tensor_tensor(xT[:, j, :], bank, xT[:, j, :], ALU.add).then_inc(x_ready, 1)
                    e.wait_ge(x_ready, k * DC + j + 1)
                    e.nop().then_inc(taken["d"], 1)
                    if first_bank(name, g) == 4:
                        e.nop().then_inc(bank_free[4 + n], 1)
            if name in ("branchA", "branchF"):
                for n in range(4):
                    j = 4 * g + n
                    e.wait_ge(mixhi_ready, (DC if name == "branchF" else 0) + j + 1)
                    e.tensor_tensor(h_lo[:, j, :], gate("gateA" if name == "branchA" else "gateF", j),
                                    h_hi[:, j, :].bitcast(F32), ALU.subtract).then_inc(mixlo_ready, 1)

        def att_dve(e, kind, i, link):
            a_, ring = A[kind], work[i % 4]
            qb, h = divmod(i, NH)
            n = (qb + 1) * P
            j = i - LAG
            if 0 <= j < STEPS:
                pt_out(e, kind, j, lambda o, s: e.tensor_copy(o, s))
            j = i - 1
            if kind == "B" and 0 <= j < STEPS:
                m = (j // NH + 1) * P
                e.wait_ge(a_["keep_ready"], j + 1)
                if j >= 2:
                    e.wait_ge(a_["p_ready"], j - 1)
                k_, o_ = keep[j % 2], after[j % 2]
                link(e.memset(o_[:, m - 1:m], 1.0))
                rev = lambda t, lo_, hi_: t[:, hi_ - 1:(lo_ - 1 if lo_ else None):-1]
                e.tensor_tensor_scan(rev(o_, 0, m - 1), rev(k_, 1, m), rev(k_, 1, m), 1.0,
                                     ALU.mult, ALU.bypass).then_inc(a_["after_ready"], 1)
            if i < STEPS:
                e.wait_ge(a_["sc_done"], i + 1)
                if i >= 4:
                    e.wait_ge(a_["tr_done"], i - 3)
                b, use = USE[("sc", kind, i)]
                if kind == "B":
                    if qb:
                        e.tensor_copy(ring[:, 0:n - P], ps[b][:, 0:n - P])
                    link(e.tensor_tensor(ring[:, n - P:n], ps[b][:, n - P:n], strict[:, :], ALU.add))
                    e.nop().then_inc(bank_free[b], 1)
                    e.nop().then_inc(a_["s_ready"], 1)
                elif kind == "A":
                    if i == 0:
                        e.wait_ge(bias_full, 16)
                        link(e.tensor_scalar(bias_mask[64:128, :, S - 64:S], bias_mask[64:128, :, S - 64:S], NEG, None, ALU.add))
                    link(e.tensor_tensor_reduce(out=ring[:, 0:n], in0=ps[b][:, 0:n], in1=bias_mask[:, h, S - n:S],
                                                scale=-1.0, scalar=3e38, op0=ALU.add, op1=ALU.min,
                                                accum_out=mneg[:, 0, i:i + 1]))
                    e.nop().then_inc(bank_free[b], 1)
                    e.nop().then_inc(a_["s_ready"], 1)
                else:
                    if i == 0:
                        e.wait_ge(ff["rows"], 16)
                    link(e.scalar_tensor_tensor(out=ring[:, 0:n], in0=ps[b][:, 0:n], scalar=ctok[:, qb, h:h + 1],
                                                in1=c_rows[:, h, 0:n], op0=ALU.add, op1=ALU.add))
                    e.nop().then_inc(bank_free[b], 1)
                    link(e.tensor_tensor(ring[:, n - P:n], ring[:, n - P:n], causal[:, :], ALU.add))
                    e.tensor_reduce(mneg[:, 1, i:i + 1], ring[:, 0:n], axis=AX.X, op=ALU.max, negate=True).then_inc(a_["s_ready"], 1)
            j = i - LAG - 1
            if 0 <= j < STEPS and j % NH == NH - 1:
                q = j // NH
                e.wait_ge(a_["pv_done"], j + 1)
                if q:
                    e.wait_ge(a_["ot_done"], q)
                b, use = USE[("out", kind, q)]
                o3 = work[6][:, :].rearrange("p (h d) -> p h d", h=NH)
                p3 = ps[b][:, :].rearrange("p (h d) -> p h d", h=NH)
                if kind == "B":
                    link(e.tensor_copy(o3, p3))
                else:
                    k = 0 if kind == "A" else 1
                    c = slice(q * NH, (q + 1) * NH)
                    link(e.reciprocal(rinv[:, k, c], rsum[:, k, c]))
                    link(e.tensor_tensor(o3, p3, rinv[:, k, c][:, :, None].to_broadcast([P, NH, HD]), ALU.mult))
                e.nop().then_inc(bank_free[b], 1)
                e.nop().then_inc(a_["ot_ready"], 1)
            j = i - LAG - 2
            if j > 0 and j % NH == 0:
                q = j // NH - 1
                e.wait_ge(a_["yhi"], q + 1)
                b, use = USE[("ot", kind, q)]
                y = kinds(kind)[3]
                link(e.tensor_tensor(tokens_of(y[1], kind, q), ps[b][:, :].rearrange("p (c t) -> p c t", c=4),
                                     tokens_of(y[0], kind, q).bitcast(F32), ALU.subtract))
                e.nop().then_inc(bank_free[b], 1)
                e.nop().then_inc(a_["ylo"], 1)

        def up_dve(e, name):
            p, q = PH[name], up_sem[name]

            def group(g, u_):
                banks = 4 * u_
                if name == "up1":
                    for n in range(4):
                        col = g * 2 + n % 2
                        e.wait_ge(q["first"], g * 4 + n + 1)
                        for shift, tap, s_ in ((1, 1, q["conv1"]), (2, 0, taken["d"])):
                            if shift == 2:
                                e.wait_ge(q["conv1"], g * 4 + n + 1)
                            o = acc[:, n, shift:S]
                            e.scalar_tensor_tensor(out=o, in0=ps[banks + n][:, 0:S - shift],
                                                   scalar=vec[:, conv_col(tap, col, n // 2)], in1=o,
                                                   op0=ALU.mult, op1=ALU.add).then_inc(s_, 1)
                    for n in range(2):
                        e.wait_ge(taken["d"], taken_before(name, g, "d") + n + 3)
                        e.wait_ge(q["silu"], g * 2 + n + 1)
                        e.tensor_tensor(acc[:, n, :], acc[:, n, :], acc[:, n + 2, :], ALU.mult).then_inc(q["prod"], 1)
                else:
                    for n in range(2):
                        tile_ready(e, name, g, n + 2)
                        e.wait_ge(taken["a"], taken_before(name, g, "a") + n + 1)
                        e.tensor_tensor(acc[:, n, :], ps[banks + 2 + n][:, :], acc[:, n, :], ALU.mult).then_inc(taken["d"], 1)
                        e.wait_ge(taken["d"], taken_before(name, g, "d") + n + 1)
                        e.nop().then_inc(q["prod"], 1)
                for n in range(2):
                    e.wait_ge(q["hi"], g * 2 + n + 1)
                    tile = bass.ds(g * 2 + n, 1)
                    dst = g_lo[:, tile, :].rearrange("p a t -> p (a t)")
                    src = g_hi[:, tile, :].rearrange("p a t -> p (a t)").bitcast(F32)
                    e.tensor_tensor(dst, acc[:, n, :], src, ALU.subtract).then_inc(q["lo"], 1)

            up_groups(e, p, group)

        def hg_dve(e, x, link):
            blocks = lambda t, w: t[:, :, :].rearrange("p h (n w) -> p (h n) w", w=w)
            if x[0] == "hg_decay":
                e.wait_ge(hgs["lb_exp"], 1)
                link(e.tensor_tensor(lb[:, 3, :], lb[:, 1, :], lb[:, 2, :], ALU.add))
                link(e.reciprocal(lb[:, 3, :], lb[:, 3, :]))
                link(e.tensor_tensor(lb[:, 4, :], lb[:, 1, :], lb[:, 3, :], ALU.mult))
                link(e.tensor_scalar(lb[:, 5, :], lb[:, 4, :], -1.0, 1.0, ALU.mult, ALU.add))
                tile_taken(e, "hf", 0, 3)
                for h in range(HH):
                    ins = e.tensor_scalar(hE[:, h, :], hk[:, h, :], lb[:, 5, h:h + 1], lb[:, 4, h:h + 1], ALU.mult, ALU.add)
                link(ins)
                link(e.tensor_scalar(hk[:, :, :], hE[:, :, :], -1.0, 1.0, ALU.mult, ALU.add))
                e.nop().then_inc(hgs["fg"], 1)
                e.wait_ge(hgs["log"], 1)
                for h in range(HH):
                    ins = e.tensor_tensor_scan(hb[:, h, :], chunk_start[:, :], hE[:, h, :], 0.0, ALU.mult, ALU.add)
                link(ins)
                link(e.memset(hS[:, :, :], 0.0))
            elif x[0] == "hg_prep":
                lev, m = x[1], LEVELS[x[1]]
                b_, e_ = blocks(hb, 2 * m), blocks(hE, 2 * m)
                mid = b_[:, :, m - 1:m].to_broadcast([P, HH * S // (2 * m), m])
                if lev:
                    e.wait_ge(hgs["K"], lev)
                    e.wait_ge(hgs["Q"], lev)
                e.tensor_tensor(e_[:, :, 0:m], mid, b_[:, :, 0:m], ALU.subtract)
                link(e.tensor_tensor(e_[:, :, m:], b_[:, :, m:], mid, ALU.subtract))
                e.nop().then_inc(hgs["diff"], 1)
            elif x[0] == "hg_qk":
                lev, m = x[1], LEVELS[x[1]]
                q_, e_, Q_ = (blocks(t, 2 * m) for t in (hq, hE, hQ))
                e.wait_ge(hgs["exp"], lev + 1)
                if lev:
                    e.wait_ge(hgs["lev_done"], HH * lev)
                else:
                    e.wait_ge(hgs["zero"], 1)
                    tile_taken(e, "hq", 0, 3)
                e.tensor_tensor(Q_[:, :, m:], q_[:, :, m:], e_[:, :, m:], ALU.mult).then_inc(hgs["Q"], 1)
            elif x[0] == "hg_merge":
                lev = x[1]
                for h in range(HH):
                    b, use = USE[("lev", lev, h)]
                    e.wait_ge(hgs["lev_done"], HH * lev + h + 1)
                    e.wait_ge(const_ready, 2)
                    mask = of_level(lev, level_mask[:, lev, :].bitcast(U32))[:, None]
                    o, new = (of_level(lev, t).rearrange("p (b n) w -> p b n w", b=TB) if lev < 6 else
                              t.rearrange("p (b t) -> p b t", b=TB) for t in (hS[:, h, :], ps[b][:, :]))
                    e.copy_predicated(o, mask.to_broadcast(list(o.shape)), new).then_inc(bank_free[b], 1)
            elif x[0] == "hg_scale":
                last = lambda t: blocks(t, CH)[:, :, CH - 1:CH]
                if x[1] == 0:
                    e.wait_ge(hgs["lev_done"], HH * 6)
                    e.tensor_tensor(blocks(hK, CH), last(hb).to_broadcast([P, HH * S // CH, CH]), blocks(hb, CH), ALU.subtract).then_inc(hgs["kd"], 1)
                elif x[1] == 1:
                    e.wait_ge(hgs["eb"], 1)
                    e.tensor_tensor(hQ[:, :, :], hq[:, :, :], hE[:, :, :], ALU.mult).then_inc(hgs["scale"], 1)
                elif x[1] == 2:
                    e.tensor_copy(decay[:, :, :].rearrange("p h c -> p (h c)")[:, :, None], last(hE)).then_inc(hgs["scale"], 1)
                else:
                    e.wait_ge(hgs["el"], 1)
                    e.tensor_tensor(hK[:, :, :], hK[:, :, :], hk[:, :, :], ALU.mult).then_inc(hgs["scale"], 1)
            elif x[0] == "hg_state":
                c = x[1]
                b, use = USE[("st", c)]
                e.wait_ge(hgs["u_done"], c + 1)
                if c == 0:
                    link(e.tensor_copy(state[:, 1, :], ps[b][:, :]))
                else:
                    for h in range(HH):
                        v = slice(h * P, (h + 1) * P)
                        ins = e.scalar_tensor_tensor(out=state[:, c + 1, v], in0=state[:, c, v], scalar=decay[:, h, c:c + 1],
                                                     in1=ps[b][:, v], op0=ALU.mult, op1=ALU.add)
                    link(ins)
                e.nop().then_inc(bank_free[b], 1)
                e.nop().then_inc(hgs["state"], 1)
            elif x[0] == "hg_out":
                if x[1] < TB:
                    pr = x[1]
                    b, use = USE[("ho", pr)]
                    e.wait_ge(hgs["o_sq"], pr + 1)
                    e.tensor_reduce(hstat[:, pr, 0, :], work[0][:, :].rearrange("p (h v) -> p h v", h=HH), axis=AX.X, op=ALU.add).then_inc(hgs["o_ms"], 1)
                    e.wait_ge(hgs["o_rs"], pr + 1)
                    if pr:
                        e.wait_ge(hgs["ot_done"], pr)
                    link(e.tensor_tensor(work[1][:, :].rearrange("p (h v) -> p h v", h=HH), ps[b][:, :].rearrange("p (h v) -> p h v", h=HH),
                                         hstat[:, pr, 2, :][:, :, None].to_broadcast([P, HH, P]), ALU.mult))
                    e.nop().then_inc(bank_free[b], 1)
                    e.nop().then_inc(hgs["o_tok"], 1)
                if x[1] > 0:
                    pr = x[1] - 1
                    b, use = USE[("hot", pr)]
                    e.wait_ge(hgs["ot_done"], pr + 1)
                    tile_taken(e, "hg", 0, 3)
                    c = slice(pr * P, (pr + 1) * P)
                    w3 = work[2 + pr % 2][:, :].rearrange("p (h t) -> p h t", h=HH)
                    link(e.scalar_tensor_tensor(out=w3, in0=ps[b][:, :].rearrange("p (h t) -> p h t", h=HH), scalar=vec[:, 44:45],
                                                in1=hgate[:, :, c], op0=ALU.mult, op1=ALU.mult))
                    e.nop().then_inc(bank_free[b], 1)
                    e.nop().then_inc(hgs["y"], 1)
                    e.wait_ge(hgs["yhi"], pr + 1)
                    e.tensor_tensor(yH[1][:, :, c], w3, yH[0][:, :, c].bitcast(F32), ALU.subtract).then_inc(hgs["ylo"], 1)

        @block.vector
        def _(e):
            seq = [0]

            def link(ins):
                seq[0] += 1
                ins.then_inc(dve_seq, 1)
                e.wait_ge(dve_seq, seq[0])

            for x in SCHEDULE:
                what = x[0]
                if what == "start":
                    e.memset(mean_d[:, :], 1.0 / D)
                    link(e.memset(mean_h[:, :], 0.0))
                    e.memset(mean_h[0:64, 0:64], 1.0 / HD)
                    e.memset(mean_h[64:128, 64:128], 1.0 / HD)
                    link(e.memset(chunk_start[:, :], 1.0))
                    link(e.memset(chunk_start[:, :].rearrange("p (n w) -> p n w", w=CH)[:, :, 0:1], 0.0))
                    e.nop().then_inc(const_dve, 1)
                    e.wait_ge(const_ready, 1)
                    for tb in range(TB):
                        e.wait_ge(x_sums, tb + 1)
                        ins = e.tensor_scalar(work[7][:, tb * P:(tb + 1) * P], ident[:, :], xstat[:, tb:tb + 1], None, ALU.mult)
                    ins.then_inc(diag_ready, 1)
                    x_out(e, 0, lambda o, i_: link(e.tensor_copy(o, i_)))
                    e.wait_ge(x_odd, DC // 2)
                    e.nop().then_inc(x_ready, DC)
                elif what == "vec":
                    b, use = USE[x]
                    c = (slice(0, 8), slice(8, 229))[x[1]]
                    e.wait_ge(vec_done, x[1] + 1)
                    link(e.tensor_copy(vec[:, c], ps[b][:, c]))
                    e.nop().then_inc(bank_free[b], 1)
                    if x[1] == 0:
                        continue
                    e.wait_ge(rb_full, 16)
                    e.tensor_copy(rb_ext[:, 0:383], rb[:, 256:257].to_broadcast([NH, 383]))
                    link(e.tensor_copy(rb_ext[:, 383:639], rb[:, 256:0:-1]))
                    link(e.memset(rb_ext[:, 639:640], 0.0))
                    e.nop().then_inc(rb_ready, 1)
                    e.tensor_scalar(qk_gain[:, 0:1], vec[:, 40:41], HD ** -0.5, None, ALU.mult)
                    e.tensor_scalar(qk_gain[:, 1:2], vec[:, 42:43], HD ** -0.5, None, ALU.mult)
                    link(e.tensor_tensor(lb[:, 0, :], vec[:, 45:49], vec[:, 49:53], ALU.max))
                    e.tensor_tensor(lb[:, 1, :], vec[:, 45:49], lb[:, 0, :], ALU.subtract)
                    e.tensor_tensor(lb[:, 2, :], vec[:, 49:53], lb[:, 0, :], ALU.subtract).then_inc(hgs["lb"], 1)
                elif what == "norm":
                    if x[2] == 0:
                        e.wait_ge(rstd_ready, x[1] + 1)
                    gain = 8 * x[1]

                    def scaled(j):
                        if j >= 2:
                            h_done(e, x[1], j - 2)
                        e.scalar_tensor_tensor(out=work[j % 2][:, :], in0=xT[:, j, :], scalar=vec[:, gain + j:gain + j + 1],
                                               in1=work[2][:, :], op0=ALU.mult, op1=ALU.mult).then_inc(hf_ready, 1)
                    if x[2] == 0:
                        scaled(0)
                    for j in range(4 * x[2], 4 * x[2] + 4):
                        if j + 1 < DC:
                            scaled(j + 1)
                        if j % 2 == 0:
                            h_rest(e, x[1], j)
                elif what == "x_add" and x[2] > 0:
                    e.wait_ge(added, x[2] + ADDED * (x[1] - 1))
                    e.wait_ge(sq_ready, SQUARE[x])
                    e.tensor_tensor(sq_sum[:, :], sq_sum[:, :], sq_ring[(SQUARE[x] - 1) % 2][:, :], ALU.add).then_inc(added, 1)
                elif what == "take":
                    take_dve(e, *x[1:], link)
                elif what == "scale":
                    _, name, n = x
                    count = {"qA": 0, "kA": 4, "fq": 8, "fk": 12}[name] + n
                    e.wait_ge(qkrs_ready, count + 1)
                    t = qk1[name][:, n, :]
                    g = {"qA": qk_gain[:, 0:1], "kA": vec[:, 41:42], "fq": qk_gain[:, 1:2], "fk": vec[:, 43:44]}[name]
                    e.scalar_tensor_tensor(out=t, in0=t, scalar=g, in1=work[4 + n % 2][:, :], op0=ALU.mult, op1=ALU.mult).then_inc(qk_ready[name], 1)
                elif what == "att":
                    att_dve(e, x[1], x[2], link)
                elif what == "up":
                    up_dve(e, x[1])
                elif what == "foxw":
                    e.wait_ge(ff["w_hi"], 1)
                    e.tensor_tensor(wf_lo[:, :, :], wf_raw[:, :, :], wf_hi[:, :, :].bitcast(F32), ALU.subtract).then_inc(ff["w_lo"], 1)
                elif x == ("foxf", 1):
                    e.wait_ge(ff["mm"], 1)
                    e.wait_ge(small_full, 32)
                    b, use = USE[("foxf", 0)]
                    link(e.tensor_scalar(fx[:, 0, :], ps[b][0:NH, :], fbias[:, 0:1], None, ALU.add))
                    e.nop().then_inc(bank_free[b], 1)
                    e.scalar_tensor_tensor(out=fx[:, 1, :], in0=fx[:, 0, :], scalar=-1.0, in1=fx[:, 0, :],
                                           op0=ALU.mult, op1=ALU.min).then_inc(ff["x"], 1)
                    e.wait_ge(ff["l"], 1)
                    link(e.scalar_tensor_tensor(out=fx[:, 1, :], in0=fx[:, 0, :], scalar=0.0, in1=fx[:, 1, :],
                                                op0=ALU.min, op1=ALU.subtract))
                    link(e.tensor_tensor_scan(fx[:, 2, :], fx[:, 1, :], fx[:, 1, :], 0.0, ALU.add, ALU.bypass))
                    e.tensor_scalar(cT[:, :], fx[:, 2, :], -1.0, None, ALU.mult).then_inc(ff["c"], 1)
                elif x == ("foxf", 2):
                    e.wait_ge(ff["ct"], 1)
                    b, use = USE[x]
                    link(e.tensor_copy(ctok[:, :, :], ps[b][:, 0:32].rearrange("p (t h) -> p t h", h=NH)))
                    e.nop().then_inc(bank_free[b], 1)
                elif what in ("hg_decay", "hg_prep", "hg_qk", "hg_merge", "hg_scale", "hg_state", "hg_out"):
                    hg_dve(e, x, link)
                elif what == "pT":
                    for c in range(2):
                        b, use = USE[("pT", c)]
                        e.wait_ge(p_hi, c + 1)
                        link(e.tensor_tensor(pT_lo[:, c, :], ps[b][:, :], pT_hi[:, c, :].bitcast(F32), ALU.subtract))
                        e.nop().then_inc(bank_free[b], 1)
                    e.nop().then_inc(p_lo, 1)
                elif what == "xback":
                    j = x[1]
                    b, use = USE[x]
                    e.wait_ge(xback_done, j + 1)
                    link(e.tensor_copy(xback[:, j, :], ps[b][:, :]))
                    e.nop().then_inc(bank_free[b], 1)
                    e.nop().then_inc(xback_ready, 1)

        def att_pe(e, kind, i):
            a_ = A[kind]
            qn, kn, vn, _ = kinds(kind)
            j = i - LAG - 1
            if 0 <= j < STEPS:
                qb, h = divmod(j, NH)
                if h == 0:
                    bank_wait(e, ("out", kind, qb))
                if j == 0:
                    tile_taken(e, vn, 0, 2)
                    tile_taken(e, vn, 0, 3)
                b, use = USE[("pt", kind, j)]
                e.wait_ge(bank_free[b], use + 1)
                for c in range(qb + 1):
                    mm = e.matmul(ps[7][:, h * HD:(h + 1) * HD], work[4 + j % 2][:, c * P:(c + 1) * P],
                                  vtok[vn][:, c, h * HD:(h + 1) * HD], start=c == 0, stop=c == qb)
                mm.then_inc(a_["pv_done"], 1)
            j = i - LAG
            if 0 <= j < STEPS:
                bank = bank_wait(e, ("pt", kind, j))
                e.wait_ge(a_["p_ready"], j + 1)
                for c in range(j // NH + 1):
                    mm = e.transpose(bank[:, c * P:(c + 1) * P], work[j % 4][:, c * P:(c + 1) * P], ident[:, :])
                mm.then_inc(a_["tr_done"], 1)
            if i < STEPS:
                qb, h = divmod(i, NH)
                if i == 0:
                    if kind == "B":
                        for nm in (qn, kn):
                            tile_taken(e, nm, 0, 2)
                            tile_taken(e, nm, 0, 3)
                    else:
                        e.wait_ge(qk_ready[qn], 4)
                        e.wait_ge(qk_ready[kn], 4)
                r = slice(64 * (h % 2), 64 * (h % 2) + 64)
                n = (qb + 1) * P
                bank = bank_wait(e, ("sc", kind, i))
                e.matmul(bank[:, 0:n], qk1[qn][r, h // 2, qb * P:n], qk1[kn][r, h // 2, 0:n], start=True, stop=True).then_inc(a_["sc_done"], 1)
            j = i - LAG - 2
            if j > 0 and j % NH == 0:
                q = j // NH - 1
                bank = bank_wait(e, ("ot", kind, q))
                e.wait_ge(a_["ot_ready"], q + 1)
                for c in range(4):
                    mm = e.transpose(bank[:, c * P:(c + 1) * P], work[6][:, c * P:(c + 1) * P], ident[:, :])
                mm.then_inc(a_["ot_done"], 1)

        @block.tensor
        def _(e):
            def operand(name, k):
                if name.startswith("branch"):
                    y = {"B": yB, "A": yA, "H": yH, "F": yF}[name[-1]]
                    return y[0][:, k, :], y[1][:, k, :]
                if name.startswith("down"):
                    return g_hi[:, k, :], g_lo[:, k, :]
                if name == "pproj":
                    return pT_hi[:, k, :], pT_lo[:, k, :]
                return h_hi[:, k, :], h_lo[:, k, :]

            norm_of = {"qB": 0, "kB": 0, "vB": 0, "qA": 0, "kA": 0, "vA": 0, "gateB": 0, "gateA": 0,
                       "up1": 1, "hq": 2, "hf": 2, "hi": 2, "hg": 2, "fq": 2, "fk": 2, "fv": 2,
                       "gateH": 2, "gateF": 2, "up2": 3, "pgate": 4}

            def activations_ready(name, g, k):
                first = isinstance(g, int) and g == 0
                if not first:
                    return
                if name in norm_of and name in ("qB", "up1", "hf", "up2", "pgate"):
                    h_done(e, norm_of[name], k)
                elif name in ("out1", "out2"):
                    e.wait_ge(mixlo_ready, (DC if name == "out2" else 0) + k + 1)
                elif name.startswith("down") and k % 2 == 0:
                    e.wait_ge(up_sem["up" + name[-1]]["lo"], k + 2)
                elif name.startswith("branch") and k == 0:
                    if name == "branchH":
                        e.wait_ge(hgs["ylo"], TB)
                    else:
                        e.wait_ge(A[name[-1]]["ylo"], TB)
                elif name == "pproj" and k == 0:
                    e.wait_ge(p_lo, 1)

            def tile_products(name, g, k, banks, n):
                p = PH[name]
                pos = (p.slot0 + (g * p.kc if isinstance(g, int) else 0) + k) % SPLIT_SLOTS
                x_hi, x_lo = operand(name, k)
                c = slice(n * P, (n + 1) * P)
                if name in ("vB", "vA", "fv", "hi", "pproj", "pgate"):
                    ops = [(x_hi[:, c], w_lo[:, pos, :]), (x_lo[:, c], w_hi[:, pos, :]), (x_hi[:, c], w_hi[:, pos, :])]
                else:
                    ops = [(w_lo[:, pos, c], x_hi), (w_hi[:, pos, c], x_lo), (w_hi[:, pos, c], x_hi)]
                for i, (l, r) in enumerate(ops):
                    mm = e.matmul(ps[banks + n][:, :], l, r, start=k == 0 and i == 0, stop=k == p.kc - 1 and i == 2)
                return mm

            def slot(name, g, k, banks, bank_check):
                p = PH[name]
                last = by_tile(name, g)
                first = p.kc - last
                if k > first:
                    return
                for kk in range(k, p.kc) if k == first else [k]:
                    activations_ready(name, g, kk)
                    e.wait_ge(lo_full, g * p.kc + (p.slot0 + kk + 1))
                for n in range(4):
                    if k == 0:
                        bank_check(n)
                    for kk in range(k, p.kc) if k == first else [k]:
                        mm = tile_products(name, g, kk, banks, n)
                        if n == 3 and kk < p.kc - 1:
                            mm.then_inc(slot_used, 1)
                    if k == first:
                        mm.then_inc(tile_done, 1)

            for x in SCHEDULE:
                what = x[0]
                if what == "start":
                    e.wait_ge(const_ready, 1)
                    for tb in range(TB):
                        e.wait_ge(x_full[tb], 16)
                        for j in range(DC):
                            mm = e.transpose(ps[j][:, tb * P:(tb + 1) * P], xtok[:, tb, j * P:(j + 1) * P], ident[:, :])
                            if tb == TB - 1:
                                mm.then_inc(xt_done, 1)
                    e.wait_ge(const_dve, 1)
                elif what == "warm":
                    bank = bank_wait(e, x)
                    for i in range(4 if x[1] else 7):
                        mm = e.matmul(bank[:, :], ident[:, :], chunk_start[:, :], start=True, stop=True)
                    mm.then_inc(bank_free[5], 1)
                elif what == "vec":
                    bank = bank_wait(e, x)
                    e.wait_ge(*((gain_full, 16), (vec_full, 16 * 14))[x[1]])
                    for i, n, c in (((0, 8, 0),), ((0, 53, 0), (1, 88, 53), (2, 88, 141)))[x[1]]:
                        mm = e.transpose(bank[:, c:c + n], vrows[0:n, i, :], ident[0:n, 0:n])
                    mm.then_inc(vec_done, 1)
                elif what == "sumsq":
                    if x[2] == 0:
                        bank = bank_wait(e, ("norm", x[1]))
                        if x[1] == 0:
                            e.wait_ge(diag_ready, 1)
                            e.matmul(bank[:, :], mean_d[:, :], work[7][:, :], start=True, stop=True).then_inc(x_mean, 1)
                        else:
                            e.wait_ge(added, ADDED * x[1])
                            e.matmul(bank[:, :], mean_d[:, :], sq_sum[:, :], start=True, stop=False)
                    else:
                        e.wait_ge(sq_ready, SQUARE[x])
                        e.matmul(ps[4][:, :], mean_d[:, :], sq_ring[(SQUARE[x] - 1) % 2][:, :], start=False, stop=x[2] == DC - 1).then_inc(sq_used, 1)
                elif what == "slot":
                    _, name, g, k = x

                    def check(n):
                        prev = previous_group(name, g)
                        if prev is None:
                            e.wait_ge(x_ready, DC)
                        elif first_bank(name, g) == 4:
                            bank_wait(e, (name, n))
                            if prev[0] in ("up1", "up2"):
                                tile_taken(e, prev[0], prev[1] - 1, n)
                        elif first_bank(*prev) == 4:
                            up, last = previous_group(*prev)
                            tile_taken(e, up, last, n)
                        else:
                            tile_taken(e, *prev, n)
                    slot(name, g, k, first_bank(name, g), check)
                elif what == "up":
                    name = x[1]
                    p = PH[name]

                    def group(g, u_):
                        def check(n):
                            if isinstance(g, int) and g == 0:
                                tile_taken(e, *previous_group(name, 0), n)
                            elif isinstance(g, int) and g == 1:
                                b, use = USE[(name, 4 + n)]
                                e.wait_ge(bank_free[b], use)
                            else:
                                tile_taken(e, name, g - 2, n)
                        for k in range(p.kc):
                            slot(name, g, k, 4 * u_, check)

                    up_groups(e, p, group)
                elif what == "scale":
                    bank = bank_wait(e, x)
                    e.wait_ge(sq_ready, SQUARE[x])
                    e.matmul(bank[:, :], mean_h[:, :], sq_ring[(SQUARE[x] - 1) % 2][:, :], start=True, stop=True).then_inc(sq_used, 1)
                elif what == "att":
                    att_pe(e, x[1], x[2])
                elif x == ("foxf", 0):
                    bank = bank_wait(e, x)
                    e.wait_ge(ff["w_lo"], 1)
                    for k in range(DC):
                        for i, (l, r) in enumerate(((wf_lo, h_hi), (wf_hi, h_lo), (wf_hi, h_hi))):
                            mm = e.matmul(bank[0:NH, :], l[:, k, :], r[:, k, :], start=k == 0 and i == 0, stop=k == DC - 1 and i == 2)
                    mm.then_inc(ff["mm"], 1)
                elif x == ("foxf", 2):
                    bank = bank_wait(e, x)
                    e.wait_ge(ff["c"], 1)
                    for tb in range(TB):
                        mm = e.transpose(bank[:, tb * NH:(tb + 1) * NH], fx[:, 2, tb * P:(tb + 1) * P], ident[0:NH, 0:NH])
                    mm.then_inc(ff["ct"], 1)
                elif what == "hg_mm":
                    lev = x[1]
                    if lev < 6:
                        e.wait_ge(hgs["Q"], lev + 1)
                        e.wait_ge(hgs["K"], lev + 1)
                    q_, k_ = (hQ, hK) if lev < 6 else (hq, hk)
                    for h in range(HH):
                        bank = bank_wait(e, ("lev", lev, h))
                        for pr in range(TB):
                            c = slice(pr * P, (pr + 1) * P)
                            mm = e.matmul(of_level(lev, bank[:, c]), k_[:, h, c], of_level(lev, q_[:, h, c]), start=True, stop=True)
                        mm.then_inc(hgs["lev_done"], 1)
                elif what == "hg_kt":
                    e.wait_ge(hgs["scale"], 3)
                    for h in range(HH):
                        bank = bank_wait(e, ("kt", h))
                        for pr in range(TB):
                            c = slice(pr * P, (pr + 1) * P)
                            mm = e.transpose(bank[:, c], hK[:, h, c], ident[:, :])
                        mm.then_inc(hgs["kt_done"], 1)
                elif what == "hg_state":
                    c = x[1]
                    pr, r = c // 2, slice(64 * (c % 2), 64 * (c % 2) + 64)
                    bank = bank_wait(e, ("st", c))
                    if c == 0:
                        for h in range(HH):
                            b, use = USE[("kt", h)]
                            e.wait_ge(bank_free[b], use + 1)
                        tile_taken(e, "hi", 0, 2)
                        tile_taken(e, "hi", 0, 3)
                    for h in range(HH):
                        mm = e.matmul(bank[:, h * P:(h + 1) * P], hKt[r, h, pr * P:(pr + 1) * P], hv[r, pr, h * P:(h + 1) * P],
                                      start=True, stop=True)
                    mm.then_inc(hgs["u_done"], 1)
                elif what == "hg_out":
                    if x[1] < TB:
                        pr = x[1]
                        bank = bank_wait(e, ("ho", pr))
                        e.wait_ge(hgs["state"], min(2 * pr + 1, 7))
                        for h in range(HH):
                            v = slice(h * P, (h + 1) * P)
                            e.matmul(bank[:, v], hS[:, h, pr * P:(pr + 1) * P], hv[:, pr, v], start=True, stop=False, skip_group_check=True)
                            for half in range(2):
                                c = 2 * pr + half
                                if c:
                                    mm = e.matmul(bank[64 * half:64 * half + 64, v], hQ[:, h, c * CH:(c + 1) * CH], state[:, c, v],
                                                  start=False, stop=True, skip_group_check=True)
                        mm.then_inc(hgs["o_done"], 1)
                    if x[1] > 0:
                        pr = x[1] - 1
                        bank = bank_wait(e, ("hot", pr))
                        e.wait_ge(hgs["o_tok"], pr + 1)
                        for h in range(HH):
                            mm = e.transpose(bank[:, h * P:(h + 1) * P], work[1][:, h * P:(h + 1) * P], ident[:, :])
                        mm.then_inc(hgs["ot_done"], 1)
                elif what == "pT":
                    e.wait_ge(p_full, 16)
                    for c in range(2):
                        bank = bank_wait(e, ("pT", c))
                        for tb in range(TB):
                            mm = e.transpose(bank[:, tb * P:(tb + 1) * P], ptok[:, tb, c * P:(c + 1) * P], ident[:, :])
                        mm.then_inc(p_done, 1)
                elif what == "xback":
                    half, tb = x[1] // TB, x[1] % TB
                    bank = bank_wait(e, x)
                    for c in range(4):
                        mm = e.transpose(bank[:, c * P:(c + 1) * P], xT[:, 4 * half + c, tb * P:(tb + 1) * P], ident[:, :])
                    mm.then_inc(xback_done, 1)


_INS = ['x', 'norm1_g', 'w_in', 'q_norm_g', 'k_norm_g', 'rel_bias', 'w_branch_a', 'w_branch_b', 'w_out',
        'norm2_g', 'w_ffn_up', 'ffn_conv_w', 'ffn_conv_b', 'w_ffn_down', 'p_2', 'norm_mix_g_2', 'w_in_2',
        'hg_lb_logits_2', 'hg_onorm_g_2', 'fox_f_bias_2', 'fox_q_norm_g_2', 'fox_k_norm_g_2',
        'w_branch_a_2', 'w_branch_b_2', 'w_out_2', 'norm_ffn_g_2', 'w_ffn_gate_2', 'w_ffn_up_2',
        'w_ffn_down_2', 'norm_ple_g_2', 'w_ple_gate_2', 'w_ple_proj_2']


def kernel(**inputs):
    import numpy as np
    import concourse.bacc as bacc
    from concourse.bass_utils import run_bass_kernel_spmd

    nc = bacc.Bacc("TRN2", target_bir_lowering=False, num_devices=1, dynamic_dma_scratch_size=1024)
    arrays, aps = {}, {}
    for name in _INS:
        v = np.ascontiguousarray(inputs[name])
        arrays[f"in_{name}"] = v
        aps[name] = nc.dram_tensor(f"in_{name}", v.shape, mybir.dt.from_np(v.dtype), kind="ExternalInput").ap()
    out = nc.dram_tensor("out_x", (1, S, D), F32, kind="ExternalOutput").ap()
    two_block_kernel(nc, aps, out)
    r = run_bass_kernel_spmd(nc, [arrays], core_ids=[0])
    return r.results[0]["out_x"]
```
